# Optimizing a Trainium2 kernel written in Bass

```python
import math
import jax, jax.numpy as jnp
from jax import lax
import numpy as np

D_MODEL = 1024
BATCH = 1
SEQ = 256
DEPTH = 2

N_MEM = 256
SSM_WIDTH = D_MODEL // 2
SSM_GROUP = 16
SSM_GROUPS = SSM_WIDTH // SSM_GROUP
SSM_STATE = 64
DT_MIN = 1e-3
DT_MAX = 1e-1
POOL_WIDTH = D_MODEL // 2
POOL_WINDOWS = (2, 4, 8, 16)
POOL_GROUP = POOL_WIDTH // len(POOL_WINDOWS)
IN_COLS = SSM_WIDTH + POOL_WIDTH + 2 * D_MODEL
N_XHEADS = 4
XHEAD_DIM = D_MODEL // N_XHEADS
D_FF_DENSE = ((8 * D_MODEL // 3 + 127) // 128) * 128
N_EXPERTS = 8
TOP_K = 2
D_FF_EXPERT = 7 * D_MODEL // 2
N_DENSE = (DEPTH + 1) // 2
N_MOE = DEPTH // 2
ALPHA = (2 * DEPTH) ** 0.25
BETA = (8 * DEPTH) ** -0.25
LN_EPS = 1e-5

kernel_name = 'hybrid_s5_pool_xattn_moe_deepnorm'

def layer_norm(x, g, b):
    xf = x.astype(jnp.float32)
    mu = jnp.mean(xf, axis=-1, keepdims=True)
    xc = xf - mu
    var = jnp.mean(xc * xc, axis=-1, keepdims=True)
    return (xc * lax.rsqrt(var + LN_EPS)).astype(x.dtype) * g + b

def _complex_affine_combine(earlier, later):
    a1r, a1i, b1r, b1i = earlier
    a2r, a2i, b2r, b2i = later
    ar = a2r * a1r - a2i * a1i
    ai = a2r * a1i + a2i * a1r
    br = a2r * b1r - a2i * b1i + b2r
    bi = a2r * b1i + a2i * b1r + b2i
    return (ar, ai, br, bi)

def ssm_branch(u, a_re, a_im, log_dt, b_re, b_im, c_re, c_im, d, w_glu, b_glu):
    dtype = u.dtype
    bsz, seq, _ = u.shape
    f32 = jnp.float32
    uf = u.astype(f32)
    ug = uf.reshape(bsz, seq, SSM_GROUPS, SSM_GROUP)
    a_re, a_im = a_re.astype(f32), a_im.astype(f32)
    dt = jnp.exp(log_dt.astype(f32))[:, None]
    mag = jnp.exp(a_re * dt)
    lam_re = mag * jnp.cos(a_im * dt)
    lam_im = mag * jnp.sin(a_im * dt)
    den = a_re * a_re + a_im * a_im
    num_re = lam_re - 1.0
    f_re = (num_re * a_re + lam_im * a_im) / den
    f_im = (lam_im * a_re - num_re * a_im) / den
    b_re, b_im = b_re.astype(f32), b_im.astype(f32)
    bb_re = f_re[..., None] * b_re - f_im[..., None] * b_im
    bb_im = f_re[..., None] * b_im + f_im[..., None] * b_re
    bu_re = jnp.einsum('bsgc,gpc->bsgp', ug, bb_re)
    bu_im = jnp.einsum('bsgc,gpc->bsgp', ug, bb_im)
    a_seq_re = jnp.broadcast_to(lam_re, (1, seq, SSM_GROUPS, SSM_STATE))
    a_seq_im = jnp.broadcast_to(lam_im, (1, seq, SSM_GROUPS, SSM_STATE))
    _, _, h_re, h_im = lax.associative_scan(
        _complex_affine_combine, (a_seq_re, a_seq_im, bu_re, bu_im), axis=1)
    y = (jnp.einsum('bsgp,gcp->bsgc', h_re, c_re.astype(f32))
         - jnp.einsum('bsgp,gcp->bsgc', h_im, c_im.astype(f32)))
    y = y.reshape(bsz, seq, SSM_WIDTH) + d.astype(f32) * uf
    y = jax.nn.gelu(y)
    y = y * jax.nn.sigmoid(y @ w_glu.astype(f32) + b_glu.astype(f32))
    return y.astype(dtype)

def pool_branch(u, pool_w, pool_scale):
    dtype = u.dtype
    bsz, seq, _ = u.shape
    uf = u.astype(jnp.float32)
    cs = jnp.cumsum(uf, axis=1)
    pos = jnp.arange(1, seq + 1, dtype=jnp.float32)
    outs = []
    for gi, win in enumerate(POOL_WINDOWS):
        sl = slice(gi * POOL_GROUP, (gi + 1) * POOL_GROUP)
        c = cs[..., sl]
        prev = jnp.pad(c[:, :-win], ((0, 0), (win, 0), (0, 0)))
        mean = (c - prev) / jnp.minimum(pos, float(win))[None, :, None]
        outs.append(mean - uf[..., sl])
    y = jnp.stack(outs, axis=2)
    y = jnp.einsum('bsgc,gcd->bsgd', y, pool_w.astype(jnp.float32))
    y = y.reshape(bsz, seq, POOL_WIDTH) * pool_scale.astype(jnp.float32)
    return y.astype(dtype)

def hybrid_mixer(x, w_in, a_re, a_im, log_dt, b_re, b_im, c_re, c_im, d,
                 w_glu, b_glu, w_ssm_up, pool_w, pool_scale, w_pool_up, w_out):
    proj = x @ w_in
    u_ssm = proj[..., :SSM_WIDTH]
    u_pool = proj[..., SSM_WIDTH:SSM_WIDTH + POOL_WIDTH]
    gates = jax.nn.sigmoid(proj[..., SSM_WIDTH + POOL_WIDTH:])
    g_ssm, g_pool = gates[..., :D_MODEL], gates[..., D_MODEL:]
    y_ssm = ssm_branch(u_ssm, a_re, a_im, log_dt, b_re, b_im, c_re, c_im,
                       d, w_glu, b_glu) @ w_ssm_up
    y_pool = pool_branch(u_pool, pool_w, pool_scale) @ w_pool_up
    return (g_ssm * y_ssm + g_pool * y_pool) @ w_out

def cross_attention(x, mem, wq, wk, wv, wo):
    bsz, seq, _ = x.shape
    q = (x @ wq).reshape(bsz, seq, N_XHEADS, XHEAD_DIM)
    k = (mem @ wk).reshape(bsz, -1, N_XHEADS, XHEAD_DIM)
    v = (mem @ wv).reshape(bsz, -1, N_XHEADS, XHEAD_DIM)
    scores = jnp.einsum('bshd,bmhd->bhsm', q, k) * (XHEAD_DIM ** -0.5)
    probs = jax.nn.softmax(scores.astype(jnp.float32), axis=-1).astype(v.dtype)
    out = jnp.einsum('bhsm,bmhd->bshd', probs, v).reshape(bsz, seq, D_MODEL)
    return out @ wo

def swiglu_ffn(x, w1, w3, w2):
    return (jax.nn.silu(x @ w1) * (x @ w3)) @ w2

def moe_ffn(x, router, w1, w3, w2):
    bsz, seq, d = x.shape
    xt = x.reshape(-1, d)
    logits = (xt @ router).astype(jnp.float32)
    top_val, top_idx = lax.top_k(logits, TOP_K)
    top_w = jax.nn.softmax(top_val, axis=-1)
    gates = jnp.sum(jax.nn.one_hot(top_idx, N_EXPERTS, dtype=jnp.float32)
                    * top_w[..., None], axis=1).astype(x.dtype)
    out = jnp.zeros_like(xt)
    for e in range(N_EXPERTS):
        out = out + gates[:, e:e + 1] * swiglu_ffn(xt, w1[e], w3[e], w2[e])
    return out.reshape(bsz, seq, d)

def setup_inputs(seed: int = 0) -> dict:
    key = jax.random.key(seed)
    ks = jax.random.split(key, 40)
    f32 = jnp.float32
    L, G, P, C, D = DEPTH, SSM_GROUPS, SSM_STATE, SSM_GROUP, D_MODEL

    def nrm(i, shape, scale):
        return scale * jax.random.normal(ks[i], shape, f32)

    a_im_init = jnp.broadcast_to(math.pi * jnp.arange(P, dtype=f32), (L, G, P))
    return {
        'x': nrm(0, (BATCH, SEQ, D), 1.0),
        'mem': nrm(1, (BATCH, N_MEM, D), 1.0),
        'ln_mix_g': 1.0 + nrm(2, (L, D), 0.02),
        'ln_mix_b': nrm(3, (L, D), 0.02),
        'w_in': nrm(4, (L, D, IN_COLS), D ** -0.5),
        'ssm_a_re': -0.5 + nrm(5, (L, G, P), 0.01),
        'ssm_a_im': a_im_init + nrm(6, (L, G, P), 0.01),
        'ssm_log_dt': jax.random.uniform(ks[7], (L, G), f32, math.log(DT_MIN), math.log(DT_MAX)),
        'ssm_b_re': nrm(8, (L, G, P, C), (2 * C) ** -0.5),
        'ssm_b_im': nrm(9, (L, G, P, C), (2 * C) ** -0.5),
        'ssm_c_re': nrm(10, (L, G, C, P), (2 * P) ** -0.5),
        'ssm_c_im': nrm(11, (L, G, C, P), (2 * P) ** -0.5),
        'ssm_d': nrm(12, (L, SSM_WIDTH), 1.0),
        'ssm_w_glu': nrm(13, (L, SSM_WIDTH, SSM_WIDTH), SSM_WIDTH ** -0.5),
        'ssm_b_glu': nrm(14, (L, SSM_WIDTH), 0.01),
        'w_ssm_up': nrm(15, (L, SSM_WIDTH, D), BETA * SSM_WIDTH ** -0.5),
        'pool_w': nrm(16, (L, len(POOL_WINDOWS), POOL_GROUP, POOL_GROUP), POOL_GROUP ** -0.5),
        'pool_scale': 1.0 + nrm(17, (L, POOL_WIDTH), 0.02),
        'w_pool_up': nrm(18, (L, POOL_WIDTH, D), BETA * POOL_WIDTH ** -0.5),
        'w_out': nrm(19, (L, D, D), BETA * D ** -0.5),
        'ln_xa_g': 1.0 + nrm(20, (L, D), 0.02),
        'ln_xa_b': nrm(21, (L, D), 0.02),
        'xa_wq': nrm(22, (L, D, D), D ** -0.5),
        'xa_wk': nrm(23, (L, D, D), D ** -0.5),
        'xa_wv': nrm(24, (L, D, D), BETA * D ** -0.5),
        'xa_wo': nrm(25, (L, D, D), BETA * D ** -0.5),
        'ln_ffn_g': 1.0 + nrm(26, (L, D), 0.02),
        'ln_ffn_b': nrm(27, (L, D), 0.02),
        'ffn_w1': nrm(28, (N_DENSE, D, D_FF_DENSE), BETA * D ** -0.5),
        'ffn_w3': nrm(29, (N_DENSE, D, D_FF_DENSE), BETA * D ** -0.5),
        'ffn_w2': nrm(30, (N_DENSE, D_FF_DENSE, D), BETA * D_FF_DENSE ** -0.5),
        'moe_router': nrm(31, (N_MOE, D, N_EXPERTS), D ** -0.5),
        'moe_w1': nrm(32, (N_MOE, N_EXPERTS, D, D_FF_EXPERT), BETA * D ** -0.5),
        'moe_w3': nrm(33, (N_MOE, N_EXPERTS, D, D_FF_EXPERT), BETA * D ** -0.5),
        'moe_w2': nrm(34, (N_MOE, N_EXPERTS, D_FF_EXPERT, D), BETA * D_FF_EXPERT ** -0.5),
    }

def reference(x, mem, ln_mix_g, ln_mix_b, w_in, ssm_a_re, ssm_a_im, ssm_log_dt,
              ssm_b_re, ssm_b_im, ssm_c_re, ssm_c_im, ssm_d, ssm_w_glu, ssm_b_glu,
              w_ssm_up, pool_w, pool_scale, w_pool_up, w_out, ln_xa_g, ln_xa_b,
              xa_wq, xa_wk, xa_wv, xa_wo, ln_ffn_g, ln_ffn_b, ffn_w1, ffn_w3, ffn_w2,
              moe_router, moe_w1, moe_w3, moe_w2):
    for l in range(DEPTH):
        y = hybrid_mixer(x, w_in[l], ssm_a_re[l], ssm_a_im[l], ssm_log_dt[l],
                         ssm_b_re[l], ssm_b_im[l], ssm_c_re[l], ssm_c_im[l], ssm_d[l],
                         ssm_w_glu[l], ssm_b_glu[l], w_ssm_up[l], pool_w[l],
                         pool_scale[l], w_pool_up[l], w_out[l])
        x = layer_norm(ALPHA * x + y, ln_mix_g[l], ln_mix_b[l])
        y = cross_attention(x, mem, xa_wq[l], xa_wk[l], xa_wv[l], xa_wo[l])
        x = layer_norm(ALPHA * x + y, ln_xa_g[l], ln_xa_b[l])
        if l % 2 == 0:
            y = swiglu_ffn(x, ffn_w1[l // 2], ffn_w3[l // 2], ffn_w2[l // 2])
        else:
            y = moe_ffn(x, moe_router[l // 2], moe_w1[l // 2], moe_w3[l // 2], moe_w2[l // 2])
        x = layer_norm(ALPHA * x + y, ln_ffn_g[l], ln_ffn_b[l])
    return x


_drawn_inputs = setup_inputs


def setup_inputs(seed=0):
    import zlib

    import numpy as np

    out = dict(_drawn_inputs(seed))
    spreads = {}
    factors = {'ssm_a_re': 64.0,
     'ssm_a_im': 64.0,
     'ssm_log_dt': 64.0,
     'ssm_b_re': 64.0,
     'ssm_b_im': 64.0,
     'ssm_c_re': 64.0,
     'ssm_c_im': 64.0,
     'ssm_w_glu': 18.319,
     'ssm_b_glu': 200.0,
     'pool_scale': 28.794,
     'ssm_d': 2.857}
    for name, (base, spread) in spreads.items():
        noise = np.random.default_rng([zlib.crc32(name.encode()), seed]).standard_normal(out[name].shape)
        drawn = base * np.exp(spread * noise) if base else spread * noise
        out[name] = __import__('jax').numpy.asarray(drawn.astype(out[name].dtype))
    for name, factor in factors.items():
        out[name] = (out[name] * factor).astype(out[name].dtype)
    return out
```

```python
from contextlib import ExitStack

import concourse.bass as bass
from concourse import mybir

F32 = mybir.dt.float32
F32R = mybir.dt.float32r
I32 = mybir.dt.int32
ALU = mybir.AluOpType
ACT = mybir.ActivationFunctionType
AX_X = mybir.AxisListType.X

P = 128
D = 1024
T = 256
DEPTH = 2
KD = D // P
TT = T // P
SSM_W = 512
KS = SSM_W // P
GROUP_W = 16
STATE_TILES = 16
HALF = 128
PAD = 16
HEADS = 4
D_FF = 2816
FF_CHUNKS = [512] * 5 + [256]
EXPERTS = 8
D_FE = 3584
FE_CHUNKS = D_FE // 512
OVER_MAX = 3
ALPHA = (2 * DEPTH) ** 0.25
LN_EPS = 1e-5

RAW = 7
SPLIT = 4
LEAD = SPLIT - 1
UNIT = 1024
MAGIC = 12582912.0
TABLE_STEPS = [1, 2, 4, 8, 16, 32, 64]


def plan():
    units, gemms, uses = [], {}, [0, 0]

    def gemm(name, weight, stack, row0, rows, col0, cols, paired=True):
        per = UNIT // cols * P
        g = {"first": len(units), "cols": cols, "k": UNIT // cols}
        for r in range(row0, row0 + rows, per):
            units.append((weight, stack, r, UNIT // cols, col0, cols))
        g["end"] = len(units)
        if paired:
            g["pair"] = (uses[0] + uses[1]) % 2
            g["use"] = uses[g["pair"]]
            uses[g["pair"]] += 1
        gemms[name] = g

    def halves(stage, layer, weight, rows, which=(0, 1)):
        for c in which:
            gemm((stage, layer, c), weight, layer, 0, rows, 512 * c, 512)

    for l in range(DEPTH):
        for c in range(6):
            gemm(("in", l, c), "w_in", l, 0, D, 512 * c, 512)
        halves("v", l, "xa_wv", D, (0, 1) if l == 0 else (1,))
        halves("pool_up", l, "w_pool_up", SSM_W, (0,))
        gemm(("glu", l, 0), "ssm_w_glu", l, 0, SSM_W, 0, 512)
        halves("pool_up", l, "w_pool_up", SSM_W, (1,))
        halves("ssm_up", l, "w_ssm_up", SSM_W)
        halves("out", l, "w_out", D)
        halves("k", l, "xa_wk", D, (0, 1) if l == 0 else (1,))
        halves("q", l, "xa_wq", D)
        halves("o", l, "xa_wo", D)
        if l == 0:
            halves("v", 1, "xa_wv", D, (0,))
            for c, cols in enumerate(FF_CHUNKS):
                gemm(("ffn1", c), "ffn_w1", 0, 0, D, 512 * c, cols)
                gemm(("ffn3", c), "ffn_w3", 0, 0, D, 512 * c, cols)
                if c:
                    for h in range(2):
                        gemm(("ffn2", c - 1, h), "ffn_w2", 0, 512 * (c - 1), 512, 512 * h, 512, False)
            c = len(FF_CHUNKS) - 1
            for h in range(2):
                gemm(("ffn2", c, h), "ffn_w2", 0, 512 * c, FF_CHUNKS[c], 512 * h, 512, False)
            halves("k", 1, "xa_wk", D, (0,))
    return units, gemms


def plan_job():
    stages = [("w1", 0), ("w3", 0)]
    for c in range(1, FE_CHUNKS):
        stages += [("w1", c), ("w3", c), ("w2", c - 1)]
    return stages + [("w2", FE_CHUNKS - 1)]


def job_units(stages):
    units = []
    for kind, c in stages:
        if kind == "w2":
            units += [("moe_w2", 512 * c + 256 * k, 512 * h) for h in range(2) for k in range(2)]
        else:
            units += [("moe_" + kind, 256 * k, 512 * c) for k in range(4)]
    return units


class Order:

    def __init__(self, engine, sem):
        self.engine, self.sem, self.n, self.turns = engine, sem, 0, 0

    def add(self, instruction):
        instruction.then_inc(self.sem, 1)
        self.n += 1

    def settle(self):
        self.engine.wait_ge(self.sem, self.n + self.turns)

    def link(self, instruction):
        self.add(instruction)
        self.settle()


def build_trunk(nc, a, out):
    units, gemms = plan()
    stages = plan_job()
    moe_units = job_units(stages)
    N0 = len(units)
    NJ = len(moe_units)
    assert NJ % RAW == 0 and NJ % SPLIT == 0
    stage_at = {s: 4 * i for i, s in enumerate(stages)}

    ctx = ExitStack()
    with ctx:
        def sb(name, shape, dt=F32, stack=ctx):
            return stack.enter_context(nc.sbuf_tensor(name, shape, dt))

        def sem(name):
            return ctx.enter_context(nc.semaphore(name))

        raw = sb("raw", [P, RAW, UNIT])
        w_hi = sb("w_hi", [P, SPLIT, UNIT], F32R)
        w_lo = sb("w_lo", [P, SPLIT, UNIT], F32R)
        x_tok = sb("x_tok", [P, TT, D])
        xs = sb("xs", [P, 16, T], F32R)
        v_sb = sb("v_sb", [P, 2, D])
        k_sb = sb("k_sb", [P, KD, T])
        ln_gb = sb("ln_gb", [P, 2, D])
        ident = sb("ident", [P, P])
        iota8 = sb("iota8", [P, 8])
        tiny = sb("tiny", [P, 64])
        small = sb("small", [P, 3, DEPTH, KS])
        pool_w = sb("pool_w", [P, KS, P])
        inv_count = sb("inv_count", [P, KS, PAD])
        router = sb("router", [P, KD * EXPERTS])
        router_s = sb("router_s", [P, 2, KD * EXPERTS], F32R)
        sp_in = sb("sp_in", [P, 3, 2 * STATE_TILES])
        sp = sb("sp", [P, 14, 2 * STATE_TILES])
        turn = sb("turn", [P, 2, STATE_TILES])
        turn_t = sb("turn_t", [P, 3, STATE_TILES])
        carry = sb("carry", [P, 4, 4])

        mixer = ExitStack()
        ms = sb("ms", [P, 16, T], F32R, mixer)
        table = sb("table", [P, 2, STATE_TILES, HALF], F32, mixer)
        prod = sb("prod", [P, 2048], F32, mixer)
        u_sb = sb("u_sb", [P, KS, T], F32, mixer)
        u_pool = sb("u_pool", [P, KS, PAD + T], F32, mixer)
        rot = sb("rot", [P, 2 * (PAD + T)], F32, mixer)
        b_t = sb("b_t", [P, 2, KS, P], F32, mixer)
        c_t = sb("c_t", [P, 3, STATE_TILES * 32], F32, mixer)
        first = ExitStack()
        wave = sb("wave", [P, 4096], F32, first)
        first.close()
        second = ExitStack()
        mx = sb("mx", [P, 16, T], F32R, second)
        second.close()
        skip = ExitStack()
        sb("wave_place", [P, 4096], F32, skip)
        g1 = ExitStack()
        gates = sb("gates", [P, 16, T], F32, g1)
        g1.close()
        g2 = ExitStack()
        hs = sb("hs", [P, 2, 2, 4, T], F32R, g2)
        g2.close()
        skip.close()
        mixer.close()
        moe = ExitStack()
        acc = sb("acc", [P, TT, D], F32, moe)
        xts = sb("xts", [P, 2, TT, D], F32R, moe)
        sel = sb("sel", [P, TT, P], F32R, moe)
        gsel = sb("gsel", [P, TT, P], F32, moe)
        gsel2 = sb("gsel2", [P, TT, P], F32, moe)
        gsel_t = sb("gsel_t", [P, TT, P], F32, moe)
        xe = sb("xe", [P, 2, KD, P], F32R, moe)
        he = sb("he", [P, 2, 512], F32, moe)
        het = sb("het", [P, 2, 2, 4, P], F32R, moe)
        y_sb = sb("y_sb", [P, D], F32, moe)
        tri = sb("tri", [P, P], F32, moe)
        ones = sb("ones", [P, P], F32, moe)
        iota = sb("iota", [P, P], F32, moe)
        rt = sb("rt", [P, 12, TT, EXPERTS], F32, moe)
        rs = sb("rs", [P, 12, TT], F32, moe)
        dest = sb("dest", [P, 2, TT], F32, moe)
        gate_w = sb("gate_w", [P, 2, TT], F32, moe)
        ovf = sb("ovf", [P, 8, EXPERTS], F32, moe)
        jobs_f = sb("jobs_f", [P, 16], F32, moe)
        jobs = sb("jobs", [P, 16], I32, moe)
        moe.close()

        ps = ctx.enter_context(nc.psum_tensor("ps", [P, 8, 512], F32))

        raw_landed = [sem(f"raw_landed{i}") for i in range(RAW)]
        hi_ready, lo_ready, unit_used = sem("hi_ready"), sem("lo_ready"), sem("unit_used")
        pair_free = [sem("pair_free0"), sem("pair_free1")]
        x_in, mem_in, small_in, bc_in = sem("x_in"), sem("mem_in"), sem("small_in"), [sem("bc_in0"), sem("bc_in1")]
        xtok_in, poolw_in, ln_in, moe_in = sem("xtok_in"), [sem("poolw_in0"), sem("poolw_in1")], sem("ln_in"), sem("moe_in")
        xs_hi, xs_ready = sem("xs_hi"), sem("xs_ready")
        ms_hi, ms_ready = sem("ms_hi"), sem("ms_ready")
        dve_order, dve_tail, pool_order = sem("dve_order"), sem("dve_tail"), sem("pool_order")
        bb_ready, bt_done, bt_ready = sem("bb_ready"), sem("bt_done"), sem("bt_ready")
        table_ready = sem("table_ready")
        prep_ready = sem("prep_ready")
        bu_done, rotated, z_ready = sem("bu_done"), sem("rotated"), sem("z_ready")
        prod_ready, y_used = sem("prod_ready"), sem("y_used")
        y_linear, y_gelu, ys_ready = sem("y_linear"), sem("y_gelu"), sem("ys_ready")
        pooled, pool_mixed, pool_scaled, ps_ready = sem("pooled"), sem("pool_mixed"), sem("pool_scaled"), sem("ps_ready")
        pad_ready = sem("pad_ready")
        mx_ready = sem("mx_ready")
        ln_var, ln_rstd, ln_shift, ln_norm = sem("ln_var"), sem("ln_rstd"), sem("ln_shift"), sem("ln_norm")
        ln_done, xt_done, xt_hi, xt_ready = sem("ln_done"), sem("xt_done"), sem("xt_hi"), sem("xt_ready")
        score_done, score_max, prob_exp, prob_ready = sem("score_done"), sem("score_max"), sem("prob_exp"), sem("prob_ready")
        pt_done, pt_ready, pv_done, at_hi, at_ready = sem("pt_done"), sem("pt_ready"), sem("pv_done"), sem("at_hi"), sem("at_ready")
        silu_ready, hs_ready = sem("silu_ready"), sem("hs_ready")
        router_hi, router_ready, logits_done = sem("router_hi"), sem("router_ready"), sem("logits_done")
        expo_in, expo_done, picked, ranked, routed = sem("expo_in"), sem("expo_done"), sem("picked"), sem("ranked"), sem("routed")
        ones_ready = sem("ones_ready")
        xts_hi, xts_ready, c_ready = sem("xts_hi"), sem("xts_ready"), sem("c_ready")
        sel_ready, gsel_ready = sem("sel_ready"), sem("gsel_ready")
        misc_filled, misc_free = sem("misc_filled"), [sem("misc_free0"), sem("misc_free1")]
        het_hi = sem("het_hi")
        w1_free, w3_free, y_ready = sem("w1_free"), sem("w3_free"), sem("y_ready")
        out_ready, out_landed = sem("out_ready"), sem("out_landed")

        block = ctx.enter_context(nc.Block())

        def evacuated(engine, name):
            g = gemms[name]
            engine.wait_ge(pair_free[g["pair"]], g["use"] + 1)

        def gemm_ended(engine, name):
            engine.wait_ge(unit_used, gemms[name]["end"])

        def pair_of(name):
            return ps[:, 2 * gemms[name]["pair"]:2 * gemms[name]["pair"] + 2, :]

        def blocks(ap):
            return ap.rearrange("p b (h t) -> p (b h) t", t=T)

        def freed(instruction, name):
            instruction.then_inc(pair_free[gemms[name]["pair"]], 1)

        def view(buffer, slot, n, cols):
            return buffer[:, n % slot, :].rearrange("p (k c) -> p k c", c=cols)

        def hi_blocks(t, i, n):
            return t[:, i:i + n, :]

        wave_v = wave[:, :].rearrange("p (b j r t) -> p b j r t", b=2, j=4, r=2)
        prod_v = prod[:, :].rearrange("p (b q r t) -> p b q r t", b=2, q=2, r=2)
        y_v = prod[:, 0:1024].rearrange("p (f t) -> p f t", t=T)
        sil_v = wave[:, 0:2048].rearrange("p (b f t) -> p b f t", b=2, f=4)
        q_v = gates[:, 0:8, :]
        probs = gates[:, 8:12, :].rearrange("p (b q) t -> p b q t", b=2)
        probs_t = gates[:, 12:16, :].rearrange("p (b m) t -> p b m t", b=2)
        b_in = k_sb[:, 0:4, :].rearrange("p (r a) t -> p r (a t)", r=2)
        bb = prod[:, 0:1024].rearrange("p (r n) -> p r n", r=2)
        SSM_SLOTS = 24
        Y_LAG = 8

        def ssm_units(l):
            return gemms[("in", l, 2 if l == 0 else 1)]["first"]

        def discretise(engine, order, l, done):
            def wide(i):
                return sp[:, i, STATE_TILES * l:STATE_TILES * (l + 1)].unsqueeze(2).broadcast_to([P, STATE_TILES, 32])
            def per_tile(ap):
                return ap.rearrange("p (j c) -> p j c", c=32)
            b_re, b_im = per_tile(b_in[:, 0, :]), per_tile(b_in[:, 1, :])
            t1, t2 = per_tile(prod[:, 1024:1536]), per_tile(prod[:, 1536:2048])
            for k, (x, y, op) in enumerate(((b_re, b_im, ALU.subtract), (b_im, b_re, ALU.add))):
                order.add(engine.tensor_tensor(t1, x, wide(6), ALU.mult))
                order.link(engine.tensor_tensor(t2, y, wide(7), ALU.mult))
                last = engine.tensor_tensor(per_tile(bb[:, k, :]), t1, t2, op)
                if k == 0:
                    order.link(last)
            last.then_inc(done, 1)

        def phase_table(engine, order, l, done, between):
            js = slice(STATE_TILES * l, STATE_TILES * (l + 1))
            tt = engine.tensor_tensor
            cos, sin = table[:, 0], table[:, 1]
            order.add(engine.memset(cos[:, :, 0:1], 1.0))
            order.add(engine.memset(sin[:, :, 0:1], 0.0))
            order.add(engine.tensor_copy(turn[:, 0, :], sp[:, 4, js]))
            order.link(engine.tensor_copy(turn[:, 1, :], sp[:, 5, js]))
            for m in TABLE_STEPS:
                pc, ps_ = [turn[:, i, :].unsqueeze(2).broadcast_to([P, STATE_TILES, m]) for i in range(2)]
                t1, t2 = [prod[:, 1024 * i:1024 * i + STATE_TILES * m].rearrange("p (j t) -> p j t", t=m) for i in range(2)]
                c, s = cos[:, :, 0:m], sin[:, :, 0:m]
                order.add(tt(t1, c, pc, ALU.mult))
                order.link(tt(t2, s, ps_, ALU.mult))
                order.link(tt(cos[:, :, m:2 * m], t1, t2, ALU.subtract))
                order.add(tt(t1, s, pc, ALU.mult))
                order.link(tt(t2, c, ps_, ALU.mult))
                order.add(tt(sin[:, :, m:2 * m], t1, t2, ALU.add))
                order.add(tt(turn_t[:, 0, :], turn[:, 0, :], turn[:, 0, :], ALU.mult))
                order.add(tt(turn_t[:, 1, :], turn[:, 1, :], turn[:, 1, :], ALU.mult))
                order.link(tt(turn_t[:, 2, :], turn[:, 0, :], turn[:, 1, :], ALU.mult))
                order.add(tt(turn[:, 0, :], turn_t[:, 0, :], turn_t[:, 1, :], ALU.subtract))
                last = tt(turn[:, 1, :], turn_t[:, 2, :], turn_t[:, 2, :], ALU.add)
                if m < TABLE_STEPS[-1]:
                    order.link(last)
                between(m)
            last.then_inc(done, 1)

        @block.sync
        def _(sp_):
            sp_.dma_start(wave[:, 0:2048].rearrange("p (k t) -> p k t", t=T), a["x_t"]).then_inc(x_in, 16)
            for n, (name, stack, r0, k, c0, cols) in enumerate(units):
                if n >= RAW:
                    sp_.wait_ge(lo_ready, n - RAW + 1)
                src = a[name][stack, r0:r0 + k * P, c0:c0 + cols].rearrange("(k p) c -> p k c", p=P)
                sp_.dma_start(view(raw, RAW, n, cols), src).then_inc(raw_landed[n % RAW], 16)

            def load(i, expert, shift):
                name, r0, c0 = moe_units[i % NJ]
                n = N0 + i
                sp_.wait_ge(lo_ready, n - RAW + 1 + shift)
                rows = a[name].shape[1]
                src = a[name].rearrange("e r c -> (e r) c")[bass.ds(expert * rows + r0, 2 * P), c0:c0 + 512]
                src = src.rearrange("(k p) c -> p k c", p=P)
                sp_.dma_start(view(raw, RAW, n, 512), src).then_inc(raw_landed[n % RAW], 16)

            for i in range(LEAD):
                load(i, 0, 0)

            def job(j, expert, following):
                for i in range(LEAD, NJ):
                    load(i, expert, NJ * j)
                nxt = following()
                for i in range(NJ, NJ + LEAD):
                    load(i, nxt, NJ * j)

            with sp_.Fori(0, EXPERTS - 1) as j:
                job(j, j, lambda: j + 1)
            sp_.wait_ge(routed, 1)
            over = sp_.value_load(jobs[0:1, 0:1], min_val=0, max_val=OVER_MAX)
            job(EXPERTS - 1, EXPERTS - 1,
                lambda: sp_.value_load(jobs[0:1, 1:2], min_val=0, max_val=EXPERTS - 1))
            for o in range(OVER_MAX):
                with sp_.If(over > o):
                    expert = sp_.value_load(jobs[0:1, 1 + o:2 + o], min_val=0, max_val=EXPERTS - 1)
                    job(EXPERTS + o, expert,
                        lambda: sp_.value_load(jobs[0:1, 2 + o:3 + o], min_val=0, max_val=EXPERTS - 1))
                sp_.nop()
            for t in range(TT):
                sp_.wait_ge(out_ready, t + 1)
                sp_.dma_start(out[t * P:(t + 1) * P, :], acc[:, t, :]).then_inc(out_landed, 16)
            sp_.wait_ge(out_landed, 16 * TT)

        @block.scalar
        def _(act):
            split = [0]

            def split_hi(n):
                act.wait_ge(raw_landed[n % RAW], 16 * (n // RAW + 1))
                if n >= SPLIT:
                    act.wait_ge(unit_used, n - SPLIT + 1)
                nc.scalar.activation(w_hi[:, n % SPLIT, :], raw[:, n % RAW, :], ACT.Copy).then_inc(hi_ready, 1)

            def splits_to(n):
                while split[0] < min(n + LEAD, N0 + LEAD):
                    split_hi(split[0])
                    split[0] += 1

            act.dma_start(sp_in[:, :, :], a["ssm_par"]).then_inc(small_in, 16)
            act.dma_start(small[:, :, :, :], a["chan_par"]).then_inc(small_in, 16)
            act.dma_start(ident[:, :], a["c_ident"]).then_inc(small_in, 16)
            act.dma_start(iota8[:, :], a["c_iota8"]).then_inc(small_in, 16)
            act.dma_start(inv_count[:, :, :], a["c_inv"]).then_inc(small_in, 16)
            act.dma_start(router[:, :], a["router"]).then_inc(small_in, 16)
            act.dma_start(b_in, a["ssm_b"][0]).then_inc(bc_in[0], 16)
            act.dma_start(c_t[:, 0, :], a["ssm_c"][0, 0]).then_inc(bc_in[0], 16)
            act.dma_start(c_t[:, 2, :], a["ssm_c"][0, 1]).then_inc(bc_in[0], 16)
            act.dma_start(pool_w[:, :, :], a["pool_wt"][0]).then_inc(poolw_in[0], 16)
            act.dma_start(wave[:, 2048:4096].rearrange("p (k t) -> p k t", t=T), a["mem_t"]).then_inc(mem_in, 16)
            act.dma_start(x_tok[:, :, :], a["x"].rearrange("(t p) d -> p t d", p=P)).then_inc(xtok_in, 16)

            act.wait_ge(x_in, 16)
            nc.scalar.activation(xs[:, 0:8, :], wave[:, 0:2048].rearrange("p (k t) -> p k t", t=T),
                                 ACT.Copy).then_inc(xs_hi, 1)
            splits_to(1)
            act.wait_ge(mem_in, 16)
            nc.scalar.activation(ms[:, 0:8, :], wave[:, 2048:4096].rearrange("p (k t) -> p k t", t=T),
                                 ACT.Copy).then_inc(ms_hi, 1)
            act.wait_ge(small_in, 96)
            nc.scalar.activation(router_s[:, 0, :], router[:, :], ACT.Copy).then_inc(router_hi, 1)

            def epilogue(name, fn):
                splits_to(gemms[name]["end"])
                gemm_ended(act, name)
                freed(fn(pair_of(name)), name)

            def values(l, c):
                epilogue(("v", l, c), lambda p: nc.scalar.activation(v_sb[:, :, 512 * c:512 * c + 512], p, ACT.Copy))

            def keys(l, c):
                epilogue(("k", l, c), lambda p: nc.scalar.activation(k_sb[:, 4 * c:4 * c + 4, :], blocks(p), ACT.Copy))

            def hi_of_x(i):
                for t in range(TT):
                    act.wait_ge(xt_done, TT * i + t + 1)
                    src = ps[:, 4 + 2 * t:6 + 2 * t, :].rearrange("p b (k t) -> p (b k) t", t=P)
                    nc.scalar.activation(xs[:, 0:8, t * P:(t + 1) * P], src, ACT.Copy).then_inc(xt_hi, 1)

            def normalise(i, tensor):
                for t in range(TT):
                    act.wait_ge(ln_shift, TT * i + t + 1)
                    nc.scalar.activation(tensor[:, t, :], tensor[:, t, :], ACT.Identity,
                                         scale=tiny[:, 4 * t + 2:4 * t + 3], bias=tiny[:, 4 * t + 3:4 * t + 4]
                                         ).then_inc(ln_norm, 1)

            for l in range(DEPTH):
                epilogue(("in", l, 0), lambda p: nc.scalar.activation(u_sb[:, :, :], blocks(p), ACT.Copy))
                act.wait_ge(bt_done, l + 1)
                nc.scalar.activation(b_t[:, :, :, :], ps[:, 4:6, :].rearrange("p r (j s) -> p r j s", s=P),
                                     ACT.Copy).then_inc(bt_ready, 1)
                if l == 0:
                    act.wait_ge(pad_ready, 1)
                epilogue(("in", l, 1), lambda p: nc.scalar.activation(u_pool[:, :, PAD:PAD + T], blocks(p), ACT.Copy))
                for c in range(2, 6):
                    epilogue(("in", l, c), lambda p, c=c: nc.scalar.activation(
                        gates[:, 4 * (c - 2):4 * (c - 2) + 4, :], blocks(p), ACT.Sigmoid))
                for c in ((0, 1) if l == 0 else (1,)):
                    values(l, c)
                act.wait_ge(pool_mixed, l + 1)
                for g in range(KS):
                    last = nc.scalar.activation(u_pool[:, g, PAD:PAD + T], ps[:, 4 + g // 2, T * (g % 2):T * (g % 2) + T],
                                                ACT.Copy, scale=small[:, 2, l, g:g + 1])
                last.then_inc(pool_scaled, 1)
                act.wait_ge(y_linear, l + 1)
                nc.scalar.activation(y_v, y_v, ACT.Gelu_apprx_tanh).then_inc(y_gelu, 1)
                splits_to(gemms[("glu", l, 0)]["end"])
                gemm_ended(act, ("glu", l, 0))
                for f in range(KS):
                    last = nc.scalar.activation(u_sb[:, f, :], blocks(pair_of(("glu", l, 0)))[:, f, :], ACT.Sigmoid,
                                                bias=small[:, 1, l, f:f + 1])
                freed(last, ("glu", l, 0))
                splits_to(gemms[("out", l, 1)]["end"])
                normalise(3 * l, x_tok)
                for c in ((0, 1) if l == 0 else (1,)):
                    keys(l, c)
                hi_of_x(3 * l)
                for c in range(2):
                    epilogue(("q", l, c), lambda p, c=c: nc.scalar.activation(
                        q_v[:, 4 * c:4 * c + 4, :], blocks(p), ACT.Copy, scale=1.0 / 16.0))
                for h in range(HEADS + 1):
                    if h < HEADS:
                        n = HEADS * l + h
                        act.wait_ge(score_max, n + 1)
                        for t in range(TT):
                            last = nc.scalar.activation(probs[:, h % 2, t, :], ps[:, 4 + h % 2, T * t:T * t + T], ACT.Exp,
                                                        bias=tiny[:, 16 + 4 * (h % 2) + t:17 + 4 * (h % 2) + t],
                                                        accum_out=tiny[:, 24 + 4 * (h % 2) + t:25 + 4 * (h % 2) + t])
                        last.then_inc(prob_exp, 1)
                    if h >= 1:
                        n = HEADS * l + h - 1
                        act.wait_ge(pt_done, n + 1)
                        nc.scalar.activation(probs_t[:, (h - 1) % 2, :, :],
                                             ps[:, 6 + (h - 1) % 2, :].rearrange("p (m t) -> p m t", t=T),
                                             ACT.Copy).then_inc(pt_ready, 1)
                        act.wait_ge(pv_done, n + 1)
                        nc.scalar.activation(xs[:, 2 * (h - 1):2 * h, :], ps[:, h - 1, :].rearrange("p (b t) -> p b t", t=T),
                                             ACT.Copy).then_inc(at_hi, 1)
                splits_to(gemms[("o", l, 1)]["end"])
                normalise(3 * l + 1, x_tok)
                if l == 0:
                    values(1, 0)
                hi_of_x(3 * l + 1)
                if l == 0:
                    for c, cols in enumerate(FF_CHUNKS):
                        name, f = ("ffn1", c), cols // P
                        splits_to(gemms[name]["end"])
                        gemm_ended(act, name)
                        if c >= 2:
                            act.wait_ge(hs_ready, c - 1)
                        freed(nc.scalar.activation(sil_v[:, c % 2, 0:f, :], blocks(pair_of(name))[:, 0:f, :], ACT.Silu), name)
                    splits_to(gemms[("ffn2", len(FF_CHUNKS) - 1, 1)]["end"])
                    normalise(2, x_tok)
                    act.wait_ge(bb_ready, 2)
                    keys(1, 0)
                    hi_of_x(2)

            act.wait_ge(ln_done, 2 * 5)
            nc.scalar.activation(xts[:, 0, :, :], x_tok[:, :, :], ACT.Copy).then_inc(xts_hi, 1)
            nc.scalar.activation(acc[:, :, :], x_tok[:, :, :], ACT.Copy, scale=ALPHA).then_inc(w1_free, 1)
            act.wait_ge(expo_in, 1)
            nc.scalar.activation(rs[:, 3, :], rs[:, 2, :], ACT.Exp).then_inc(expo_done, 1)

            def gather_out(r_first, which, turn_):
                for i in which:
                    act.wait_ge(misc_filled, 4 + r_first + i + 1 + turn_)
                    r = r_first + i
                    nc.scalar.activation(xe[:, i // 2, 4 * (i % 2):4 * (i % 2) + 4, :],
                                         ps[:, 6 + r % 2, :].rearrange("p (k s) -> p k s", s=P),
                                         ACT.Copy).then_inc(misc_free[r % 2], 1)

            gather_out(-4, range(4), 0)

            def job(j):
                done = [LEAD]

                def through(n):
                    while done[0] < n + LEAD:
                        i = done[0]
                        m = N0 + i
                        act.wait_ge(raw_landed[m % RAW], 16 * (m // RAW + 1) + 16 * (NJ // RAW) * j)
                        act.wait_ge(unit_used, m - SPLIT + 1 + NJ * j)
                        nc.scalar.activation(w_hi[:, m % SPLIT, :], raw[:, m % RAW, :], ACT.Copy).then_inc(hi_ready, 1)
                        done[0] += 1

                for i, (kind, c) in enumerate(stages):
                    through(4 * i + 4)
                    ended = N0 + 4 * i + 4
                    if kind == "w1":
                        act.wait_ge(unit_used, ended + NJ * j)
                        nc.scalar.activation(he[:, c % 2, :], ps[:, 2 * (c % 2), :], ACT.Silu).then_inc(w1_free, 1)
                        if c:
                            r = 4 + c
                            act.wait_ge(misc_filled, 4 + r + 1 + 16 * j)
                            nc.scalar.activation(het[:, (c - 1) % 2, 0, :, :],
                                                 ps[:, 6 + r % 2, :].rearrange("p (k s) -> p k s", s=P),
                                                 ACT.Copy).then_inc(het_hi, 1)
                    if (kind, c) == ("w3", 0):
                        act.wait_ge(misc_filled, 4 + 4 + 1 + 16 * j)
                        nc.scalar.activation(gsel_t[:, :, :], ps[:, 6, 0:2 * P].rearrange("p (t s) -> p t s", s=P),
                                             ACT.Copy).then_inc(misc_free[0], 1)
                    if (kind, c) == ("w3", FE_CHUNKS - 1):
                        gather_out(11, (0, 1), 16 * j)
                        gather_out(11, (2, 3), 16 * j)
                    if (kind, c) == ("w2", FE_CHUNKS - 2):
                        act.wait_ge(misc_filled, 4 + 15 + 1 + 16 * j)
                        nc.scalar.activation(het[:, (FE_CHUNKS - 1) % 2, 0, :, :],
                                             ps[:, 7, :].rearrange("p (k s) -> p k s", s=P),
                                             ACT.Copy).then_inc(het_hi, 1)
                act.wait_ge(unit_used, N0 + NJ + NJ * j)
                nc.scalar.activation(y_sb[:, :], ps[:, 4:6, :].rearrange("p b c -> p (b c)"), ACT.Copy).then_inc(y_ready, 1)

            with act.Fori(0, EXPERTS) as j:
                job(j)
            over = act.value_load(jobs[0:1, 0:1], min_val=0, max_val=OVER_MAX)
            for o in range(OVER_MAX):
                with act.If(over > o):
                    job(EXPERTS + o)
                act.nop()
            normalise(5, acc)

        @block.vector
        def _(dve):
            order = Order(dve, dve_order)
            add, settle, link = order.add, order.settle, order.link
            split = [0]
            tt = nc.vector.tensor_tensor
            ts = nc.vector.tensor_scalar
            stt = nc.vector.scalar_tensor_tensor

            def split_lo(n, shift):
                dve.wait_ge(hi_ready, n + 1 + shift)
                tt(w_lo[:, n % SPLIT, :], raw[:, n % RAW, :], w_hi[:, n % SPLIT, :].bitcast(F32),
                   ALU.subtract).then_inc(lo_ready, 1)

            def splits_to(n):
                while split[0] < min(n + LEAD, N0 + LEAD):
                    split_lo(split[0], 0)
                    split[0] += 1

            def hi_lo(hi, lo, src, last_sem):
                link(nc.vector.tensor_copy(hi, src))
                tt(lo, src, hi.bitcast(F32), ALU.subtract).then_inc(last_sem, 1)

            dve.wait_ge(xs_hi, 1)
            tt(xs[:, 8:16, :], wave[:, 0:2048].rearrange("p (k t) -> p k t", t=T), xs[:, 0:8, :].bitcast(F32),
               ALU.subtract).then_inc(xs_ready, 1)
            splits_to(1)
            nc.vector.memset(u_pool[:, :, 0:PAD], 0.0).then_inc(pad_ready, 1)

            (DT, RE, TH, MAG, COS, SIN, FRE, FIM, A, B, C, E, F, G) = [sp[:, i, :] for i in range(14)]
            are, aim, ldt = sp_in[:, 0, :], sp_in[:, 1, :], sp_in[:, 2, :]
            n1, n2 = F.bitcast(I32), G.bitcast(I32)
            dve.wait_ge(small_in, 96)

            def exp_exact(dst, x):
                link(ts(A, x, -170.0, 100.0, ALU.max, ALU.min))
                link(ts(B, A, 1.4426950408889634, MAGIC, ALU.mult, ALU.add))
                link(ts(B, B, MAGIC, None, ALU.subtract))
                link(stt(C, B, -0.693359375, A, ALU.mult, ALU.add))
                link(stt(C, B, 2.12194440e-4, C, ALU.mult, ALU.add))
                link(ts(E, C, 1.9875691500e-4, None, ALU.mult))
                for k in (1.3981999507e-3, 8.3334519073e-3, 4.1665795894e-2, 1.6666665459e-1, 5.0000001201e-1, 1.0):
                    link(stt(E, E, k, C, ALU.add, ALU.mult))
                link(ts(E, E, 1.0, None, ALU.add))
                link(ts(A, B, 0.5, MAGIC, ALU.mult, ALU.add))
                link(ts(A, A, MAGIC, None, ALU.subtract))
                link(tt(B, B, A, ALU.subtract))
                link(ts(n1, A, 127.0, 8388608.0, ALU.add, ALU.mult))
                link(ts(n2, B, 127.0, 8388608.0, ALU.add, ALU.mult))
                link(tt(E, E, F, ALU.mult))
                link(tt(dst, E, G, ALU.mult))

            exp_exact(DT, ldt)
            link(tt(RE, are, DT, ALU.mult))
            exp_exact(MAG, RE)
            link(tt(TH, aim, DT, ALU.mult))
            link(ts(A, TH, 0.15915494309189535, MAGIC, ALU.mult, ALU.add))
            link(ts(A, A, MAGIC, None, ALU.subtract))
            link(stt(TH, A, -6.28125, TH, ALU.mult, ALU.add))
            link(stt(TH, A, -1.9350051879882812e-3, TH, ALU.mult, ALU.add))
            link(stt(TH, A, -3.0199159819591886e-7, TH, ALU.mult, ALU.add))
            link(ts(A, TH, 0.25, None, ALU.mult))
            link(tt(B, A, A, ALU.mult))
            link(ts(C, B, -1.9515295891e-4, 8.3321608736e-3, ALU.mult, ALU.add))
            link(tt(C, C, B, ALU.mult))
            link(stt(C, C, -1.6666654611e-1, B, ALU.add, ALU.mult))
            link(stt(SIN, C, 1.0, A, ALU.add, ALU.mult))
            link(ts(C, B, 2.443315711809948e-5, -1.388731625493765e-3, ALU.mult, ALU.add))
            link(tt(C, C, B, ALU.mult))
            link(stt(C, C, 4.166664568298827e-2, B, ALU.add, ALU.mult))
            link(stt(C, C, -0.5, B, ALU.add, ALU.mult))
            link(ts(COS, C, 1.0, None, ALU.add))
            for _ in range(2):
                link(tt(A, SIN, SIN, ALU.mult))
                link(stt(SIN, SIN, 2.0, COS, ALU.mult, ALU.mult))
                link(ts(COS, A, -2.0, 1.0, ALU.mult, ALU.add))
            link(tt(A, MAG, COS, ALU.mult))
            link(tt(B, MAG, SIN, ALU.mult))
            link(ts(A, A, 1.0, None, ALU.subtract))
            link(tt(C, are, are, ALU.mult))
            link(tt(E, aim, aim, ALU.mult))
            link(tt(C, C, E, ALU.add))
            link(nc.vector.reciprocal(C, C))
            link(tt(E, A, are, ALU.mult))
            link(tt(F, B, aim, ALU.mult))
            link(tt(E, E, F, ALU.add))
            link(tt(FRE, E, C, ALU.mult))
            link(tt(E, B, are, ALU.mult))
            link(tt(F, A, aim, ALU.mult))
            link(tt(E, E, F, ALU.subtract))
            tt(FIM, E, C, ALU.mult).then_inc(prep_ready, 1)
            dve.wait_ge(prep_ready, 1)
            splits_to(3)

            dve.wait_ge(bc_in[0], 48)
            discretise(nc.vector, order, 0, bb_ready)
            splits_to(5)
            dve.wait_ge(ms_hi, 1)
            tt(ms[:, 8:16, :], wave[:, 2048:4096].rearrange("p (k t) -> p k t", t=T), ms[:, 0:8, :].bitcast(F32),
               ALU.subtract).then_inc(ms_ready, 1)
            dve.wait_ge(router_hi, 1)
            tt(router_s[:, 1, :], router[:, :], router_s[:, 0, :].bitcast(F32), ALU.subtract).then_inc(router_ready, 1)
            dve.wait_ge(bt_done, 1)
            phase_table(nc.vector, order, 0, table_ready, lambda m: splits_to(min(5 + m, 10)))

            def window_means(l, g):
                bufs = [rot[:, 0:PAD + T], rot[:, PAD + T:2 * (PAD + T)]]
                add(nc.vector.memset(bufs[0][:, 0:PAD], 0.0))
                link(nc.vector.memset(bufs[1][:, 0:PAD], 0.0))
                s = u_pool[:, g, :]
                for level in range(g + 1):
                    d = bufs[level % 2]
                    link(tt(d[:, PAD:], s[:, PAD:], s[:, PAD - 2 ** level:PAD + T - 2 ** level], ALU.add))
                    s = d
                w = 2 ** (g + 1)
                u = u_pool[:, g, :]
                link(tt(s[:, PAD:2 * PAD], s[:, PAD:2 * PAD], inv_count[:, g, :], ALU.mult))
                add(stt(u[:, 2 * PAD:], s[:, 2 * PAD:], 1.0 / w, u[:, 2 * PAD:], ALU.mult, ALU.subtract))
                tt(u[:, PAD:2 * PAD], s[:, PAD:2 * PAD], u[:, PAD:2 * PAD], ALU.subtract).then_inc(pooled, 1)
                dve.wait_ge(pooled, KS * l + g + 1)

            def rotate(l, j):
                n = STATE_TILES * l + j
                q, b = j // 4, (j // 4) % 2
                dve.wait_ge(bu_done, n + 1)
                if q >= 2 and j % 4 == 0:
                    dve.wait_ge(prod_ready, STATE_TILES * l + 4 * (q - 1))
                elif l and j % 4 == 0:
                    dve.wait_ge(prod_ready, STATE_TILES * l)
                w = wave_v[:, b, j % 4]
                bu = ps[:, 4 + n % 2, :]
                cos = table[:, 0, j:j + 1, :].broadcast_to([P, 4, HALF])
                sin = table[:, 1, j:j + 1, :].broadcast_to([P, 2, HALF])
                add(tt(w.rearrange("p r (s t) -> p (r s) t", t=HALF), bu.rearrange("p (s t) -> p s t", t=HALF), cos, ALU.mult))
                r2 = rot[:, 0:512].rearrange("p (r s t) -> p r s t", r=2, t=HALF)
                add(tt(r2[:, 0], bu[:, T:2 * T].rearrange("p (s t) -> p s t", t=HALF), sin, ALU.mult))
                tt(r2[:, 1], bu[:, 0:T].rearrange("p (s t) -> p s t", t=HALF), sin, ALU.mult).then_inc(rotated, 1)
                dve.wait_ge(rotated, n + 1)
                add(tt(w[:, 0, :], w[:, 0, :], rot[:, 0:T], ALU.add))
                link(tt(w[:, 1, :], w[:, 1, :], rot[:, T:2 * T], ALU.subtract))

            def scan(l, q):
                w = wave_v[:, q % 2]
                for half in range(2):
                    for j in range(4):
                        mag = MAG[:, STATE_TILES * l + 4 * q + j:STATE_TILES * l + 4 * q + j + 1].broadcast_to([P, HALF])
                        for r in range(2):
                            z = w[:, j, r, HALF * half:HALF * half + HALF]
                            init = carry[:, 2 + r, j:j + 1] if half else 0.0
                            last = nc.vector.tensor_tensor_scan(z, mag, z, init, ALU.mult, ALU.add)
                            if half and (j, r) == (3, 1):
                                last.then_inc(z_ready, 1)
                            else:
                                add(last)
                    if not half:
                        settle()
                        zr, zi = w[:, :, 0, HALF - 1:HALF].rearrange("p j t -> p (j t)"), w[:, :, 1, HALF - 1:HALF].rearrange("p j t -> p (j t)")
                        c, s = turn[:, 0, 4 * q:4 * q + 4], turn[:, 1, 4 * q:4 * q + 4]
                        add(tt(carry[:, 0, :], zr, c, ALU.mult))
                        add(tt(carry[:, 1, :], zi, s, ALU.mult))
                        link(tt(carry[:, 3, :], zr, s, ALU.mult))
                        link(tt(carry[:, 2, :], carry[:, 0, :], carry[:, 1, :], ALU.subtract))
                        link(tt(carry[:, 0, :], zi, c, ALU.mult))
                        link(tt(carry[:, 3, :], carry[:, 3, :], carry[:, 0, :], ALU.add))

            def layer_norm(i, sources, tensor, last_of=None, scaled=True):
                if scaled:
                    for half, (wait, bank, release) in enumerate(sources):
                        wait()
                        for t in range(TT):
                            xt = tensor[:, t, 512 * half:512 * half + 512]
                            last = stt(xt, xt, ALPHA, bank(t), ALU.mult, ALU.add)
                            if t == TT - 1:
                                release(last)
                            else:
                                add(last)
                    settle()
                    last_of()
                st = tiny[:, 32:56].rearrange("p (t h s) -> p t h s", t=TT, h=2)
                for t in range(TT):
                    for half in range(2):
                        add(nc.vector.bn_stats(st[:, t, half, :], tensor[:, t, 512 * half:512 * half + 512]))
                    settle()
                    link(nc.vector.bn_aggr(tiny[:, 4 * t:4 * t + 2], st[:, t, :, :].rearrange("p h s -> p (h s)")))
                    ts(tiny[:, 8 + t:9 + t], tiny[:, 4 * t + 1:4 * t + 2], LN_EPS, None, ALU.add).then_inc(ln_var, 1)
                for t in range(TT):
                    dve.wait_ge(ln_rstd, TT * i + t + 1)
                    stt(tiny[:, 4 * t + 3:4 * t + 4], tiny[:, 4 * t:4 * t + 1], -1.0, tiny[:, 4 * t + 2:4 * t + 3],
                        ALU.mult, ALU.mult).then_inc(ln_shift, 1)

                def rest(t):
                    dve.wait_ge(ln_norm, TT * i + t + 1)
                    if t == 0:
                        dve.wait_ge(ln_in, 32 * (i + 1))
                    link(tt(tensor[:, t, :], tensor[:, t, :], ln_gb[:, 0, :], ALU.mult))
                    tt(tensor[:, t, :], tensor[:, t, :], ln_gb[:, 1, :], ALU.add).then_inc(ln_done if i < 5 else out_ready, 1)
                return rest

            def paired_source(name, half_tokens):
                g = gemms[name]
                return (lambda: gemm_ended(dve, name), lambda t: ps[:, 2 * g["pair"] + t, :], lambda ins: freed(ins, name))

            def lo_of_x(i):
                for t in range(TT):
                    dve.wait_ge(xt_hi, TT * i + t + 1)
                    src = ps[:, 4 + 2 * t:6 + 2 * t, :].rearrange("p b (k t) -> p (b k) t", t=P)
                    tt(xs[:, 8:16, t * P:(t + 1) * P], src, xs[:, 0:8, t * P:(t + 1) * P].bitcast(F32),
                       ALU.subtract).then_inc(xt_ready, 1)

            for l in range(DEPTH):
                dve.wait_ge(table_ready, l + 1)
                dve.wait_ge(bc_in[l], 48)
                base = ssm_units(l)
                add(ts(c_t[:, 1, :], c_t[:, 0, :], -1.0, None, ALU.mult))
                ts(c_t[:, 2, :], c_t[:, 2, :], -1.0, None, ALU.mult).then_inc(c_ready, 1)
                for i in range(STATE_TILES):
                    splits_to(base + 1 + i)
                    rotate(l, i)
                    if i % 4 == 3:
                        scan(l, i // 4)
                    if i in (4, 6, 8, 10):
                        if i == 4:
                            evacuated(dve, ("in", l, 1))
                        window_means(l, (i - 4) // 2)
                splits_to(base + SSM_SLOTS)
                splits_to(gemms[("v", l, 1)]["end"])
                dve.wait_ge(y_used, STATE_TILES * (l + 1))
                for f in range(KS):
                    last = stt(y_v[:, f, :], u_sb[:, f, :], small[:, 0, l, f:f + 1], ps[:, 6 + f // 2, T * (f % 2):T * (f % 2) + T],
                               ALU.mult, ALU.add)
                    if f < KS - 1:
                        add(last)
                last.then_inc(y_linear, 1)
                dve.wait_ge(pool_scaled, l + 1)
                gemm_ended(dve, ("in", l, 5))
                hi_lo(xs[:, 8:12, :], xs[:, 12:16, :], u_pool[:, :, PAD:PAD + T], ps_ready)
                dve.wait_ge(y_gelu, l + 1)
                hi_lo(xs[:, 0:4, :], xs[:, 4:8, :], y_v, ys_ready)

                def gate_pool(c):
                    name = ("pool_up", l, c)
                    splits_to(gemms[name]["end"])
                    gemm_ended(dve, name)
                    g = gates[:, 8 + 4 * c:12 + 4 * c, :]
                    freed(tt(g, blocks(pair_of(name)), g, ALU.mult), name)

                gate_pool(0)
                splits_to(gemms[("glu", l, 0)]["end"])
                evacuated(dve, ("glu", l, 0))
                link(tt(y_v, y_v, u_sb[:, :, :], ALU.mult))
                hi_lo(xs[:, 0:4, :], xs[:, 4:8, :], y_v, ys_ready)
                gate_pool(1)
                for c in range(2):
                    name = ("ssm_up", l, c)
                    splits_to(gemms[name]["end"])
                    gemm_ended(dve, name)
                    g = gates[:, 4 * c:4 * c + 4, :]
                    freed(tt(g, blocks(pair_of(name)), g, ALU.mult), name)
                    evacuated(dve, name)
                    evacuated(dve, ("pool_up", l, c))
                    link(tt(g, g, gates[:, 8 + 4 * c:12 + 4 * c, :], ALU.add))
                    hi_lo(mx[:, 4 * c:4 * c + 4, :], mx[:, 8 + 4 * c:12 + 4 * c, :], g, mx_ready)
                splits_to(gemms[("out", l, 1)]["end"])
                if l == 0:
                    dve.wait_ge(xtok_in, 16)
                rest = layer_norm(3 * l, [paired_source(("out", l, c), c) for c in range(2)], x_tok,
                                  lambda: evacuated(dve, ("out", l, 1)))
                k_first, k_last = gemms[("k", l, 0 if l == 0 else 1)]["first"], gemms[("k", l, 1)]["end"]
                splits_to(k_first + 2)
                rest(0)
                splits_to(k_first + 4)
                rest(1)
                splits_to(k_last)
                lo_of_x(3 * l)
                splits_to(gemms[("q", l, 1)]["end"])
                for h in range(HEADS + 2):
                    if h < HEADS:
                        n, o = HEADS * l + h, 4 * (h % 2)
                        dve.wait_ge(score_done, n + 1)
                        link(nc.vector.tensor_reduce(tiny[:, 56:58], ps[:, 4 + h % 2, :].rearrange("p (t m) -> p t m", t=TT), AX_X, ALU.max))
                        ts(tiny[:, 16 + o:18 + o], tiny[:, 56:58], -1.0, None, ALU.mult).then_inc(score_max, 1)
                        dve.wait_ge(score_max, n + 1)
                    if 1 <= h <= HEADS:
                        g = h - 1
                        n, o = HEADS * l + g, 4 * (g % 2)
                        dve.wait_ge(prob_exp, n + 1)
                        link(nc.vector.reciprocal(tiny[:, 58:60], tiny[:, 24 + o:26 + o]))
                        for t in range(TT):
                            last = ts(probs[:, g % 2, t, :], probs[:, g % 2, t, :], tiny[:, 58 + t:59 + t], None, ALU.mult)
                            if t < TT - 1:
                                add(last)
                        last.then_inc(prob_ready, 1)
                        dve.wait_ge(prob_ready, n + 1)
                    if h >= 2:
                        g = h - 2
                        dve.wait_ge(at_hi, HEADS * l + g + 1)
                        tt(xs[:, 8 + 2 * g:10 + 2 * g, :], ps[:, g, :].rearrange("p (b t) -> p b t", t=T),
                           xs[:, 2 * g:2 * g + 2, :].bitcast(F32), ALU.subtract).then_inc(at_ready, 1)
                splits_to(gemms[("o", l, 1)]["end"])
                rest = layer_norm(3 * l + 1, [paired_source(("o", l, c), c) for c in range(2)], x_tok,
                                  lambda: evacuated(dve, ("o", l, 1)))
                f0 = gemms[("o", l, 1)]["end"]
                if l == 0:
                    splits_to(f0 + 2)
                rest(0)
                if l == 0:
                    splits_to(f0 + 4)
                rest(1)
                lo_of_x(3 * l + 1)
                if l == 0:
                    for c, cols in enumerate(FF_CHUNKS):
                        name, f = ("ffn3", c), cols // P
                        splits_to(gemms[name]["end"])
                        gemm_ended(dve, name)
                        evacuated(dve, ("ffn1", c))
                        if c >= 2:
                            gemm_ended(dve, ("ffn2", c - 2, 1))
                        h_ = sil_v[:, c % 2, 0:f, :]
                        freed(tt(h_, blocks(pair_of(name))[:, 0:f, :], h_, ALU.mult), name)
                        evacuated(dve, name)
                        hi_lo(hs[:, c % 2, 0, 0:f, :], hs[:, c % 2, 1, 0:f, :], h_, hs_ready)
                    last = ("ffn2", len(FF_CHUNKS) - 1, 1)
                    splits_to(gemms[last]["end"])
                    rest = layer_norm(2, [(lambda h=h: gemm_ended(dve, ("ffn2", len(FF_CHUNKS) - 1, h)),
                                           lambda t, h=h: ps[:, 4 + 2 * t + h, :], add) for h in range(2)], x_tok, lambda: None)
                    f0 = gemms[last]["end"]
                    splits_to(f0 + 2)
                    rest(0)
                    splits_to(f0 + 4)
                    rest(1)
                    lo_of_x(2)

            lg, eq, oh1, oh2, lg2, both, rank, dexp, hi_r, tmp = [rt[:, i] for i in range(10)]
            m1, m2, diff, ex, idx, i1, i2 = [rs[:, i] for i in range(7)]

            def per_token(x):
                return x.unsqueeze(2).broadcast_to([P, TT, EXPERTS])

            def per_expert(x):
                return x.unsqueeze(1).broadcast_to([P, TT, EXPERTS])

            dve.wait_ge(ln_done, 2 * 5)
            dve.wait_ge(logits_done, 1)
            link(nc.vector.tensor_copy(lg, ps[:, 4, 0:TT * EXPERTS].rearrange("p (t e) -> p t e", t=TT)))

            def best(scores, m, i_, oh):
                link(nc.vector.tensor_reduce(m, scores, AX_X, ALU.max))
                link(tt(eq, scores, per_token(m), ALU.is_equal))
                link(ts(tmp, per_expert(iota8[:, :]), -8.0, None, ALU.add))
                link(tt(eq, eq, tmp, ALU.mult))
                link(nc.vector.tensor_reduce(i_, eq, AX_X, ALU.min))
                link(ts(i_, i_, 8.0, None, ALU.add))
                link(tt(oh, per_expert(iota8[:, :]), per_token(i_), ALU.is_equal))

            best(lg, m1, i1, oh1)
            link(stt(lg2, oh1, -1e30, lg, ALU.mult, ALU.add))
            best(lg2, m2, i2, oh2)
            tt(diff, m2, m1, ALU.subtract).then_inc(expo_in, 1)
            tt(both, oh1, oh2, ALU.add).then_inc(picked, 1)
            dve.wait_ge(expo_done, 1)
            link(ts(idx, ex, 1.0, None, ALU.add))
            link(nc.vector.reciprocal(gate_w[:, 0, :], idx))
            link(tt(gate_w[:, 1, :], ex, gate_w[:, 0, :], ALU.mult))
            dve.wait_ge(xts_hi, 1)
            tt(xts[:, 1, :, :], x_tok[:, :, :], xts[:, 0, :, :].bitcast(F32), ALU.subtract).then_inc(xts_ready, 1)
            dve.wait_ge(ranked, 1)
            link(nc.vector.tensor_copy(rank, ps[:, 5, 0:TT * EXPERTS].rearrange("p (t e) -> p t e", t=TT)))
            cnt, over_, incl, pos, base_o, sel_o, one8 = [ovf[:, i, :] for i in range(7)]
            link(nc.vector.memset(one8, 1.0))
            link(nc.vector.tensor_copy(cnt, ps[:, 5, TT * EXPERTS:(TT + 1) * EXPERTS]))
            link(ts(over_, cnt, 128.0, None, ALU.is_gt))
            link(nc.vector.tensor_tensor_scan(incl, one8, over_, 0.0, ALU.mult, ALU.add))
            link(tt(pos, incl, over_, ALU.subtract))
            link(ts(base_o, iota8[:, :], -128.0, 128.0 * (EXPERTS - 1), ALU.mult, ALU.add))
            link(stt(base_o, pos, 128.0, base_o, ALU.mult, ALU.add))
            link(ts(hi_r, rank, 128.0, None, ALU.is_ge))
            link(tt(hi_r, hi_r, per_expert(base_o), ALU.mult))
            link(tt(dexp, rank, hi_r, ALU.add))
            link(stt(dexp, per_expert(iota8[:, :]), 128.0, dexp, ALU.mult, ALU.add))
            for k, oh in enumerate((oh1, oh2)):
                link(tt(tmp, oh, dexp, ALU.mult))
                link(nc.vector.tensor_reduce(dest[:, k, :], tmp, AX_X, ALU.add))
            link(nc.vector.memset(jobs_f[:, :], 0.0))
            link(nc.vector.tensor_copy(jobs_f[:, 0:1], incl[:, EXPERTS - 1:EXPERTS]))
            for o in range(OVER_MAX):
                link(stt(sel_o, pos, float(o), over_, ALU.is_equal, ALU.mult))
                link(tt(sel_o, sel_o, iota8[:, :], ALU.mult))
                link(nc.vector.tensor_reduce(jobs_f[:, 1 + o:2 + o], sel_o, AX_X, ALU.add))
            nc.vector.tensor_copy(jobs[:, :], jobs_f[:, :]).then_inc(routed, 1)

            dve.wait_ge(moe_in, 32)

            def select():
                for t in range(TT):
                    link(ts(gsel2[:, t, :], iota[:, :], dest[:, 0, t:t + 1], None, ALU.is_equal))
                    last = stt(sel[:, t, :], iota[:, :], dest[:, 1, t:t + 1], gsel2[:, t, :], ALU.is_equal, ALU.add)
                    if t < TT - 1:
                        add(last)
                last.then_inc(sel_ready, 1)

            def select_gated():
                for t in range(TT):
                    add(ts(gsel[:, t, :], iota[:, :], dest[:, 0, t:t + 1], gate_w[:, 0, t:t + 1], ALU.is_equal, ALU.mult))
                    link(ts(gsel2[:, t, :], iota[:, :], dest[:, 1, t:t + 1], gate_w[:, 1, t:t + 1], ALU.is_equal, ALU.mult))
                    last = tt(gsel[:, t, :], gsel[:, t, :], gsel2[:, t, :], ALU.add)
                    if t < TT - 1:
                        add(last)
                last.then_inc(gsel_ready, 1)

            nc.vector.memset(gsel_t[:, :, :], 0.0).then_inc(w3_free, 1)
            nc.vector.memset(y_sb[:, :], 0.0).then_inc(y_ready, 1)
            select()

            def add_out(r, turn_):
                dve.wait_ge(misc_filled, 4 + r + 1 + turn_)
                piece = acc[:, r // 2, 512 * (r % 2):512 * (r % 2) + 512]
                tt(piece, ps[:, 6 + r % 2, :], piece, ALU.add).then_inc(misc_free[r % 2], 1)

            def job(j, steps):
                order.turns = steps * j
                done = [LEAD]

                def through(n):
                    while done[0] < n + LEAD:
                        split_lo(N0 + done[0], NJ * j)
                        done[0] += 1

                for i, (kind, c) in enumerate(stages):
                    through(4 * i + 4)
                    ended = N0 + 4 * i + 4
                    if (kind, c) == ("w1", 0):
                        dve.wait_ge(misc_filled, 4 + 16 * j)
                        select_gated()
                        dve.wait_ge(gsel_ready, 1 + j)
                        link(ts(dest[:, :, :], dest[:, :, :], -128.0, None, ALU.add))
                        select()
                    if kind == "w3":
                        dve.wait_ge(unit_used, ended + NJ * j)
                        dve.wait_ge(w1_free, 2 + c + FE_CHUNKS * j)
                        tt(he[:, c % 2, :], ps[:, 2 * (c % 2) + 1, :], he[:, c % 2, :], ALU.mult).then_inc(w3_free, 1)
                    if (kind, c) == ("w3", 0):
                        for r in range(4):
                            add_out(r, 16 * j)
                    if kind == "w1" and c:
                        turned_lo(c - 1, 4 + c, j)
                    if (kind, c) == ("w2", FE_CHUNKS - 2):
                        turned_lo(FE_CHUNKS - 1, 15, j)

            def turned_lo(c, r, j):
                dve.wait_ge(het_hi, c + 1 + FE_CHUNKS * j)
                tt(het[:, c % 2, 1, :, :], ps[:, 6 + r % 2, :].rearrange("p (k s) -> p k s", s=P),
                   het[:, c % 2, 0, :, :].bitcast(F32), ALU.subtract).then_inc(misc_free[r % 2], 1)

            JOB_STEPS = 9
            with dve.Fori(0, EXPERTS) as j:
                before = order.n
                job(j, JOB_STEPS)
                assert order.n - before == JOB_STEPS, order.n - before
            order.n = before
            over = dve.value_load(jobs[0:1, 0:1], min_val=0, max_val=OVER_MAX)
            for o in range(OVER_MAX):
                with dve.If(over > o):
                    order.n = before
                    job(EXPERTS + o, JOB_STEPS)
                dve.nop()
            order.sem, order.n, order.turns = dve_tail, 0, 0
            for r in range(4):
                add_out(r, over * 16 + EXPERTS * 16)
            dve.wait_ge(misc_free[0], over * 8 + (2 + 8 * EXPERTS + 2))
            dve.wait_ge(misc_free[1], over * 8 + (2 + 8 * EXPERTS + 2))
            rest = layer_norm(5, None, acc, None, scaled=False)
            rest(0)
            rest(1)

        @block.gpsimd
        def _(pool):
            order = Order(pool, pool_order)

            def load_ln(i):
                l, which = divmod(i, 3)
                g, b = (("ln_mix_g", "ln_mix_b"), ("ln_xa_g", "ln_xa_b"), ("ln_ffn_g", "ln_ffn_b"))[which]
                if i:
                    pool.wait_ge(ln_done, TT * i)
                pool.dma_start(ln_gb[:, 0, :], a[g][l:l + 1, :].broadcast_to([P, D])).then_inc(ln_in, 16)
                pool.dma_start(ln_gb[:, 1, :], a[b][l:l + 1, :].broadcast_to([P, D])).then_inc(ln_in, 16)

            def deviation(i):
                for t in range(TT):
                    pool.wait_ge(ln_var, TT * i + t + 1)
                    nc.gpsimd.tensor_tensor(tiny[:, 4 * t + 2:4 * t + 3], tiny[:, 8 + t:9 + t], tiny[:, 60:61],
                                            ALU.pow).then_inc(ln_rstd, 1)

            order.link(nc.gpsimd.memset(tiny[:, 60:61], -0.5))
            load_ln(0)
            for l in range(DEPTH):
                for j in range(STATE_TILES):
                    n = STATE_TILES * l + j
                    if j % 4 == 0:
                        pool.wait_ge(z_ready, 4 * l + j // 4 + 1)
                    if n >= 2:
                        pool.wait_ge(y_used, n - 1)
                    z = wave_v[:, (j // 4) % 2, j % 4].rearrange("p r (s t) -> p (r s) t", t=HALF)
                    for k in range(2):
                        tab = table[:, k, j:j + 1, :].broadcast_to([P, 4, HALF])
                        dst = prod_v[:, j % 2, k].rearrange("p r (s t) -> p (r s) t", t=HALF)
                        last = nc.gpsimd.tensor_tensor(dst, z, tab, ALU.mult)
                        if k == 0:
                            order.add(last)
                    last.then_inc(prod_ready, 1)
                deviation(3 * l)
                load_ln(3 * l + 1)
                deviation(3 * l + 1)
                load_ln(3 * l + 2)
                if l == 0:
                    pool.wait_ge(y_used, STATE_TILES)
                    pool.dma_start(c_t[:, 0, :], a["ssm_c"][1, 0]).then_inc(bc_in[1], 16)
                    pool.dma_start(c_t[:, 2, :], a["ssm_c"][1, 1]).then_inc(bc_in[1], 16)
                    pool.dma_start(b_in, a["ssm_b"][1]).then_inc(bc_in[1], 16)
                    pool.dma_start(pool_w[:, :, :], a["pool_wt"][1]).then_inc(poolw_in[1], 16)
                    pool.wait_ge(bc_in[1], 48)
                    pool.wait_ge(prep_ready, 1)
                    phase_table(nc.gpsimd, order, 1, table_ready, lambda m: None)
                    discretise(nc.gpsimd, order, 1, bb_ready)
                    deviation(2)
                    load_ln(3)
            pool.wait_ge(ln_done, 2 * 5)
            pool.dma_start(tri[:, :], a["c_tri"]).then_inc(moe_in, 16)
            pool.dma_start(iota[:, :], a["c_iota"]).then_inc(moe_in, 16)
            nc.gpsimd.memset(ones[:, :], 1.0).then_inc(ones_ready, 1)
            deviation(5)

        @block.tensor
        def _(pe):
            mm = nc.tensor.matmul

            def take(n, cols, shift=0):
                pe.wait_ge(hi_ready, n + 1 + shift)
                return view(w_hi, SPLIT, n, cols), view(w_lo, SPLIT, n, cols)

            def claim(name):
                g = gemms[name]
                if g["use"]:
                    pe.wait_ge(pair_free[g["pair"]], g["use"])

            def by_feature(name, hi, lo, hook=None):
                g = gemms[name]
                claim(name)
                out_ = blocks(pair_of(name))
                fs, k = g["cols"] // P, 0
                for n in range(g["first"], g["end"]):
                    wh, wl = take(n, g["cols"])
                    for i in range(g["k"]):
                        for f in range(fs):
                            w = wh[:, i, f * P:(f + 1) * P]
                            mm(out_[:, f, :], w, hi(k + i), start=(k + i == 0 and f % 2 == 0), stop=False, skip_group_check=True)
                            mm(out_[:, f, :], w, lo(k + i), start=False, stop=False, skip_group_check=True)
                    pe.wait_ge(lo_ready, n + 1)
                    for i in range(g["k"]):
                        for f in range(fs):
                            last = mm(out_[:, f, :], wl[:, i, f * P:(f + 1) * P], hi(k + i), start=False,
                                      stop=(n == g["end"] - 1 and i == g["k"] - 1), skip_group_check=True)
                    last.then_inc(unit_used, 1)
                    k += g["k"]
                    if hook:
                        hook(n)

            def by_token(name, hi, lo, banks=None, first_=True, last_=True, hook=None):
                g = gemms[name]
                if banks is None:
                    claim(name)
                    banks = [2 * g["pair"] + t for t in range(TT)]
                k = 0
                for n in range(g["first"], g["end"]):
                    wh, wl = take(n, g["cols"])
                    for i in range(g["k"]):
                        for t in range(TT):
                            mm(ps[:, banks[t], :], hi(k + i, t), wh[:, i, :], start=(first_ and k + i == 0), stop=False, skip_group_check=True)
                            mm(ps[:, banks[t], :], lo(k + i, t), wh[:, i, :], start=False, stop=False, skip_group_check=True)
                    pe.wait_ge(lo_ready, n + 1)
                    for i in range(g["k"]):
                        for t in range(TT):
                            last = mm(ps[:, banks[t], :], hi(k + i, t), wl[:, i, :], start=False,
                                      stop=(last_ and n == g["end"] - 1 and i == g["k"] - 1), skip_group_check=True)
                    last.then_inc(unit_used, 1)
                    k += g["k"]
                    if hook:
                        hook(n)

            def pair(t, lo_at):
                return (lambda k, q=None: t[:, k, :] if q is None else t[:, k, q * P:(q + 1) * P],
                        lambda k, q=None: t[:, lo_at + k, :] if q is None else t[:, lo_at + k, q * P:(q + 1) * P])

            x_hl, mem_hl, mx_hl = pair(xs, 8), pair(ms, 8), pair(mx, 8)
            y_hl = pair(xs, 4)
            p_hl = (lambda k: xs[:, 8 + k, :], lambda k: xs[:, 12 + k, :])

            def turn_b(l):
                pe.wait_ge(bb_ready, l + 1)
                for r in range(2):
                    for q in range(KS):
                        last = nc.tensor.transpose(ps[:, 4 + r, q * P:(q + 1) * P], bb[:, r, q * P:(q + 1) * P], ident[:, :])
                last.then_inc(bt_done, 1)

            def ssm_step(l, i):
                if i == 0:
                    pe.wait_ge(bt_ready, l + 1)
                    evacuated(pe, ("in", l, 0))
                if i < STATE_TILES:
                    n, q, row = STATE_TILES * l + i, i // 4, 32 * (i % 4)
                    if i >= 2:
                        pe.wait_ge(rotated, n - 1)
                    for r in range(2):
                        last = mm(ps[:, 4 + n % 2, r * T:(r + 1) * T], b_t[row:row + 32, r, q, :], u_sb[row:row + 32, q, :],
                                  start=True, stop=True, tile_position=(row, 0))
                    last.then_inc(bu_done, 1)
                if Y_LAG <= i < STATE_TILES + Y_LAG:
                    j = i - Y_LAG
                    n, q, row = STATE_TILES * l + j, j // 4, 32 * (j % 4)
                    if j == 0:
                        pe.wait_ge(c_ready, l + 1)
                    pe.wait_ge(prod_ready, n + 1)
                    p = prod_v[:, j % 2]
                    parts = ((0, p[:, 0, 0, :]), (1, p[:, 1, 1, :]), (2, p[:, 1, 0, :]), (2, p[:, 0, 1, :]))
                    for s, (c, mov) in enumerate(parts):
                        last = mm(ps[row:row + 32, 6 + q // 2, T * (q % 2):T * (q % 2) + T], c_t[:, c, 32 * j:32 * j + 32], mov,
                                  start=(s == 0), stop=(s == 3), tile_position=(0, row), skip_group_check=True)
                    last.then_inc(y_used, 1)

            def turn_x(i):
                for t in range(TT):
                    pe.wait_ge(ln_done, TT * i + t + 1)
                    for k in range(KD):
                        last = nc.tensor.transpose(ps[:, 4 + 2 * t + k // 4, P * (k % 4):P * (k % 4) + P],
                                                   x_tok[:, t, k * P:(k + 1) * P], ident[:, :])
                    last.then_inc(xt_done, 1)

            pe.wait_ge(xs_ready, 1)
            for l in range(DEPTH):
                if l:
                    pe.wait_ge(xt_ready, TT * 3)
                by_feature(("in", l, 0), *x_hl)
                if l == 0:
                    pe.wait_ge(small_in, 96)
                turn_b(l)
                base = ssm_units(l)
                step = lambda n: ssm_step(l, n - base) if n >= base else None
                for c in range(1, 6):
                    by_feature(("in", l, c), *x_hl, hook=step)
                pe.wait_ge(ms_ready, 1)
                for c in ((0, 1) if l == 0 else (1,)):
                    by_token(("v", l, c), *mem_hl, hook=step)
                assert gemms[("v", l, 1)]["end"] - base == SSM_SLOTS
                pe.wait_ge(pooled, KS * (l + 1))
                pe.wait_ge(poolw_in[l], 16)
                pe.wait_ge(rotated, STATE_TILES * (l + 1))
                for g in range(KS):
                    last = mm(ps[:, 4 + g // 2, T * (g % 2):T * (g % 2) + T], pool_w[:, g, :], u_pool[:, g, PAD:PAD + T],
                              start=True, stop=True)
                last.then_inc(pool_mixed, 1)
                pe.wait_ge(ps_ready, l + 1)
                by_feature(("pool_up", l, 0), *p_hl)
                pe.wait_ge(ys_ready, 2 * l + 1)
                by_feature(("glu", l, 0), *y_hl)
                by_feature(("pool_up", l, 1), *p_hl)
                pe.wait_ge(ys_ready, 2 * l + 2)
                by_feature(("ssm_up", l, 0), *y_hl)
                by_feature(("ssm_up", l, 1), *y_hl)
                pe.wait_ge(mx_ready, 2 * l + 2)
                by_token(("out", l, 0), *mx_hl)
                by_token(("out", l, 1), *mx_hl)
                for c in ((0, 1) if l == 0 else (1,)):
                    by_feature(("k", l, c), *mem_hl)
                turn_x(3 * l)
                pe.wait_ge(xt_ready, TT * (3 * l + 1))
                by_feature(("q", l, 0), *x_hl)
                by_feature(("q", l, 1), *x_hl)
                for c in range(2):
                    evacuated(pe, ("q", l, c))
                    evacuated(pe, ("k", l, c))
                for h in range(HEADS + 1):
                    if h < HEADS:
                        n = HEADS * l + h
                        if h >= 2:
                            pe.wait_ge(prob_exp, n - 1)
                        for t in range(TT):
                            for e in range(2):
                                last = mm(ps[:, 4 + h % 2, T * t:T * t + T], q_v[:, 2 * h + e, t * P:(t + 1) * P],
                                          k_sb[:, 2 * h + e, :], start=(e == 0), stop=(e == 1), skip_group_check=True)
                        last.then_inc(score_done, 1)
                    if h >= 1:
                        g = h - 1
                        n = HEADS * l + g
                        pe.wait_ge(prob_ready, n + 1)
                        if g >= 2:
                            pe.wait_ge(pt_ready, n - 1)
                        for t in range(TT):
                            for m in range(2):
                                last = nc.tensor.transpose(ps[:, 6 + g % 2, T * m + P * t:T * m + P * t + P],
                                                           probs[:, g % 2, t, m * P:(m + 1) * P], ident[:, :])
                        last.then_inc(pt_done, 1)
                        pe.wait_ge(pt_ready, n + 1)
                        for e in range(2):
                            for m in range(2):
                                last = mm(ps[:, g, T * e:T * e + T], v_sb[:, m, T * g + P * e:T * g + P * e + P],
                                          probs_t[:, g % 2, m, :], start=(m == 0), stop=(m == 1), skip_group_check=True)
                        last.then_inc(pv_done, 1)
                pe.wait_ge(at_ready, HEADS * (l + 1))
                by_token(("o", l, 0), *x_hl)
                by_token(("o", l, 1), *x_hl)
                if l == 0:
                    by_token(("v", 1, 0), *mem_hl)
                turn_x(3 * l + 1)
                pe.wait_ge(xt_ready, TT * (3 * l + 2))
                if l == 0:
                    def down(c):
                        pe.wait_ge(hs_ready, c + 1)
                        hi = lambda k, t: hs[:, c % 2, 0, k, t * P:(t + 1) * P]
                        lo = lambda k, t: hs[:, c % 2, 1, k, t * P:(t + 1) * P]
                        for h in range(2):
                            by_token(("ffn2", c, h), hi, lo, banks=[4 + h, 6 + h], first_=(c == 0), last_=(c == len(FF_CHUNKS) - 1))

                    for c in range(len(FF_CHUNKS)):
                        by_feature(("ffn1", c), *x_hl)
                        by_feature(("ffn3", c), *x_hl)
                        if c:
                            down(c - 1)
                    down(len(FF_CHUNKS) - 1)
                    by_feature(("k", 1, 0), *mem_hl)
                    turn_x(2)

            pe.wait_ge(router_ready, 1)
            rhs = [router_s[:, i, :].rearrange("p (k e) -> p k e", e=EXPERTS) for i in range(2)]
            for t in range(TT):
                for k in range(KD):
                    for s, (x_part, r_part) in enumerate(((0, 0), (8, 0), (0, 1))):
                        last = mm(ps[:, 4, t * EXPERTS:(t + 1) * EXPERTS], xs[:, x_part + k, t * P:(t + 1) * P], rhs[r_part][:, k, :],
                                  start=(t == 0 and k == 0 and s == 0), stop=(k == KD - 1 and s == 2), skip_group_check=True)
            last.then_inc(logits_done, 1)
            pe.wait_ge(picked, 1)
            pe.wait_ge(moe_in, 32)
            pe.wait_ge(ones_ready, 1)
            both = rt[:, 5]
            products = ((0, tri, 0), (1, tri, 1), (1, ones, 0), (2, ones, 0), (2, ones, 1))
            for i, (o, m, t) in enumerate(products):
                last = mm(ps[:, 5, o * EXPERTS:(o + 1) * EXPERTS], m[:, :], both[:, t, :], start=(i == 0), stop=True,
                          skip_group_check=True)
            last.then_inc(ranked, 1)

            def gather(i, r, turn_):
                for k in range(4):
                    for t in range(TT):
                        d0 = P * (4 * (i % 2) + k)
                        last = mm(ps[:, 6 + r % 2, k * P:(k + 1) * P], xts[:, i // 2, t, d0:d0 + P], sel[:, t, :],
                                  start=(t == 0), stop=(t == TT - 1), skip_group_check=True)
                last.then_inc(misc_filled, 1)

            def bank_free(r, turn_):
                pe.wait_ge(misc_free[r % 2], 2 + r // 2 + turn_)

            def scatter(r):
                return mm(ps[:, 6 + r % 2, :], gsel_t[:, r // 2, :], y_sb[:, 512 * (r % 2):512 * (r % 2) + 512], start=True, stop=True)

            pe.wait_ge(xts_ready, 1)
            pe.wait_ge(sel_ready, 1)
            for i in range(4):
                if i >= 2:
                    pe.wait_ge(misc_free[i % 2], 1)
                gather(i, i, 0)

            def job(j):
                def up(kind, c):
                    first_ = N0 + stage_at[(kind, c)]
                    bank = 2 * (c % 2) + (kind == "w3")
                    pe.wait_ge(w1_free if kind == "w1" else w3_free, (1 if c < 2 else c) + 7 * j)
                    for n in range(4):
                        wh, wl = take(first_ + n, 512, NJ * j)
                        for i in range(2):
                            k = 2 * n + i
                            mm(ps[:, bank, :], xe[:, 0, k, :], wh[:, i, :], start=(k == 0), stop=False, skip_group_check=True)
                            mm(ps[:, bank, :], xe[:, 1, k, :], wh[:, i, :], start=False, stop=False, skip_group_check=True)
                        pe.wait_ge(lo_ready, first_ + n + 1 + NJ * j)
                        for i in range(2):
                            k = 2 * n + i
                            last = mm(ps[:, bank, :], xe[:, 0, k, :], wl[:, i, :], start=False, stop=(k == 7), skip_group_check=True)
                        last.then_inc(unit_used, 1)

                def turned(c, r):
                    pe.wait_ge(w3_free, 1 + c + 1 + 7 * j)
                    bank_free(r, 8 * j)
                    for k in range(4):
                        last = nc.tensor.transpose(ps[:, 6 + r % 2, k * P:(k + 1) * P], he[:, c % 2, k * P:(k + 1) * P], ident[:, :])
                    last.then_inc(misc_filled, 1)

                def down(c, r, between=None):
                    first_ = N0 + stage_at[("w2", c)]
                    pe.wait_ge(misc_free[r % 2], 2 + r // 2 + 1 + 8 * j)
                    for n in range(4):
                        h, k0 = n // 2, 2 * (n % 2)
                        wh, wl = take(first_ + n, 512, NJ * j)
                        for i in range(2):
                            mm(ps[:, 4 + h, :], het[:, c % 2, 0, k0 + i, :], wh[:, i, :], start=(c == 0 and k0 + i == 0), stop=False, skip_group_check=True)
                            mm(ps[:, 4 + h, :], het[:, c % 2, 1, k0 + i, :], wh[:, i, :], start=False, stop=False, skip_group_check=True)
                        pe.wait_ge(lo_ready, first_ + n + 1 + NJ * j)
                        for i in range(2):
                            last = mm(ps[:, 4 + h, :], het[:, c % 2, 0, k0 + i, :], wl[:, i, :], start=False,
                                      stop=(c == FE_CHUNKS - 1 and k0 + i == 3), skip_group_check=True)
                        last.then_inc(unit_used, 1)
                        if between:
                            between(n)

                for b in range(2):
                    pe.wait_ge(misc_free[b], 2 + 8 * j)
                up("w1", 0)
                up("w3", 0)
                pe.wait_ge(y_ready, 1 + j)
                for r in range(4):
                    bank_free(r, 8 * j)
                    scatter(r).then_inc(misc_filled, 1)
                pe.wait_ge(gsel_ready, 1 + j)
                bank_free(4, 8 * j)
                for t in range(TT):
                    last = nc.tensor.transpose(ps[:, 6, t * P:(t + 1) * P], gsel[:, t, :], ident[:, :])
                last.then_inc(misc_filled, 1)
                for c in range(1, FE_CHUNKS):
                    up("w1", c)
                    turned(c - 1, 4 + c)
                    up("w3", c)
                    if c < FE_CHUNKS - 1:
                        down(c - 1, 4 + c)
                pe.wait_ge(sel_ready, 2 + j)
                for i in range(2):
                    bank_free(11 + i, 8 * j)
                    gather(i, 11 + i, 0)

                def between(n):
                    if n < 2:
                        bank_free(13 + n, 8 * j)
                        gather(2 + n, 13 + n, 0)
                    elif n == 2:
                        turned(FE_CHUNKS - 1, 15)
                down(FE_CHUNKS - 2, 4 + FE_CHUNKS - 1, between)
                down(FE_CHUNKS - 1, 15)

            with pe.Fori(0, EXPERTS) as j:
                job(j)
            over = pe.value_load(jobs[0:1, 0:1], min_val=0, max_val=OVER_MAX)
            for o in range(OVER_MAX):
                with pe.If(over > o):
                    job(EXPERTS + o)
                pe.nop()
            pe.wait_ge(y_ready, over + (1 + EXPERTS))
            for r in range(4):
                pe.wait_ge(misc_free[r % 2], over * 8 + (2 + r // 2 + 8 * EXPERTS))
                scatter(r).then_inc(misc_filled, 1)


def build(nc, arrays):
    a = {k: nc.dram_tensor(f"in_{k}", list(v.shape), F32, kind="ExternalInput").ap() for k, v in arrays.items()}
    out = nc.dram_tensor("out_0", [T, D], F32, kind="ExternalOutput").ap()
    build_trunk(nc, a, out)


_AS_THEY_ARE = ["ln_mix_g", "ln_mix_b", "w_in", "ssm_w_glu", "w_ssm_up", "w_pool_up", "w_out", "ln_xa_g", "ln_xa_b",
                "xa_wq", "xa_wk", "xa_wv", "xa_wo", "ln_ffn_g", "ln_ffn_b", "ffn_w1", "ffn_w3", "ffn_w2"]


def lay_out(inputs):
    import numpy as np
    i = {k: np.asarray(v) for k, v in inputs.items()}
    L = DEPTH
    a = {k: i[k] for k in _AS_THEY_ARE}
    for k in ("moe_w1", "moe_w3", "moe_w2"):
        a[k] = i[k][0]
    a["x"] = i["x"][0]
    for k, n in (("x_t", "x"), ("mem_t", "mem")):
        a[k] = i[n][0].T.reshape(KD, P, T).transpose(1, 0, 2)

    def states(v):
        return v.reshape(L, STATE_TILES, P).transpose(2, 0, 1).reshape(P, L * STATE_TILES)
    log_dt = np.broadcast_to(i["ssm_log_dt"][:, :, None], i["ssm_a_re"].shape)
    a["ssm_par"] = np.stack([states(i["ssm_a_re"]), states(i["ssm_a_im"]), states(log_dt)], axis=1)

    def block_diagonal(v):
        v = v.reshape(L, STATE_TILES, 2, P // 2, GROUP_W)
        z = np.zeros((L, 2, P // 2, STATE_TILES, 2, GROUP_W), v.dtype)
        for h in range(2):
            z[:, h, :, :, h, :] = v[:, :, h].transpose(0, 2, 1, 3)
        return z.reshape(L, P, STATE_TILES * 2 * GROUP_W)
    a["ssm_b"] = np.stack([block_diagonal(i["ssm_b_re"]), block_diagonal(i["ssm_b_im"])], axis=2)
    a["ssm_c"] = np.stack([block_diagonal(i["ssm_c_re"].transpose(0, 1, 3, 2)),
                           block_diagonal(i["ssm_c_im"].transpose(0, 1, 3, 2))], axis=1)
    a["chan_par"] = np.stack([i[n].reshape(L, KS, P).transpose(2, 0, 1) for n in ("ssm_d", "ssm_b_glu", "pool_scale")], axis=1)
    a["pool_wt"] = i["pool_w"].transpose(0, 2, 1, 3)
    a["router"] = i["moe_router"][0].reshape(KD, P, EXPERTS).transpose(1, 0, 2).reshape(P, KD * EXPERTS)
    f = np.float32
    a["c_ident"] = np.eye(P, dtype=f)
    a["c_tri"] = np.triu(np.ones((P, P), f), 1)
    a["c_iota"] = np.broadcast_to(np.arange(P, dtype=f), (P, P))
    a["c_iota8"] = np.broadcast_to(np.arange(EXPERTS, dtype=f), (P, EXPERTS))
    steps = np.arange(1, PAD + 1, dtype=f)
    a["c_inv"] = np.broadcast_to(np.stack([1.0 / np.minimum(steps, f(2 ** (g + 1))) for g in range(KS)]), (P, KS, PAD))
    return {k: np.ascontiguousarray(v) for k, v in a.items()}


def kernel(**inputs):
    import concourse.bacc as bacc
    from concourse.bass_utils import run_bass_kernel_spmd

    arrays = lay_out(inputs)
    nc = bacc.Bacc("TRN2", target_bir_lowering=False, num_devices=1)
    build(nc, arrays)
    r = run_bass_kernel_spmd(nc, [{f"in_{k}": v for k, v in arrays.items()}], core_ids=[0])
    return r.results[0]["out_0"].reshape(1, T, D)
```

```python
from contextlib import ExitStack

import concourse.bass as bass
from concourse import mybir

F32 = mybir.dt.float32
F32R = mybir.dt.float32r
I32 = mybir.dt.int32
ALU = mybir.AluOpType
ACT = mybir.ActivationFunctionType
AX_X = mybir.AxisListType.X

P = 128
D = 1024
T = 256
DEPTH = 2
KD = D // P
TT = T // P
SSM_W = 512
KS = SSM_W // P
GROUP_W = 16
STATE_TILES = 16
HALF = 128
PAD = 16
HEADS = 4
D_FF = 2816
FF_CHUNKS = [512] * 5 + [256]
EXPERTS = 8
D_FE = 3584
FE_CHUNKS = D_FE // 512
OVER_MAX = 3
ALPHA = (2 * DEPTH) ** 0.25
LN_EPS = 1e-5

RAW = 7
SPLIT = 4
LEAD = SPLIT - 1
UNIT = 1024
MAGIC = 12582912.0
TABLE_STEPS = [1, 2, 4, 8, 16, 32, 64]


def plan():
    units, gemms, uses = [], {}, [0, 0]

    def gemm(name, weight, stack, row0, rows, col0, cols, paired=True):
        per = UNIT // cols * P
        g = {"first": len(units), "cols": cols, "k": UNIT // cols}
        for r in range(row0, row0 + rows, per):
            units.append((weight, stack, r, UNIT // cols, col0, cols))
        g["end"] = len(units)
        if paired:
            g["pair"] = (uses[0] + uses[1]) % 2
            g["use"] = uses[g["pair"]]
            uses[g["pair"]] += 1
        gemms[name] = g

    def halves(stage, layer, weight, rows, which=(0, 1)):
        for c in which:
            gemm((stage, layer, c), weight, layer, 0, rows, 512 * c, 512)

    for l in range(DEPTH):
        for c in range(6):
            gemm(("in", l, c), "w_in", l, 0, D, 512 * c, 512)
        halves("v", l, "xa_wv", D, (0, 1) if l == 0 else (1,))
        halves("pool_up", l, "w_pool_up", SSM_W, (0,))
        gemm(("glu", l, 0), "ssm_w_glu", l, 0, SSM_W, 0, 512)
        halves("pool_up", l, "w_pool_up", SSM_W, (1,))
        halves("ssm_up", l, "w_ssm_up", SSM_W)
        halves("out", l, "w_out", D)
        halves("k", l, "xa_wk", D, (0, 1) if l == 0 else (1,))
        halves("q", l, "xa_wq", D)
        halves("o", l, "xa_wo", D)
        if l == 0:
            halves("v", 1, "xa_wv", D, (0,))
            for c, cols in enumerate(FF_CHUNKS):
                gemm(("ffn1", c), "ffn_w1", 0, 0, D, 512 * c, cols)
                gemm(("ffn3", c), "ffn_w3", 0, 0, D, 512 * c, cols)
                if c:
                    for h in range(2):
                        gemm(("ffn2", c - 1, h), "ffn_w2", 0, 512 * (c - 1), 512, 512 * h, 512, False)
            c = len(FF_CHUNKS) - 1
            for h in range(2):
                gemm(("ffn2", c, h), "ffn_w2", 0, 512 * c, FF_CHUNKS[c], 512 * h, 512, False)
            halves("k", 1, "xa_wk", D, (0,))
    return units, gemms


def plan_job():
    stages = [("w1", 0), ("w3", 0)]
    for c in range(1, FE_CHUNKS):
        stages += [("w1", c), ("w3", c), ("w2", c - 1)]
    return stages + [("w2", FE_CHUNKS - 1)]


def job_units(stages):
    units = []
    for kind, c in stages:
        if kind == "w2":
            units += [("moe_w2", 512 * c + 256 * k, 512 * h) for h in range(2) for k in range(2)]
        else:
            units += [("moe_" + kind, 256 * k, 512 * c) for k in range(4)]
    return units


def plan_rounds():
    rounds = [("out", 0, ("w1", 0), 4), ("out", 1, ("w3", 0), 4)]
    extra = {1: [("out", 2), ("out", 3)], 2: [("gates", 0), ("in", 0)], 3: [("in", 1)], 4: [("in", 2)], 5: [("in", 3)]}
    for c in range(1, FE_CHUNKS):
        rounds.append(("turn", c - 1, ("w1", c), 4))
        places = [("w3", c), ("w2", c - 1)] if c < 3 else [("w2", c - 1)]
        rounds += [(kind, i, place, 4) for (kind, i), place in zip(extra.get(c, []), places)]
    rounds.append(("turn", FE_CHUNKS - 1, ("w2", FE_CHUNKS - 2), 2))
    return rounds


class Order:

    def __init__(self, engine, sem):
        self.engine, self.sem, self.n, self.turns = engine, sem, 0, 0

    def add(self, instruction):
        instruction.then_inc(self.sem, 1)
        self.n += 1

    def settle(self):
        self.engine.wait_ge(self.sem, self.n + self.turns)

    def link(self, instruction):
        self.add(instruction)
        self.settle()


def build_trunk(nc, a, out):
    units, gemms = plan()
    stages = plan_job()
    moe_units = job_units(stages)
    N0 = len(units)
    NJ = len(moe_units)
    assert NJ % RAW == 0 and NJ % SPLIT == 0
    stage_at = {s: 4 * i for i, s in enumerate(stages)}
    rounds = plan_rounds()
    NR = len(rounds)
    FIRST = 4
    assert NR % 2 == 0
    round_of = {(kind, i): r for r, (kind, i, _, _) in enumerate(rounds)}
    rounds_at = {}
    for r, (_, _, stage, n) in enumerate(rounds):
        rounds_at.setdefault(stage_at[stage] + n, []).append(r)

    ctx = ExitStack()
    with ctx:
        def sb(name, shape, dt=F32, stack=ctx):
            return stack.enter_context(nc.sbuf_tensor(name, shape, dt))

        def sem(name):
            return ctx.enter_context(nc.semaphore(name))

        raw = sb("raw", [P, RAW, UNIT])
        w_hi = sb("w_hi", [P, SPLIT, UNIT], F32R)
        w_lo = sb("w_lo", [P, SPLIT, UNIT], F32R)
        x_tok = sb("x_tok", [P, TT, D])
        xs = sb("xs", [P, 16, T], F32R)
        v_sb = sb("v_sb", [P, 2, D])
        k_sb = sb("k_sb", [P, KD, T])
        ln_gb = sb("ln_gb", [P, 2, D])
        ident = sb("ident", [P, P])
        iota8 = sb("iota8", [P, 8])
        tiny = sb("tiny", [P, 64])
        small = sb("small", [P, 3, DEPTH, KS])
        pool_w = sb("pool_w", [P, KS, P])
        inv_count = sb("inv_count", [P, KS, PAD])
        router = sb("router", [P, KD * EXPERTS])
        router_s = sb("router_s", [P, 2, KD * EXPERTS], F32R)
        sp_in = sb("sp_in", [P, 3, 2 * STATE_TILES])
        sp = sb("sp", [P, 14, 2 * STATE_TILES])
        turn = sb("turn", [P, 2, STATE_TILES])
        turn_t = sb("turn_t", [P, 3, STATE_TILES])
        carry = sb("carry", [P, 4, 4])

        mixer = ExitStack()
        ms = sb("ms", [P, 16, T], F32R, mixer)
        table = sb("table", [P, 2, STATE_TILES, HALF], F32, mixer)
        prod = sb("prod", [P, 2048], F32, mixer)
        u_sb = sb("u_sb", [P, KS, T], F32, mixer)
        u_pool = sb("u_pool", [P, KS, PAD + T], F32, mixer)
        rot = sb("rot", [P, 2 * (PAD + T)], F32, mixer)
        b_t = sb("b_t", [P, 2, KS, P], F32, mixer)
        c_t = sb("c_t", [P, 3, STATE_TILES * 32], F32, mixer)
        first = ExitStack()
        wave = sb("wave", [P, 4096], F32, first)
        first.close()
        second = ExitStack()
        mx = sb("mx", [P, 16, T], F32R, second)
        second.close()
        skip = ExitStack()
        sb("wave_place", [P, 4096], F32, skip)
        g1 = ExitStack()
        gates = sb("gates", [P, 16, T], F32, g1)
        g1.close()
        g2 = ExitStack()
        hs = sb("hs", [P, 2, 2, 4, T], F32R, g2)
        g2.close()
        skip.close()
        mixer.close()
        moe = ExitStack()
        acc = sb("acc", [P, TT, D], F32, moe)
        xts = sb("xts", [P, 2, TT, D], F32R, moe)
        sel = sb("sel", [P, TT, P], F32R, moe)
        gsel = sb("gsel", [P, TT, P], F32, moe)
        gsel2 = sb("gsel2", [P, TT, P], F32, moe)
        gsel_t = sb("gsel_t", [P, TT, P], F32, moe)
        xe = sb("xe", [P, 2, 2, KD, P], F32R, moe)
        he = sb("he", [P, 2, 512], F32, moe)
        het = sb("het", [P, 2, 2, 4, P], F32R, moe)
        y_sb = sb("y_sb", [P, D], F32, moe)
        tri = sb("tri", [P, P], F32, moe)
        ones = sb("ones", [P, P], F32, moe)
        iota = sb("iota", [P, P], F32, moe)
        rt = sb("rt", [P, 12, TT, EXPERTS], F32, moe)
        rs = sb("rs", [P, 12, TT], F32, moe)
        dest = sb("dest", [P, 2, TT], F32, moe)
        gate_w = sb("gate_w", [P, 2, TT], F32, moe)
        ovf = sb("ovf", [P, 8, EXPERTS], F32, moe)
        jobs_f = sb("jobs_f", [P, 16], F32, moe)
        jobs = sb("jobs", [P, 16], I32, moe)
        moe.close()

        ps = ctx.enter_context(nc.psum_tensor("ps", [P, 8, 512], F32))

        raw_landed = [sem(f"raw_landed{i}") for i in range(RAW)]
        hi_ready, lo_ready, unit_used = sem("hi_ready"), sem("lo_ready"), sem("unit_used")
        pair_free = [sem("pair_free0"), sem("pair_free1")]
        x_in, mem_in, small_in, bc_in = sem("x_in"), sem("mem_in"), sem("small_in"), [sem("bc_in0"), sem("bc_in1")]
        xtok_in, poolw_in, ln_in, moe_in = sem("xtok_in"), [sem("poolw_in0"), sem("poolw_in1")], sem("ln_in"), sem("moe_in")
        xs_hi, xs_ready = sem("xs_hi"), sem("xs_ready")
        ms_hi, ms_ready = sem("ms_hi"), sem("ms_ready")
        dve_order, dve_tail, pool_order = sem("dve_order"), sem("dve_tail"), sem("pool_order")
        bb_ready, bt_done, bt_ready = sem("bb_ready"), sem("bt_done"), sem("bt_ready")
        table_ready = sem("table_ready")
        prep_ready = sem("prep_ready")
        bu_done, rotated, z_ready = sem("bu_done"), sem("rotated"), sem("z_ready")
        prod_ready, y_used = sem("prod_ready"), sem("y_used")
        y_linear, y_gelu, ys_ready = sem("y_linear"), sem("y_gelu"), sem("ys_ready")
        pooled, pool_mixed, pool_scaled, ps_ready = sem("pooled"), sem("pool_mixed"), sem("pool_scaled"), sem("ps_ready")
        pad_ready = sem("pad_ready")
        mx_ready = sem("mx_ready")
        ln_var, ln_rstd, ln_shift, ln_norm = sem("ln_var"), sem("ln_rstd"), sem("ln_shift"), sem("ln_norm")
        ln_done, xt_done, xt_hi, xt_ready = sem("ln_done"), sem("xt_done"), sem("xt_hi"), sem("xt_ready")
        score_done, score_max, prob_exp, prob_ready = sem("score_done"), sem("score_max"), sem("prob_exp"), sem("prob_ready")
        pt_done, pt_ready, pv_done, at_hi, at_ready = sem("pt_done"), sem("pt_ready"), sem("pv_done"), sem("at_hi"), sem("at_ready")
        silu_ready, hs_ready = sem("silu_ready"), sem("hs_ready")
        router_hi, router_ready, logits_done = sem("router_hi"), sem("router_ready"), sem("logits_done")
        expo_in, expo_done, picked, ranked, routed = sem("expo_in"), sem("expo_done"), sem("picked"), sem("ranked"), sem("routed")
        ones_ready = sem("ones_ready")
        xts_hi, xts_ready, c_ready = sem("xts_hi"), sem("xts_ready"), sem("c_ready")
        sel_ready, gsel_ready = sem("sel_ready"), sem("gsel_ready")
        misc_filled, misc_free = sem("misc_filled"), [sem("misc_free0"), sem("misc_free1")]
        het_hi = sem("het_hi")
        w1_free, w3_free, y_ready = sem("w1_free"), sem("w3_free"), sem("y_ready")
        out_ready, out_landed = sem("out_ready"), sem("out_landed")

        block = ctx.enter_context(nc.Block())

        def evacuated(engine, name):
            g = gemms[name]
            engine.wait_ge(pair_free[g["pair"]], g["use"] + 1)

        def gemm_ended(engine, name):
            engine.wait_ge(unit_used, gemms[name]["end"])

        def pair_of(name):
            return ps[:, 2 * gemms[name]["pair"]:2 * gemms[name]["pair"] + 2, :]

        def blocks(ap):
            return ap.rearrange("p b (h t) -> p (b h) t", t=T)

        def freed(instruction, name):
            instruction.then_inc(pair_free[gemms[name]["pair"]], 1)

        def view(buffer, slot, n, cols):
            return buffer[:, n % slot, :].rearrange("p (k c) -> p k c", c=cols)

        def hi_blocks(t, i, n):
            return t[:, i:i + n, :]

        wave_v = wave[:, :].rearrange("p (b j r t) -> p b j r t", b=2, j=4, r=2)
        prod_v = prod[:, :].rearrange("p (b q r t) -> p b q r t", b=2, q=2, r=2)
        y_v = prod[:, 0:1024].rearrange("p (f t) -> p f t", t=T)
        sil_v = wave[:, 0:2048].rearrange("p (b f t) -> p b f t", b=2, f=4)
        q_v = gates[:, 0:8, :]
        probs = gates[:, 8:12, :].rearrange("p (b q) t -> p b q t", b=2)
        probs_t = gates[:, 12:16, :].rearrange("p (b m) t -> p b m t", b=2)
        b_in = k_sb[:, 0:4, :].rearrange("p (r a) t -> p r (a t)", r=2)
        bb = prod[:, 0:1024].rearrange("p (r n) -> p r n", r=2)
        SSM_SLOTS = 24
        Y_LAG = 8

        def ssm_units(l):
            return gemms[("in", l, 2 if l == 0 else 1)]["first"]

        def discretise(engine, order, l, done):
            def wide(i):
                return sp[:, i, STATE_TILES * l:STATE_TILES * (l + 1)].unsqueeze(2).broadcast_to([P, STATE_TILES, 32])
            def per_tile(ap):
                return ap.rearrange("p (j c) -> p j c", c=32)
            b_re, b_im = per_tile(b_in[:, 0, :]), per_tile(b_in[:, 1, :])
            t1, t2 = per_tile(prod[:, 1024:1536]), per_tile(prod[:, 1536:2048])
            for k, (x, y, op) in enumerate(((b_re, b_im, ALU.subtract), (b_im, b_re, ALU.add))):
                order.add(engine.tensor_tensor(t1, x, wide(6), ALU.mult))
                order.link(engine.tensor_tensor(t2, y, wide(7), ALU.mult))
                last = engine.tensor_tensor(per_tile(bb[:, k, :]), t1, t2, op)
                if k == 0:
                    order.link(last)
            last.then_inc(done, 1)

        def phase_table(engine, order, l, done, between):
            js = slice(STATE_TILES * l, STATE_TILES * (l + 1))
            tt = engine.tensor_tensor
            cos, sin = table[:, 0], table[:, 1]
            order.add(engine.memset(cos[:, :, 0:1], 1.0))
            order.add(engine.memset(sin[:, :, 0:1], 0.0))
            order.add(engine.tensor_copy(turn[:, 0, :], sp[:, 4, js]))
            order.link(engine.tensor_copy(turn[:, 1, :], sp[:, 5, js]))
            for m in TABLE_STEPS:
                pc, ps_ = [turn[:, i, :].unsqueeze(2).broadcast_to([P, STATE_TILES, m]) for i in range(2)]
                t1, t2 = [prod[:, 1024 * i:1024 * i + STATE_TILES * m].rearrange("p (j t) -> p j t", t=m) for i in range(2)]
                c, s = cos[:, :, 0:m], sin[:, :, 0:m]
                order.add(tt(t1, c, pc, ALU.mult))
                order.link(tt(t2, s, ps_, ALU.mult))
                order.link(tt(cos[:, :, m:2 * m], t1, t2, ALU.subtract))
                order.add(tt(t1, s, pc, ALU.mult))
                order.link(tt(t2, c, ps_, ALU.mult))
                order.add(tt(sin[:, :, m:2 * m], t1, t2, ALU.add))
                order.add(tt(turn_t[:, 0, :], turn[:, 0, :], turn[:, 0, :], ALU.mult))
                order.add(tt(turn_t[:, 1, :], turn[:, 1, :], turn[:, 1, :], ALU.mult))
                order.link(tt(turn_t[:, 2, :], turn[:, 0, :], turn[:, 1, :], ALU.mult))
                order.add(tt(turn[:, 0, :], turn_t[:, 0, :], turn_t[:, 1, :], ALU.subtract))
                last = tt(turn[:, 1, :], turn_t[:, 2, :], turn_t[:, 2, :], ALU.add)
                if m < TABLE_STEPS[-1]:
                    order.link(last)
                between(m)
            last.then_inc(done, 1)

        @block.sync
        def _(sp_):
            sp_.dma_start(wave[:, 0:2048].rearrange("p (k t) -> p k t", t=T), a["x_t"]).then_inc(x_in, 16)
            for n, (name, stack, r0, k, c0, cols) in enumerate(units):
                if n >= RAW:
                    sp_.wait_ge(lo_ready, n - RAW + 1)
                src = a[name][stack, r0:r0 + k * P, c0:c0 + cols].rearrange("(k p) c -> p k c", p=P)
                sp_.dma_start(view(raw, RAW, n, cols), src).then_inc(raw_landed[n % RAW], 16)

            def load(i, expert, shift):
                name, r0, c0 = moe_units[i % NJ]
                n = N0 + i
                sp_.wait_ge(lo_ready, n - RAW + 1 + shift)
                rows = a[name].shape[1]
                src = a[name].rearrange("e r c -> (e r) c")[bass.ds(expert * rows + r0, 2 * P), c0:c0 + 512]
                src = src.rearrange("(k p) c -> p k c", p=P)
                sp_.dma_start(view(raw, RAW, n, 512), src).then_inc(raw_landed[n % RAW], 16)

            for i in range(LEAD):
                load(i, 0, 0)

            def job(j, expert, following):
                for i in range(LEAD, NJ):
                    load(i, expert, NJ * j)
                nxt = following()
                for i in range(NJ, NJ + LEAD):
                    load(i, nxt, NJ * j)

            with sp_.Fori(0, EXPERTS - 1) as j:
                job(j, j, lambda: j + 1)
            sp_.wait_ge(routed, 1)
            over = sp_.value_load(jobs[0:1, 0:1], min_val=0, max_val=OVER_MAX)
            job(EXPERTS - 1, EXPERTS - 1,
                lambda: sp_.value_load(jobs[0:1, 1:2], min_val=0, max_val=EXPERTS - 1))
            for o in range(OVER_MAX):
                with sp_.If(over > o):
                    expert = sp_.value_load(jobs[0:1, 1 + o:2 + o], min_val=0, max_val=EXPERTS - 1)
                    job(EXPERTS + o, expert,
                        lambda: sp_.value_load(jobs[0:1, 2 + o:3 + o], min_val=0, max_val=EXPERTS - 1))
                sp_.nop()
            for t in range(TT):
                sp_.wait_ge(out_ready, t + 1)
                sp_.dma_start(out[t * P:(t + 1) * P, :], acc[:, t, :]).then_inc(out_landed, 16)
            sp_.wait_ge(out_landed, 16 * TT)

        @block.scalar
        def _(act):
            split = [0]

            def split_hi(n):
                act.wait_ge(raw_landed[n % RAW], 16 * (n // RAW + 1))
                if n >= SPLIT:
                    act.wait_ge(unit_used, n - SPLIT + 1)
                nc.scalar.activation(w_hi[:, n % SPLIT, :], raw[:, n % RAW, :], ACT.Copy).then_inc(hi_ready, 1)

            def splits_to(n):
                while split[0] < min(n + LEAD, N0 + LEAD):
                    split_hi(split[0])
                    split[0] += 1

            act.dma_start(sp_in[:, :, :], a["ssm_par"]).then_inc(small_in, 16)
            act.dma_start(small[:, :, :, :], a["chan_par"]).then_inc(small_in, 16)
            act.dma_start(ident[:, :], a["c_ident"]).then_inc(small_in, 16)
            act.dma_start(iota8[:, :], a["c_iota8"]).then_inc(small_in, 16)
            act.dma_start(inv_count[:, :, :], a["c_inv"]).then_inc(small_in, 16)
            act.dma_start(router[:, :], a["router"]).then_inc(small_in, 16)
            act.dma_start(b_in, a["ssm_b"][0]).then_inc(bc_in[0], 16)
            act.dma_start(c_t[:, 0, :], a["ssm_c"][0, 0]).then_inc(bc_in[0], 16)
            act.dma_start(c_t[:, 2, :], a["ssm_c"][0, 1]).then_inc(bc_in[0], 16)
            act.dma_start(pool_w[:, :, :], a["pool_wt"][0]).then_inc(poolw_in[0], 16)
            act.dma_start(wave[:, 2048:4096].rearrange("p (k t) -> p k t", t=T), a["mem_t"]).then_inc(mem_in, 16)
            act.dma_start(x_tok[:, :, :], a["x"].rearrange("(t p) d -> p t d", p=P)).then_inc(xtok_in, 16)

            act.wait_ge(x_in, 16)
            nc.scalar.activation(xs[:, 0:8, :], wave[:, 0:2048].rearrange("p (k t) -> p k t", t=T),
                                 ACT.Copy).then_inc(xs_hi, 1)
            splits_to(1)
            act.wait_ge(mem_in, 16)
            nc.scalar.activation(ms[:, 0:8, :], wave[:, 2048:4096].rearrange("p (k t) -> p k t", t=T),
                                 ACT.Copy).then_inc(ms_hi, 1)
            act.wait_ge(small_in, 96)
            nc.scalar.activation(router_s[:, 0, :], router[:, :], ACT.Copy).then_inc(router_hi, 1)

            def epilogue(name, fn):
                splits_to(gemms[name]["end"])
                gemm_ended(act, name)
                freed(fn(pair_of(name)), name)

            def values(l, c):
                epilogue(("v", l, c), lambda p: nc.scalar.activation(v_sb[:, :, 512 * c:512 * c + 512], p, ACT.Copy))

            def keys(l, c):
                epilogue(("k", l, c), lambda p: nc.scalar.activation(k_sb[:, 4 * c:4 * c + 4, :], blocks(p), ACT.Copy))

            def hi_of_x(i):
                for t in range(TT):
                    act.wait_ge(xt_done, TT * i + t + 1)
                    src = ps[:, 4 + 2 * t:6 + 2 * t, :].rearrange("p b (k t) -> p (b k) t", t=P)
                    nc.scalar.activation(xs[:, 0:8, t * P:(t + 1) * P], src, ACT.Copy).then_inc(xt_hi, 1)

            def normalise(i, tensor):
                for t in range(TT):
                    act.wait_ge(ln_shift, TT * i + t + 1)
                    nc.scalar.activation(tensor[:, t, :], tensor[:, t, :], ACT.Identity,
                                         scale=tiny[:, 4 * t + 2:4 * t + 3], bias=tiny[:, 4 * t + 3:4 * t + 4]
                                         ).then_inc(ln_norm, 1)

            for l in range(DEPTH):
                epilogue(("in", l, 0), lambda p: nc.scalar.activation(u_sb[:, :, :], blocks(p), ACT.Copy))
                act.wait_ge(bt_done, l + 1)
                nc.scalar.activation(b_t[:, :, :, :], ps[:, 4:6, :].rearrange("p r (j s) -> p r j s", s=P),
                                     ACT.Copy).then_inc(bt_ready, 1)
                if l == 0:
                    act.wait_ge(pad_ready, 1)
                epilogue(("in", l, 1), lambda p: nc.scalar.activation(u_pool[:, :, PAD:PAD + T], blocks(p), ACT.Copy))
                for c in range(2, 6):
                    epilogue(("in", l, c), lambda p, c=c: nc.scalar.activation(
                        gates[:, 4 * (c - 2):4 * (c - 2) + 4, :], blocks(p), ACT.Sigmoid))
                for c in ((0, 1) if l == 0 else (1,)):
                    values(l, c)
                act.wait_ge(pool_mixed, l + 1)
                for g in range(KS):
                    last = nc.scalar.activation(u_pool[:, g, PAD:PAD + T], ps[:, 4 + g // 2, T * (g % 2):T * (g % 2) + T],
                                                ACT.Copy, scale=small[:, 2, l, g:g + 1])
                last.then_inc(pool_scaled, 1)
                act.wait_ge(y_linear, l + 1)
                nc.scalar.activation(y_v, y_v, ACT.Gelu_apprx_tanh).then_inc(y_gelu, 1)
                splits_to(gemms[("glu", l, 0)]["end"])
                gemm_ended(act, ("glu", l, 0))
                for f in range(KS):
                    last = nc.scalar.activation(u_sb[:, f, :], blocks(pair_of(("glu", l, 0)))[:, f, :], ACT.Sigmoid,
                                                bias=small[:, 1, l, f:f + 1])
                freed(last, ("glu", l, 0))
                splits_to(gemms[("out", l, 1)]["end"])
                normalise(3 * l, x_tok)
                for c in ((0, 1) if l == 0 else (1,)):
                    keys(l, c)
                hi_of_x(3 * l)
                for c in range(2):
                    epilogue(("q", l, c), lambda p, c=c: nc.scalar.activation(
                        q_v[:, 4 * c:4 * c + 4, :], blocks(p), ACT.Copy, scale=1.0 / 16.0))
                for h in range(HEADS + 1):
                    if h < HEADS:
                        n = HEADS * l + h
                        act.wait_ge(score_max, n + 1)
                        for t in range(TT):
                            last = nc.scalar.activation(probs[:, h % 2, t, :], ps[:, 4 + h % 2, T * t:T * t + T], ACT.Exp,
                                                        bias=tiny[:, 16 + 4 * (h % 2) + t:17 + 4 * (h % 2) + t],
                                                        accum_out=tiny[:, 24 + 4 * (h % 2) + t:25 + 4 * (h % 2) + t])
                        last.then_inc(prob_exp, 1)
                    if h >= 1:
                        n = HEADS * l + h - 1
                        act.wait_ge(pt_done, n + 1)
                        nc.scalar.activation(probs_t[:, (h - 1) % 2, :, :],
                                             ps[:, 6 + (h - 1) % 2, :].rearrange("p (m t) -> p m t", t=T),
                                             ACT.Copy).then_inc(pt_ready, 1)
                        act.wait_ge(pv_done, n + 1)
                        nc.scalar.activation(xs[:, 2 * (h - 1):2 * h, :], ps[:, h - 1, :].rearrange("p (b t) -> p b t", t=T),
                                             ACT.Copy).then_inc(at_hi, 1)
                splits_to(gemms[("o", l, 1)]["end"])
                normalise(3 * l + 1, x_tok)
                if l == 0:
                    values(1, 0)
                hi_of_x(3 * l + 1)
                if l == 0:
                    for c, cols in enumerate(FF_CHUNKS):
                        name, f = ("ffn1", c), cols // P
                        splits_to(gemms[name]["end"])
                        gemm_ended(act, name)
                        if c >= 2:
                            act.wait_ge(hs_ready, c - 1)
                        freed(nc.scalar.activation(sil_v[:, c % 2, 0:f, :], blocks(pair_of(name))[:, 0:f, :], ACT.Silu), name)
                    splits_to(gemms[("ffn2", len(FF_CHUNKS) - 1, 1)]["end"])
                    normalise(2, x_tok)
                    act.wait_ge(bb_ready, 2)
                    keys(1, 0)
                    hi_of_x(2)

            act.wait_ge(ln_done, 2 * 5)
            nc.scalar.activation(xts[:, 0, :, :], x_tok[:, :, :], ACT.Copy).then_inc(xts_hi, 1)
            nc.scalar.activation(acc[:, :, :], x_tok[:, :, :], ACT.Copy, scale=ALPHA).then_inc(w1_free, 1)
            act.wait_ge(expo_in, 1)
            nc.scalar.activation(rs[:, 3, :], rs[:, 2, :], ACT.Exp).then_inc(expo_done, 1)

            def tokens_out(i, r, buffer, turn_):
                act.wait_ge(misc_filled, r + 1 + turn_)
                nc.scalar.activation(xe[:, buffer, i // 2, 4 * (i % 2):4 * (i % 2) + 4, :],
                                     ps[:, 6 + r % 2, :].rearrange("p (k s) -> p k s", s=P),
                                     ACT.Copy).then_inc(misc_free[r % 2], 1)

            for i in range(4):
                tokens_out(i, i, 0, 0)

            def job(j, h):
                filled = NR * j + (NR * h + FIRST)

                def through(n0, n1):
                    for i in range(n0 + LEAD, n1 + LEAD):
                        m = N0 + i
                        act.wait_ge(raw_landed[m % RAW], NJ // RAW * 16 * j + (16 * (m // RAW + 1) + NJ // RAW * 16 * h))
                        act.wait_ge(unit_used, NJ * j + (m - SPLIT + 1 + NJ * h))
                        nc.scalar.activation(w_hi[:, m % SPLIT, :], raw[:, m % RAW, :], ACT.Copy).then_inc(hi_ready, 1)

                for i, (kind, c) in enumerate(stages):
                    for n in range(4 * i, 4 * i + 4):
                        through(n, n + 1)
                        if kind == "w1" and n == 4 * i + 3:
                            act.wait_ge(unit_used, NJ * j + (N0 + n + 1 + NJ * h))
                            nc.scalar.activation(he[:, c % 2, :], ps[:, 2 * (c % 2), :], ACT.Silu).then_inc(w1_free, 1)
                        for r in rounds_at.get(n + 1, ()):
                            what, q = rounds[r][:2]
                            bank = ps[:, 6 + r % 2, :]
                            if what == "turn":
                                act.wait_ge(misc_filled, filled + (r + 1))
                                nc.scalar.activation(het[:, q % 2, 0, :, :], bank.rearrange("p (k s) -> p k s", s=P),
                                                     ACT.Copy).then_inc(het_hi, 1)
                            elif what == "gates":
                                act.wait_ge(misc_filled, filled + (r + 1))
                                nc.scalar.activation(gsel_t[:, :, :], bank[:, 0:TT * P].rearrange("p (t s) -> p t s", s=P),
                                                     ACT.Copy).then_inc(misc_free[r % 2], 1)
                            elif what == "in":
                                tokens_out(q, r, 1 - h, filled)
                act.wait_ge(unit_used, NJ * j + (N0 + NJ + NJ * h))
                nc.scalar.activation(y_sb[:, :], ps[:, 4:6, :].rearrange("p b c -> p (b c)"), ACT.Copy).then_inc(y_ready, 1)

            with act.Fori(0, EXPERTS, 2) as j:
                job(j, 0)
                job(j, 1)
            over = act.value_load(jobs[0:1, 0:1], min_val=0, max_val=OVER_MAX)
            for o in range(OVER_MAX):
                with act.If(over > o):
                    job(EXPERTS + o - o % 2, o % 2)
                act.nop()
            normalise(5, acc)

        @block.vector
        def _(dve):
            order = Order(dve, dve_order)
            add, settle, link = order.add, order.settle, order.link
            split = [0]
            tt = nc.vector.tensor_tensor
            ts = nc.vector.tensor_scalar
            stt = nc.vector.scalar_tensor_tensor

            def split_lo(n, shift):
                dve.wait_ge(hi_ready, n + 1 + shift)
                tt(w_lo[:, n % SPLIT, :], raw[:, n % RAW, :], w_hi[:, n % SPLIT, :].bitcast(F32),
                   ALU.subtract).then_inc(lo_ready, 1)

            def splits_to(n):
                while split[0] < min(n + LEAD, N0 + LEAD):
                    split_lo(split[0], 0)
                    split[0] += 1

            def hi_lo(hi, lo, src, last_sem):
                link(nc.vector.tensor_copy(hi, src))
                tt(lo, src, hi.bitcast(F32), ALU.subtract).then_inc(last_sem, 1)

            dve.wait_ge(xs_hi, 1)
            tt(xs[:, 8:16, :], wave[:, 0:2048].rearrange("p (k t) -> p k t", t=T), xs[:, 0:8, :].bitcast(F32),
               ALU.subtract).then_inc(xs_ready, 1)
            splits_to(1)
            nc.vector.memset(u_pool[:, :, 0:PAD], 0.0).then_inc(pad_ready, 1)

            (DT, RE, TH, MAG, COS, SIN, FRE, FIM, A, B, C, E, F, G) = [sp[:, i, :] for i in range(14)]
            are, aim, ldt = sp_in[:, 0, :], sp_in[:, 1, :], sp_in[:, 2, :]
            n1, n2 = F.bitcast(I32), G.bitcast(I32)
            dve.wait_ge(small_in, 96)

            def exp_exact(dst, x):
                link(ts(A, x, -170.0, 100.0, ALU.max, ALU.min))
                link(ts(B, A, 1.4426950408889634, MAGIC, ALU.mult, ALU.add))
                link(ts(B, B, MAGIC, None, ALU.subtract))
                link(stt(C, B, -0.693359375, A, ALU.mult, ALU.add))
                link(stt(C, B, 2.12194440e-4, C, ALU.mult, ALU.add))
                link(ts(E, C, 1.9875691500e-4, None, ALU.mult))
                for k in (1.3981999507e-3, 8.3334519073e-3, 4.1665795894e-2, 1.6666665459e-1, 5.0000001201e-1, 1.0):
                    link(stt(E, E, k, C, ALU.add, ALU.mult))
                link(ts(E, E, 1.0, None, ALU.add))
                link(ts(A, B, 0.5, MAGIC, ALU.mult, ALU.add))
                link(ts(A, A, MAGIC, None, ALU.subtract))
                link(tt(B, B, A, ALU.subtract))
                link(ts(n1, A, 127.0, 8388608.0, ALU.add, ALU.mult))
                link(ts(n2, B, 127.0, 8388608.0, ALU.add, ALU.mult))
                link(tt(E, E, F, ALU.mult))
                link(tt(dst, E, G, ALU.mult))

            exp_exact(DT, ldt)
            link(tt(RE, are, DT, ALU.mult))
            exp_exact(MAG, RE)
            link(tt(TH, aim, DT, ALU.mult))
            link(ts(A, TH, 0.15915494309189535, MAGIC, ALU.mult, ALU.add))
            link(ts(A, A, MAGIC, None, ALU.subtract))
            link(stt(TH, A, -6.28125, TH, ALU.mult, ALU.add))
            link(stt(TH, A, -1.9350051879882812e-3, TH, ALU.mult, ALU.add))
            link(stt(TH, A, -3.0199159819591886e-7, TH, ALU.mult, ALU.add))
            link(ts(A, TH, 0.25, None, ALU.mult))
            link(tt(B, A, A, ALU.mult))
            link(ts(C, B, -1.9515295891e-4, 8.3321608736e-3, ALU.mult, ALU.add))
            link(tt(C, C, B, ALU.mult))
            link(stt(C, C, -1.6666654611e-1, B, ALU.add, ALU.mult))
            link(stt(SIN, C, 1.0, A, ALU.add, ALU.mult))
            link(ts(C, B, 2.443315711809948e-5, -1.388731625493765e-3, ALU.mult, ALU.add))
            link(tt(C, C, B, ALU.mult))
            link(stt(C, C, 4.166664568298827e-2, B, ALU.add, ALU.mult))
            link(stt(C, C, -0.5, B, ALU.add, ALU.mult))
            link(ts(COS, C, 1.0, None, ALU.add))
            for _ in range(2):
                link(tt(A, SIN, SIN, ALU.mult))
                link(stt(SIN, SIN, 2.0, COS, ALU.mult, ALU.mult))
                link(ts(COS, A, -2.0, 1.0, ALU.mult, ALU.add))
            link(tt(A, MAG, COS, ALU.mult))
            link(tt(B, MAG, SIN, ALU.mult))
            link(ts(A, A, 1.0, None, ALU.subtract))
            link(tt(C, are, are, ALU.mult))
            link(tt(E, aim, aim, ALU.mult))
            link(tt(C, C, E, ALU.add))
            link(nc.vector.reciprocal(C, C))
            link(tt(E, A, are, ALU.mult))
            link(tt(F, B, aim, ALU.mult))
            link(tt(E, E, F, ALU.add))
            link(tt(FRE, E, C, ALU.mult))
            link(tt(E, B, are, ALU.mult))
            link(tt(F, A, aim, ALU.mult))
            link(tt(E, E, F, ALU.subtract))
            tt(FIM, E, C, ALU.mult).then_inc(prep_ready, 1)
            dve.wait_ge(prep_ready, 1)
            splits_to(3)

            dve.wait_ge(bc_in[0], 48)
            discretise(nc.vector, order, 0, bb_ready)
            splits_to(5)
            dve.wait_ge(ms_hi, 1)
            tt(ms[:, 8:16, :], wave[:, 2048:4096].rearrange("p (k t) -> p k t", t=T), ms[:, 0:8, :].bitcast(F32),
               ALU.subtract).then_inc(ms_ready, 1)
            dve.wait_ge(router_hi, 1)
            tt(router_s[:, 1, :], router[:, :], router_s[:, 0, :].bitcast(F32), ALU.subtract).then_inc(router_ready, 1)
            dve.wait_ge(bt_done, 1)
            phase_table(nc.vector, order, 0, table_ready, lambda m: splits_to(min(5 + m, 10)))

            def window_means(l, g):
                bufs = [rot[:, 0:PAD + T], rot[:, PAD + T:2 * (PAD + T)]]
                add(nc.vector.memset(bufs[0][:, 0:PAD], 0.0))
                link(nc.vector.memset(bufs[1][:, 0:PAD], 0.0))
                s = u_pool[:, g, :]
                for level in range(g + 1):
                    d = bufs[level % 2]
                    link(tt(d[:, PAD:], s[:, PAD:], s[:, PAD - 2 ** level:PAD + T - 2 ** level], ALU.add))
                    s = d
                w = 2 ** (g + 1)
                u = u_pool[:, g, :]
                link(tt(s[:, PAD:2 * PAD], s[:, PAD:2 * PAD], inv_count[:, g, :], ALU.mult))
                add(stt(u[:, 2 * PAD:], s[:, 2 * PAD:], 1.0 / w, u[:, 2 * PAD:], ALU.mult, ALU.subtract))
                tt(u[:, PAD:2 * PAD], s[:, PAD:2 * PAD], u[:, PAD:2 * PAD], ALU.subtract).then_inc(pooled, 1)
                dve.wait_ge(pooled, KS * l + g + 1)

            def rotate(l, j):
                n = STATE_TILES * l + j
                q, b = j // 4, (j // 4) % 2
                dve.wait_ge(bu_done, n + 1)
                if q >= 2 and j % 4 == 0:
                    dve.wait_ge(prod_ready, STATE_TILES * l + 4 * (q - 1))
                elif l and j % 4 == 0:
                    dve.wait_ge(prod_ready, STATE_TILES * l)
                w = wave_v[:, b, j % 4]
                bu = ps[:, 4 + n % 2, :]
                cos = table[:, 0, j:j + 1, :].broadcast_to([P, 4, HALF])
                sin = table[:, 1, j:j + 1, :].broadcast_to([P, 2, HALF])
                add(tt(w.rearrange("p r (s t) -> p (r s) t", t=HALF), bu.rearrange("p (s t) -> p s t", t=HALF), cos, ALU.mult))
                r2 = rot[:, 0:512].rearrange("p (r s t) -> p r s t", r=2, t=HALF)
                add(tt(r2[:, 0], bu[:, T:2 * T].rearrange("p (s t) -> p s t", t=HALF), sin, ALU.mult))
                tt(r2[:, 1], bu[:, 0:T].rearrange("p (s t) -> p s t", t=HALF), sin, ALU.mult).then_inc(rotated, 1)
                dve.wait_ge(rotated, n + 1)
                add(tt(w[:, 0, :], w[:, 0, :], rot[:, 0:T], ALU.add))
                link(tt(w[:, 1, :], w[:, 1, :], rot[:, T:2 * T], ALU.subtract))

            def scan(l, q):
                w = wave_v[:, q % 2]
                for half in range(2):
                    for j in range(4):
                        mag = MAG[:, STATE_TILES * l + 4 * q + j:STATE_TILES * l + 4 * q + j + 1].broadcast_to([P, HALF])
                        for r in range(2):
                            z = w[:, j, r, HALF * half:HALF * half + HALF]
                            init = carry[:, 2 + r, j:j + 1] if half else 0.0
                            last = nc.vector.tensor_tensor_scan(z, mag, z, init, ALU.mult, ALU.add)
                            if half and (j, r) == (3, 1):
                                last.then_inc(z_ready, 1)
                            else:
                                add(last)
                    if not half:
                        settle()
                        zr, zi = w[:, :, 0, HALF - 1:HALF].rearrange("p j t -> p (j t)"), w[:, :, 1, HALF - 1:HALF].rearrange("p j t -> p (j t)")
                        c, s = turn[:, 0, 4 * q:4 * q + 4], turn[:, 1, 4 * q:4 * q + 4]
                        add(tt(carry[:, 0, :], zr, c, ALU.mult))
                        add(tt(carry[:, 1, :], zi, s, ALU.mult))
                        link(tt(carry[:, 3, :], zr, s, ALU.mult))
                        link(tt(carry[:, 2, :], carry[:, 0, :], carry[:, 1, :], ALU.subtract))
                        link(tt(carry[:, 0, :], zi, c, ALU.mult))
                        link(tt(carry[:, 3, :], carry[:, 3, :], carry[:, 0, :], ALU.add))

            def layer_norm(i, sources, tensor, last_of=None, scaled=True):
                if scaled:
                    for half, (wait, bank, release) in enumerate(sources):
                        wait()
                        for t in range(TT):
                            xt = tensor[:, t, 512 * half:512 * half + 512]
                            last = stt(xt, xt, ALPHA, bank(t), ALU.mult, ALU.add)
                            if t == TT - 1:
                                release(last)
                            else:
                                add(last)
                    settle()
                    last_of()
                st = tiny[:, 32:56].rearrange("p (t h s) -> p t h s", t=TT, h=2)
                for t in range(TT):
                    for half in range(2):
                        add(nc.vector.bn_stats(st[:, t, half, :], tensor[:, t, 512 * half:512 * half + 512]))
                    settle()
                    link(nc.vector.bn_aggr(tiny[:, 4 * t:4 * t + 2], st[:, t, :, :].rearrange("p h s -> p (h s)")))
                    ts(tiny[:, 8 + t:9 + t], tiny[:, 4 * t + 1:4 * t + 2], LN_EPS, None, ALU.add).then_inc(ln_var, 1)
                for t in range(TT):
                    dve.wait_ge(ln_rstd, TT * i + t + 1)
                    stt(tiny[:, 4 * t + 3:4 * t + 4], tiny[:, 4 * t:4 * t + 1], -1.0, tiny[:, 4 * t + 2:4 * t + 3],
                        ALU.mult, ALU.mult).then_inc(ln_shift, 1)

                def rest(t):
                    dve.wait_ge(ln_norm, TT * i + t + 1)
                    if t == 0:
                        dve.wait_ge(ln_in, 32 * (i + 1))
                    link(tt(tensor[:, t, :], tensor[:, t, :], ln_gb[:, 0, :], ALU.mult))
                    tt(tensor[:, t, :], tensor[:, t, :], ln_gb[:, 1, :], ALU.add).then_inc(ln_done if i < 5 else out_ready, 1)
                return rest

            def paired_source(name, half_tokens):
                g = gemms[name]
                return (lambda: gemm_ended(dve, name), lambda t: ps[:, 2 * g["pair"] + t, :], lambda ins: freed(ins, name))

            def lo_of_x(i):
                for t in range(TT):
                    dve.wait_ge(xt_hi, TT * i + t + 1)
                    src = ps[:, 4 + 2 * t:6 + 2 * t, :].rearrange("p b (k t) -> p (b k) t", t=P)
                    tt(xs[:, 8:16, t * P:(t + 1) * P], src, xs[:, 0:8, t * P:(t + 1) * P].bitcast(F32),
                       ALU.subtract).then_inc(xt_ready, 1)

            for l in range(DEPTH):
                dve.wait_ge(table_ready, l + 1)
                dve.wait_ge(bc_in[l], 48)
                base = ssm_units(l)
                add(ts(c_t[:, 1, :], c_t[:, 0, :], -1.0, None, ALU.mult))
                ts(c_t[:, 2, :], c_t[:, 2, :], -1.0, None, ALU.mult).then_inc(c_ready, 1)
                for i in range(STATE_TILES):
                    splits_to(base + 1 + i)
                    rotate(l, i)
                    if i % 4 == 3:
                        scan(l, i // 4)
                    if i in (4, 6, 8, 10):
                        if i == 4:
                            evacuated(dve, ("in", l, 1))
                        window_means(l, (i - 4) // 2)
                splits_to(base + SSM_SLOTS)
                splits_to(gemms[("v", l, 1)]["end"])
                dve.wait_ge(y_used, STATE_TILES * (l + 1))
                for f in range(KS):
                    last = stt(y_v[:, f, :], u_sb[:, f, :], small[:, 0, l, f:f + 1], ps[:, 6 + f // 2, T * (f % 2):T * (f % 2) + T],
                               ALU.mult, ALU.add)
                    if f < KS - 1:
                        add(last)
                last.then_inc(y_linear, 1)
                dve.wait_ge(pool_scaled, l + 1)
                gemm_ended(dve, ("in", l, 5))
                hi_lo(xs[:, 8:12, :], xs[:, 12:16, :], u_pool[:, :, PAD:PAD + T], ps_ready)
                dve.wait_ge(y_gelu, l + 1)
                hi_lo(xs[:, 0:4, :], xs[:, 4:8, :], y_v, ys_ready)

                def gate_pool(c):
                    name = ("pool_up", l, c)
                    splits_to(gemms[name]["end"])
                    gemm_ended(dve, name)
                    g = gates[:, 8 + 4 * c:12 + 4 * c, :]
                    freed(tt(g, blocks(pair_of(name)), g, ALU.mult), name)

                gate_pool(0)
                splits_to(gemms[("glu", l, 0)]["end"])
                evacuated(dve, ("glu", l, 0))
                link(tt(y_v, y_v, u_sb[:, :, :], ALU.mult))
                hi_lo(xs[:, 0:4, :], xs[:, 4:8, :], y_v, ys_ready)
                gate_pool(1)
                for c in range(2):
                    name = ("ssm_up", l, c)
                    splits_to(gemms[name]["end"])
                    gemm_ended(dve, name)
                    g = gates[:, 4 * c:4 * c + 4, :]
                    freed(tt(g, blocks(pair_of(name)), g, ALU.mult), name)
                    evacuated(dve, name)
                    evacuated(dve, ("pool_up", l, c))
                    link(tt(g, g, gates[:, 8 + 4 * c:12 + 4 * c, :], ALU.add))
                    hi_lo(mx[:, 4 * c:4 * c + 4, :], mx[:, 8 + 4 * c:12 + 4 * c, :], g, mx_ready)
                splits_to(gemms[("out", l, 1)]["end"])
                if l == 0:
                    dve.wait_ge(xtok_in, 16)
                rest = layer_norm(3 * l, [paired_source(("out", l, c), c) for c in range(2)], x_tok,
                                  lambda: evacuated(dve, ("out", l, 1)))
                k_first, k_last = gemms[("k", l, 0 if l == 0 else 1)]["first"], gemms[("k", l, 1)]["end"]
                splits_to(k_first + 2)
                rest(0)
                splits_to(k_first + 4)
                rest(1)
                splits_to(k_last)
                lo_of_x(3 * l)
                splits_to(gemms[("q", l, 1)]["end"])
                for h in range(HEADS + 2):
                    if h < HEADS:
                        n, o = HEADS * l + h, 4 * (h % 2)
                        dve.wait_ge(score_done, n + 1)
                        link(nc.vector.tensor_reduce(tiny[:, 56:58], ps[:, 4 + h % 2, :].rearrange("p (t m) -> p t m", t=TT), AX_X, ALU.max))
                        ts(tiny[:, 16 + o:18 + o], tiny[:, 56:58], -1.0, None, ALU.mult).then_inc(score_max, 1)
                        dve.wait_ge(score_max, n + 1)
                    if 1 <= h <= HEADS:
                        g = h - 1
                        n, o = HEADS * l + g, 4 * (g % 2)
                        dve.wait_ge(prob_exp, n + 1)
                        link(nc.vector.reciprocal(tiny[:, 58:60], tiny[:, 24 + o:26 + o]))
                        for t in range(TT):
                            last = ts(probs[:, g % 2, t, :], probs[:, g % 2, t, :], tiny[:, 58 + t:59 + t], None, ALU.mult)
                            if t < TT - 1:
                                add(last)
                        last.then_inc(prob_ready, 1)
                        dve.wait_ge(prob_ready, n + 1)
                    if h >= 2:
                        g = h - 2
                        dve.wait_ge(at_hi, HEADS * l + g + 1)
                        tt(xs[:, 8 + 2 * g:10 + 2 * g, :], ps[:, g, :].rearrange("p (b t) -> p b t", t=T),
                           xs[:, 2 * g:2 * g + 2, :].bitcast(F32), ALU.subtract).then_inc(at_ready, 1)
                splits_to(gemms[("o", l, 1)]["end"])
                rest = layer_norm(3 * l + 1, [paired_source(("o", l, c), c) for c in range(2)], x_tok,
                                  lambda: evacuated(dve, ("o", l, 1)))
                f0 = gemms[("o", l, 1)]["end"]
                if l == 0:
                    splits_to(f0 + 2)
                rest(0)
                if l == 0:
                    splits_to(f0 + 4)
                rest(1)
                lo_of_x(3 * l + 1)
                if l == 0:
                    for c, cols in enumerate(FF_CHUNKS):
                        name, f = ("ffn3", c), cols // P
                        splits_to(gemms[name]["end"])
                        gemm_ended(dve, name)
                        evacuated(dve, ("ffn1", c))
                        if c >= 2:
                            gemm_ended(dve, ("ffn2", c - 2, 1))
                        h_ = sil_v[:, c % 2, 0:f, :]
                        freed(tt(h_, blocks(pair_of(name))[:, 0:f, :], h_, ALU.mult), name)
                        evacuated(dve, name)
                        hi_lo(hs[:, c % 2, 0, 0:f, :], hs[:, c % 2, 1, 0:f, :], h_, hs_ready)
                    last = ("ffn2", len(FF_CHUNKS) - 1, 1)
                    splits_to(gemms[last]["end"])
                    rest = layer_norm(2, [(lambda h=h: gemm_ended(dve, ("ffn2", len(FF_CHUNKS) - 1, h)),
                                           lambda t, h=h: ps[:, 4 + 2 * t + h, :], add) for h in range(2)], x_tok, lambda: None)
                    f0 = gemms[last]["end"]
                    splits_to(f0 + 2)
                    rest(0)
                    splits_to(f0 + 4)
                    rest(1)
                    lo_of_x(2)

            lg, eq, oh1, oh2, lg2, both, rank, dexp, hi_r, tmp = [rt[:, i] for i in range(10)]
            m1, m2, diff, ex, idx, i1, i2 = [rs[:, i] for i in range(7)]

            def per_token(x):
                return x.unsqueeze(2).broadcast_to([P, TT, EXPERTS])

            def per_expert(x):
                return x.unsqueeze(1).broadcast_to([P, TT, EXPERTS])

            dve.wait_ge(ln_done, 2 * 5)
            dve.wait_ge(logits_done, 1)
            link(nc.vector.tensor_copy(lg, ps[:, 4, 0:TT * EXPERTS].rearrange("p (t e) -> p t e", t=TT)))

            def best(scores, m, i_, oh):
                link(nc.vector.tensor_reduce(m, scores, AX_X, ALU.max))
                link(tt(eq, scores, per_token(m), ALU.is_equal))
                link(ts(tmp, per_expert(iota8[:, :]), -8.0, None, ALU.add))
                link(tt(eq, eq, tmp, ALU.mult))
                link(nc.vector.tensor_reduce(i_, eq, AX_X, ALU.min))
                link(ts(i_, i_, 8.0, None, ALU.add))
                link(tt(oh, per_expert(iota8[:, :]), per_token(i_), ALU.is_equal))

            best(lg, m1, i1, oh1)
            link(stt(lg2, oh1, -1e30, lg, ALU.mult, ALU.add))
            best(lg2, m2, i2, oh2)
            tt(diff, m2, m1, ALU.subtract).then_inc(expo_in, 1)
            tt(both, oh1, oh2, ALU.add).then_inc(picked, 1)
            dve.wait_ge(expo_done, 1)
            link(ts(idx, ex, 1.0, None, ALU.add))
            link(nc.vector.reciprocal(gate_w[:, 0, :], idx))
            link(tt(gate_w[:, 1, :], ex, gate_w[:, 0, :], ALU.mult))
            dve.wait_ge(xts_hi, 1)
            tt(xts[:, 1, :, :], x_tok[:, :, :], xts[:, 0, :, :].bitcast(F32), ALU.subtract).then_inc(xts_ready, 1)
            dve.wait_ge(ranked, 1)
            link(nc.vector.tensor_copy(rank, ps[:, 5, 0:TT * EXPERTS].rearrange("p (t e) -> p t e", t=TT)))
            cnt, over_, incl, pos, base_o, sel_o, one8 = [ovf[:, i, :] for i in range(7)]
            link(nc.vector.memset(one8, 1.0))
            link(nc.vector.tensor_copy(cnt, ps[:, 5, TT * EXPERTS:(TT + 1) * EXPERTS]))
            link(ts(over_, cnt, 128.0, None, ALU.is_gt))
            link(nc.vector.tensor_tensor_scan(incl, one8, over_, 0.0, ALU.mult, ALU.add))
            link(tt(pos, incl, over_, ALU.subtract))
            link(ts(base_o, iota8[:, :], -128.0, 128.0 * (EXPERTS - 1), ALU.mult, ALU.add))
            link(stt(base_o, pos, 128.0, base_o, ALU.mult, ALU.add))
            link(ts(hi_r, rank, 128.0, None, ALU.is_ge))
            link(tt(hi_r, hi_r, per_expert(base_o), ALU.mult))
            link(tt(dexp, rank, hi_r, ALU.add))
            link(stt(dexp, per_expert(iota8[:, :]), 128.0, dexp, ALU.mult, ALU.add))
            for k, oh in enumerate((oh1, oh2)):
                link(tt(tmp, oh, dexp, ALU.mult))
                link(nc.vector.tensor_reduce(dest[:, k, :], tmp, AX_X, ALU.add))
            link(nc.vector.memset(jobs_f[:, :], 0.0))
            link(nc.vector.tensor_copy(jobs_f[:, 0:1], incl[:, EXPERTS - 1:EXPERTS]))
            for o in range(OVER_MAX):
                link(stt(sel_o, pos, float(o), over_, ALU.is_equal, ALU.mult))
                link(tt(sel_o, sel_o, iota8[:, :], ALU.mult))
                link(nc.vector.tensor_reduce(jobs_f[:, 1 + o:2 + o], sel_o, AX_X, ALU.add))
            nc.vector.tensor_copy(jobs[:, :], jobs_f[:, :]).then_inc(routed, 1)

            dve.wait_ge(moe_in, 32)

            def select(t):
                link(ts(gsel2[:, t, :], iota[:, :], dest[:, 0, t:t + 1], None, ALU.is_equal))
                stt(sel[:, t, :], iota[:, :], dest[:, 1, t:t + 1], gsel2[:, t, :], ALU.is_equal, ALU.add).then_inc(sel_ready, 1)

            def select_gated(t):
                add(ts(gsel[:, t, :], iota[:, :], dest[:, 0, t:t + 1], gate_w[:, 0, t:t + 1], ALU.is_equal, ALU.mult))
                link(ts(gsel2[:, t, :], iota[:, :], dest[:, 1, t:t + 1], gate_w[:, 1, t:t + 1], ALU.is_equal, ALU.mult))
                tt(gsel[:, t, :], gsel[:, t, :], gsel2[:, t, :], ALU.add).then_inc(gsel_ready, 1)

            nc.vector.memset(gsel_t[:, :, :], 0.0).then_inc(w3_free, 1)
            nc.vector.memset(y_sb[:, :], 0.0).then_inc(y_ready, 1)
            for t in range(TT):
                select(t)

            def add_out(q, r, turn_):
                dve.wait_ge(misc_filled, FIRST + r + 1 + turn_)
                piece = acc[:, q // 2, 512 * (q % 2):512 * (q % 2) + 512]
                tt(piece, ps[:, 6 + r % 2, :], piece, ALU.add).then_inc(misc_free[r % 2], 1)

            def job(j, steps):
                order.turns = steps * j

                for i, (kind, c) in enumerate(stages):
                    for n in range(4 * i, 4 * i + 4):
                        split_lo(N0 + n + LEAD, NJ * j)
                        if kind == "w3" and n == 4 * i + 3:
                            dve.wait_ge(unit_used, N0 + n + 1 + NJ * j)
                            dve.wait_ge(w1_free, 2 + c + FE_CHUNKS * j)
                            tt(he[:, c % 2, :], ps[:, 2 * (c % 2) + 1, :], he[:, c % 2, :], ALU.mult).then_inc(w3_free, 1)
                        for r in rounds_at.get(n + 1, ()):
                            what, q = rounds[r][:2]
                            if what == "out":
                                add_out(q, r, NR * j)
                            elif what == "turn":
                                dve.wait_ge(het_hi, q + 1 + FE_CHUNKS * j)
                                tt(het[:, q % 2, 1, :, :], ps[:, 6 + r % 2, :].rearrange("p (k s) -> p k s", s=P),
                                   het[:, q % 2, 0, :, :].bitcast(F32), ALU.subtract).then_inc(misc_free[r % 2], 1)
                        if kind == "w1" and c in (1, 2) and n == 4 * i + 1:
                            if c == 1:
                                dve.wait_ge(misc_filled, FIRST + NR * j)
                                dve.wait_ge(sel_ready, TT + TT * j)
                            select_gated(c - 1)
                        if (kind, c) in (("w3", 2), ("w2", 1)) and n == 4 * i + 1:
                            if kind == "w3":
                                dve.wait_ge(gsel_ready, TT + TT * j)
                                link(ts(dest[:, :, :], dest[:, :, :], -128.0, None, ALU.add))
                            select(0 if kind == "w3" else 1)
            JOB_STEPS = 7
            with dve.Fori(0, EXPERTS) as j:
                before = order.n
                job(j, JOB_STEPS)
                assert order.n - before == JOB_STEPS, order.n - before
            order.n = before
            over = dve.value_load(jobs[0:1, 0:1], min_val=0, max_val=OVER_MAX)
            for o in range(OVER_MAX):
                with dve.If(over > o):
                    order.n = before
                    job(EXPERTS + o, JOB_STEPS)
                dve.nop()
            order.sem, order.n, order.turns = dve_tail, 0, 0
            for r in range(4):
                add_out(r, r, over * NR + EXPERTS * NR)
            for b in range(2):
                dve.wait_ge(misc_free[b], over * (NR // 2) + (FIRST // 2 + NR // 2 * EXPERTS + 2))
            rest = layer_norm(5, None, acc, None, scaled=False)
            rest(0)
            rest(1)

        @block.gpsimd
        def _(pool):
            order = Order(pool, pool_order)

            def load_ln(i):
                l, which = divmod(i, 3)
                g, b = (("ln_mix_g", "ln_mix_b"), ("ln_xa_g", "ln_xa_b"), ("ln_ffn_g", "ln_ffn_b"))[which]
                if i:
                    pool.wait_ge(ln_done, TT * i)
                pool.dma_start(ln_gb[:, 0, :], a[g][l:l + 1, :].broadcast_to([P, D])).then_inc(ln_in, 16)
                pool.dma_start(ln_gb[:, 1, :], a[b][l:l + 1, :].broadcast_to([P, D])).then_inc(ln_in, 16)

            def deviation(i):
                for t in range(TT):
                    pool.wait_ge(ln_var, TT * i + t + 1)
                    nc.gpsimd.tensor_tensor(tiny[:, 4 * t + 2:4 * t + 3], tiny[:, 8 + t:9 + t], tiny[:, 60:61],
                                            ALU.pow).then_inc(ln_rstd, 1)

            order.link(nc.gpsimd.memset(tiny[:, 60:61], -0.5))
            load_ln(0)
            for l in range(DEPTH):
                for j in range(STATE_TILES):
                    n = STATE_TILES * l + j
                    if j % 4 == 0:
                        pool.wait_ge(z_ready, 4 * l + j // 4 + 1)
                    if n >= 2:
                        pool.wait_ge(y_used, n - 1)
                    z = wave_v[:, (j // 4) % 2, j % 4].rearrange("p r (s t) -> p (r s) t", t=HALF)
                    for k in range(2):
                        tab = table[:, k, j:j + 1, :].broadcast_to([P, 4, HALF])
                        dst = prod_v[:, j % 2, k].rearrange("p r (s t) -> p (r s) t", t=HALF)
                        last = nc.gpsimd.tensor_tensor(dst, z, tab, ALU.mult)
                        if k == 0:
                            order.add(last)
                    last.then_inc(prod_ready, 1)
                deviation(3 * l)
                load_ln(3 * l + 1)
                deviation(3 * l + 1)
                load_ln(3 * l + 2)
                if l == 0:
                    pool.wait_ge(y_used, STATE_TILES)
                    pool.dma_start(c_t[:, 0, :], a["ssm_c"][1, 0]).then_inc(bc_in[1], 16)
                    pool.dma_start(c_t[:, 2, :], a["ssm_c"][1, 1]).then_inc(bc_in[1], 16)
                    pool.dma_start(b_in, a["ssm_b"][1]).then_inc(bc_in[1], 16)
                    pool.dma_start(pool_w[:, :, :], a["pool_wt"][1]).then_inc(poolw_in[1], 16)
                    pool.wait_ge(bc_in[1], 48)
                    pool.wait_ge(prep_ready, 1)
                    phase_table(nc.gpsimd, order, 1, table_ready, lambda m: None)
                    discretise(nc.gpsimd, order, 1, bb_ready)
                    deviation(2)
                    load_ln(3)
            pool.wait_ge(ln_done, 2 * 5)
            pool.dma_start(tri[:, :], a["c_tri"]).then_inc(moe_in, 16)
            pool.dma_start(iota[:, :], a["c_iota"]).then_inc(moe_in, 16)
            nc.gpsimd.memset(ones[:, :], 1.0).then_inc(ones_ready, 1)
            deviation(5)

        @block.tensor
        def _(pe):
            mm = nc.tensor.matmul

            def take(n, cols, shift=0):
                pe.wait_ge(hi_ready, n + 1 + shift)
                return view(w_hi, SPLIT, n, cols), view(w_lo, SPLIT, n, cols)

            def claim(name):
                g = gemms[name]
                if g["use"]:
                    pe.wait_ge(pair_free[g["pair"]], g["use"])

            def by_feature(name, hi, lo, hook=None):
                g = gemms[name]
                claim(name)
                out_ = blocks(pair_of(name))
                fs, k = g["cols"] // P, 0
                for n in range(g["first"], g["end"]):
                    wh, wl = take(n, g["cols"])
                    for i in range(g["k"]):
                        for f in range(fs):
                            w = wh[:, i, f * P:(f + 1) * P]
                            mm(out_[:, f, :], w, hi(k + i), start=(k + i == 0 and f % 2 == 0), stop=False, skip_group_check=True)
                            mm(out_[:, f, :], w, lo(k + i), start=False, stop=False, skip_group_check=True)
                    pe.wait_ge(lo_ready, n + 1)
                    for i in range(g["k"]):
                        for f in range(fs):
                            last = mm(out_[:, f, :], wl[:, i, f * P:(f + 1) * P], hi(k + i), start=False,
                                      stop=(n == g["end"] - 1 and i == g["k"] - 1), skip_group_check=True)
                    last.then_inc(unit_used, 1)
                    k += g["k"]
                    if hook:
                        hook(n)

            def by_token(name, hi, lo, banks=None, first_=True, last_=True, hook=None):
                g = gemms[name]
                if banks is None:
                    claim(name)
                    banks = [2 * g["pair"] + t for t in range(TT)]
                k = 0
                for n in range(g["first"], g["end"]):
                    wh, wl = take(n, g["cols"])
                    for i in range(g["k"]):
                        for t in range(TT):
                            mm(ps[:, banks[t], :], hi(k + i, t), wh[:, i, :], start=(first_ and k + i == 0), stop=False, skip_group_check=True)
                            mm(ps[:, banks[t], :], lo(k + i, t), wh[:, i, :], start=False, stop=False, skip_group_check=True)
                    pe.wait_ge(lo_ready, n + 1)
                    for i in range(g["k"]):
                        for t in range(TT):
                            last = mm(ps[:, banks[t], :], hi(k + i, t), wl[:, i, :], start=False,
                                      stop=(last_ and n == g["end"] - 1 and i == g["k"] - 1), skip_group_check=True)
                    last.then_inc(unit_used, 1)
                    k += g["k"]
                    if hook:
                        hook(n)

            def pair(t, lo_at):
                return (lambda k, q=None: t[:, k, :] if q is None else t[:, k, q * P:(q + 1) * P],
                        lambda k, q=None: t[:, lo_at + k, :] if q is None else t[:, lo_at + k, q * P:(q + 1) * P])

            x_hl, mem_hl, mx_hl = pair(xs, 8), pair(ms, 8), pair(mx, 8)
            y_hl = pair(xs, 4)
            p_hl = (lambda k: xs[:, 8 + k, :], lambda k: xs[:, 12 + k, :])

            def turn_b(l):
                pe.wait_ge(bb_ready, l + 1)
                for r in range(2):
                    for q in range(KS):
                        last = nc.tensor.transpose(ps[:, 4 + r, q * P:(q + 1) * P], bb[:, r, q * P:(q + 1) * P], ident[:, :])
                last.then_inc(bt_done, 1)

            def ssm_step(l, i):
                if i == 0:
                    pe.wait_ge(bt_ready, l + 1)
                    evacuated(pe, ("in", l, 0))
                if i < STATE_TILES:
                    n, q, row = STATE_TILES * l + i, i // 4, 32 * (i % 4)
                    if i >= 2:
                        pe.wait_ge(rotated, n - 1)
                    for r in range(2):
                        last = mm(ps[:, 4 + n % 2, r * T:(r + 1) * T], b_t[row:row + 32, r, q, :], u_sb[row:row + 32, q, :],
                                  start=True, stop=True, tile_position=(row, 0))
                    last.then_inc(bu_done, 1)
                if Y_LAG <= i < STATE_TILES + Y_LAG:
                    j = i - Y_LAG
                    n, q, row = STATE_TILES * l + j, j // 4, 32 * (j % 4)
                    if j == 0:
                        pe.wait_ge(c_ready, l + 1)
                    pe.wait_ge(prod_ready, n + 1)
                    p = prod_v[:, j % 2]
                    parts = ((0, p[:, 0, 0, :]), (1, p[:, 1, 1, :]), (2, p[:, 1, 0, :]), (2, p[:, 0, 1, :]))
                    for s, (c, mov) in enumerate(parts):
                        last = mm(ps[row:row + 32, 6 + q // 2, T * (q % 2):T * (q % 2) + T], c_t[:, c, 32 * j:32 * j + 32], mov,
                                  start=(s == 0), stop=(s == 3), tile_position=(0, row), skip_group_check=True)
                    last.then_inc(y_used, 1)

            def turn_x(i):
                for t in range(TT):
                    pe.wait_ge(ln_done, TT * i + t + 1)
                    for k in range(KD):
                        last = nc.tensor.transpose(ps[:, 4 + 2 * t + k // 4, P * (k % 4):P * (k % 4) + P],
                                                   x_tok[:, t, k * P:(k + 1) * P], ident[:, :])
                    last.then_inc(xt_done, 1)

            pe.wait_ge(xs_ready, 1)
            for l in range(DEPTH):
                if l:
                    pe.wait_ge(xt_ready, TT * 3)
                by_feature(("in", l, 0), *x_hl)
                if l == 0:
                    pe.wait_ge(small_in, 96)
                turn_b(l)
                base = ssm_units(l)
                step = lambda n: ssm_step(l, n - base) if n >= base else None
                for c in range(1, 6):
                    by_feature(("in", l, c), *x_hl, hook=step)
                pe.wait_ge(ms_ready, 1)
                for c in ((0, 1) if l == 0 else (1,)):
                    by_token(("v", l, c), *mem_hl, hook=step)
                assert gemms[("v", l, 1)]["end"] - base == SSM_SLOTS
                pe.wait_ge(pooled, KS * (l + 1))
                pe.wait_ge(poolw_in[l], 16)
                pe.wait_ge(rotated, STATE_TILES * (l + 1))
                for g in range(KS):
                    last = mm(ps[:, 4 + g // 2, T * (g % 2):T * (g % 2) + T], pool_w[:, g, :], u_pool[:, g, PAD:PAD + T],
                              start=True, stop=True)
                last.then_inc(pool_mixed, 1)
                pe.wait_ge(ps_ready, l + 1)
                by_feature(("pool_up", l, 0), *p_hl)
                pe.wait_ge(ys_ready, 2 * l + 1)
                by_feature(("glu", l, 0), *y_hl)
                by_feature(("pool_up", l, 1), *p_hl)
                pe.wait_ge(ys_ready, 2 * l + 2)
                by_feature(("ssm_up", l, 0), *y_hl)
                by_feature(("ssm_up", l, 1), *y_hl)
                pe.wait_ge(mx_ready, 2 * l + 2)
                by_token(("out", l, 0), *mx_hl)
                by_token(("out", l, 1), *mx_hl)
                for c in ((0, 1) if l == 0 else (1,)):
                    by_feature(("k", l, c), *mem_hl)
                turn_x(3 * l)
                pe.wait_ge(xt_ready, TT * (3 * l + 1))
                by_feature(("q", l, 0), *x_hl)
                by_feature(("q", l, 1), *x_hl)
                for c in range(2):
                    evacuated(pe, ("q", l, c))
                    evacuated(pe, ("k", l, c))
                for h in range(HEADS + 1):
                    if h < HEADS:
                        n = HEADS * l + h
                        if h >= 2:
                            pe.wait_ge(prob_exp, n - 1)
                        for t in range(TT):
                            for e in range(2):
                                last = mm(ps[:, 4 + h % 2, T * t:T * t + T], q_v[:, 2 * h + e, t * P:(t + 1) * P],
                                          k_sb[:, 2 * h + e, :], start=(e == 0), stop=(e == 1), skip_group_check=True)
                        last.then_inc(score_done, 1)
                    if h >= 1:
                        g = h - 1
                        n = HEADS * l + g
                        pe.wait_ge(prob_ready, n + 1)
                        if g >= 2:
                            pe.wait_ge(pt_ready, n - 1)
                        for t in range(TT):
                            for m in range(2):
                                last = nc.tensor.transpose(ps[:, 6 + g % 2, T * m + P * t:T * m + P * t + P],
                                                           probs[:, g % 2, t, m * P:(m + 1) * P], ident[:, :])
                        last.then_inc(pt_done, 1)
                        pe.wait_ge(pt_ready, n + 1)
                        for e in range(2):
                            for m in range(2):
                                last = mm(ps[:, g, T * e:T * e + T], v_sb[:, m, T * g + P * e:T * g + P * e + P],
                                          probs_t[:, g % 2, m, :], start=(m == 0), stop=(m == 1), skip_group_check=True)
                        last.then_inc(pv_done, 1)
                pe.wait_ge(at_ready, HEADS * (l + 1))
                by_token(("o", l, 0), *x_hl)
                by_token(("o", l, 1), *x_hl)
                if l == 0:
                    by_token(("v", 1, 0), *mem_hl)
                turn_x(3 * l + 1)
                pe.wait_ge(xt_ready, TT * (3 * l + 2))
                if l == 0:
                    def down(c):
                        pe.wait_ge(hs_ready, c + 1)
                        hi = lambda k, t: hs[:, c % 2, 0, k, t * P:(t + 1) * P]
                        lo = lambda k, t: hs[:, c % 2, 1, k, t * P:(t + 1) * P]
                        for h in range(2):
                            by_token(("ffn2", c, h), hi, lo, banks=[4 + h, 6 + h], first_=(c == 0), last_=(c == len(FF_CHUNKS) - 1))

                    for c in range(len(FF_CHUNKS)):
                        by_feature(("ffn1", c), *x_hl)
                        by_feature(("ffn3", c), *x_hl)
                        if c:
                            down(c - 1)
                    down(len(FF_CHUNKS) - 1)
                    by_feature(("k", 1, 0), *mem_hl)
                    turn_x(2)

            pe.wait_ge(router_ready, 1)
            rhs = [router_s[:, i, :].rearrange("p (k e) -> p k e", e=EXPERTS) for i in range(2)]
            for t in range(TT):
                for k in range(KD):
                    for s, (x_part, r_part) in enumerate(((0, 0), (8, 0), (0, 1))):
                        last = mm(ps[:, 4, t * EXPERTS:(t + 1) * EXPERTS], xs[:, x_part + k, t * P:(t + 1) * P], rhs[r_part][:, k, :],
                                  start=(t == 0 and k == 0 and s == 0), stop=(k == KD - 1 and s == 2), skip_group_check=True)
            last.then_inc(logits_done, 1)
            pe.wait_ge(picked, 1)
            pe.wait_ge(moe_in, 32)
            pe.wait_ge(ones_ready, 1)
            both = rt[:, 5]
            products = ((0, tri, 0), (1, tri, 1), (1, ones, 0), (2, ones, 0), (2, ones, 1))
            for i, (o, m, t) in enumerate(products):
                last = mm(ps[:, 5, o * EXPERTS:(o + 1) * EXPERTS], m[:, :], both[:, t, :], start=(i == 0), stop=True,
                          skip_group_check=True)
            last.then_inc(ranked, 1)

            def gather(i, r):
                for k in range(4):
                    for t in range(TT):
                        d0 = P * (4 * (i % 2) + k)
                        last = mm(ps[:, 6 + r % 2, k * P:(k + 1) * P], xts[:, i // 2, t, d0:d0 + P], sel[:, t, :],
                                  start=(t == 0), stop=(t == TT - 1), skip_group_check=True)
                last.then_inc(misc_filled, 1)

            def scatter(r, q):
                return mm(ps[:, 6 + r % 2, :], gsel_t[:, q // 2, :], y_sb[:, 512 * (q % 2):512 * (q % 2) + 512], start=True, stop=True)

            pe.wait_ge(xts_ready, 1)
            pe.wait_ge(sel_ready, TT)
            for i in range(FIRST):
                if i >= 2:
                    pe.wait_ge(misc_free[i % 2], 1)
                gather(i, i)

            def job(j, h):
                base = NJ * j + NJ * h
                chunks = FE_CHUNKS * j + FE_CHUNKS * h

                def misc(n):
                    for r in rounds_at.get(n, ()):
                        what, q = rounds[r][:2]
                        pe.wait_ge(misc_free[r % 2], NR // 2 * j + (NR // 2 * h + FIRST // 2 + r // 2))
                        if what == "out":
                            if q == 0:
                                pe.wait_ge(y_ready, j + (1 + h))
                            scatter(r, q).then_inc(misc_filled, 1)
                        elif what == "in":
                            if q == 0:
                                pe.wait_ge(sel_ready, TT * j + (TT * h + 2 * TT))
                            gather(q, r)
                        elif what == "gates":
                            pe.wait_ge(gsel_ready, TT * j + (TT * h + TT))
                            for t in range(TT):
                                last = nc.tensor.transpose(ps[:, 6 + r % 2, t * P:(t + 1) * P], gsel[:, t, :], ident[:, :])
                            last.then_inc(misc_filled, 1)
                        else:
                            pe.wait_ge(w3_free, chunks + (1 + q + 1))
                            for k in range(4):
                                last = nc.tensor.transpose(ps[:, 6 + r % 2, k * P:(k + 1) * P], he[:, q % 2, k * P:(k + 1) * P], ident[:, :])
                            last.then_inc(misc_filled, 1)

                def products(n, bank, x_hi, x_lo, k0, first_, last_):
                    wh, wl = take(N0 + n, 512, base)
                    for i in range(2):
                        mm(ps[:, bank, :], x_hi(k0 + i), wh[:, i, :], start=(first_ and i == 0), stop=False, skip_group_check=True)
                        mm(ps[:, bank, :], x_lo(k0 + i), wh[:, i, :], start=False, stop=False, skip_group_check=True)
                    pe.wait_ge(lo_ready, base + (N0 + n + 1))
                    for i in range(2):
                        last = mm(ps[:, bank, :], x_hi(k0 + i), wl[:, i, :], start=False, stop=(last_ and i == 1), skip_group_check=True)
                    last.then_inc(unit_used, 1)
                    misc(n + 1)

                for b in range(2):
                    pe.wait_ge(misc_free[b], NR // 2 * j + (NR // 2 * h + FIRST // 2))
                for i, (kind, c) in enumerate(stages):
                    if kind == "w2":
                        r = round_of[("turn", c)]
                        pe.wait_ge(misc_free[r % 2], NR // 2 * j + (NR // 2 * h + FIRST // 2 + r // 2 + 1))
                        for n in range(4):
                            k0 = 2 * (n % 2)
                            products(4 * i + n, 4 + n // 2, lambda k: het[:, c % 2, 0, k, :], lambda k: het[:, c % 2, 1, k, :],
                                     k0, c == 0 and k0 == 0, c == FE_CHUNKS - 1 and k0 == 2)
                    else:
                        pe.wait_ge(w1_free if kind == "w1" else w3_free, chunks + (1 if c < 2 else c))
                        for n in range(4):
                            products(4 * i + n, 2 * (c % 2) + (kind == "w3"), lambda k: xe[:, h, 0, k, :], lambda k: xe[:, h, 1, k, :],
                                     2 * n, n == 0, n == 3)

            with pe.Fori(0, EXPERTS, 2) as j:
                job(j, 0)
                job(j, 1)
            over = pe.value_load(jobs[0:1, 0:1], min_val=0, max_val=OVER_MAX)
            for o in range(OVER_MAX):
                with pe.If(over > o):
                    job(EXPERTS + o - o % 2, o % 2)
                pe.nop()
            pe.wait_ge(y_ready, over + (1 + EXPERTS))
            for r in range(4):
                pe.wait_ge(misc_free[r % 2], over * (NR // 2) + (FIRST // 2 + r // 2 + NR // 2 * EXPERTS))
                scatter(r, r).then_inc(misc_filled, 1)


def build(nc, arrays):
    a = {k: nc.dram_tensor(f"in_{k}", list(v.shape), F32, kind="ExternalInput").ap() for k, v in arrays.items()}
    out = nc.dram_tensor("out_0", [T, D], F32, kind="ExternalOutput").ap()
    build_trunk(nc, a, out)


_AS_THEY_ARE = ["ln_mix_g", "ln_mix_b", "w_in", "ssm_w_glu", "w_ssm_up", "w_pool_up", "w_out", "ln_xa_g", "ln_xa_b",
                "xa_wq", "xa_wk", "xa_wv", "xa_wo", "ln_ffn_g", "ln_ffn_b", "ffn_w1", "ffn_w3", "ffn_w2"]


def lay_out(inputs):
    import numpy as np
    i = {k: np.asarray(v) for k, v in inputs.items()}
    L = DEPTH
    a = {k: i[k] for k in _AS_THEY_ARE}
    for k in ("moe_w1", "moe_w3", "moe_w2"):
        a[k] = i[k][0]
    a["x"] = i["x"][0]
    for k, n in (("x_t", "x"), ("mem_t", "mem")):
        a[k] = i[n][0].T.reshape(KD, P, T).transpose(1, 0, 2)

    def states(v):
        return v.reshape(L, STATE_TILES, P).transpose(2, 0, 1).reshape(P, L * STATE_TILES)
    log_dt = np.broadcast_to(i["ssm_log_dt"][:, :, None], i["ssm_a_re"].shape)
    a["ssm_par"] = np.stack([states(i["ssm_a_re"]), states(i["ssm_a_im"]), states(log_dt)], axis=1)

    def block_diagonal(v):
        v = v.reshape(L, STATE_TILES, 2, P // 2, GROUP_W)
        z = np.zeros((L, 2, P // 2, STATE_TILES, 2, GROUP_W), v.dtype)
        for h in range(2):
            z[:, h, :, :, h, :] = v[:, :, h].transpose(0, 2, 1, 3)
        return z.reshape(L, P, STATE_TILES * 2 * GROUP_W)
    a["ssm_b"] = np.stack([block_diagonal(i["ssm_b_re"]), block_diagonal(i["ssm_b_im"])], axis=2)
    a["ssm_c"] = np.stack([block_diagonal(i["ssm_c_re"].transpose(0, 1, 3, 2)),
                           block_diagonal(i["ssm_c_im"].transpose(0, 1, 3, 2))], axis=1)
    a["chan_par"] = np.stack([i[n].reshape(L, KS, P).transpose(2, 0, 1) for n in ("ssm_d", "ssm_b_glu", "pool_scale")], axis=1)
    a["pool_wt"] = i["pool_w"].transpose(0, 2, 1, 3)
    a["router"] = i["moe_router"][0].reshape(KD, P, EXPERTS).transpose(1, 0, 2).reshape(P, KD * EXPERTS)
    f = np.float32
    a["c_ident"] = np.eye(P, dtype=f)
    a["c_tri"] = np.triu(np.ones((P, P), f), 1)
    a["c_iota"] = np.broadcast_to(np.arange(P, dtype=f), (P, P))
    a["c_iota8"] = np.broadcast_to(np.arange(EXPERTS, dtype=f), (P, EXPERTS))
    steps = np.arange(1, PAD + 1, dtype=f)
    a["c_inv"] = np.broadcast_to(np.stack([1.0 / np.minimum(steps, f(2 ** (g + 1))) for g in range(KS)]), (P, KS, PAD))
    return {k: np.ascontiguousarray(v) for k, v in a.items()}


def kernel(**inputs):
    import concourse.bacc as bacc
    from concourse.bass_utils import run_bass_kernel_spmd

    arrays = lay_out(inputs)
    nc = bacc.Bacc("TRN2", target_bir_lowering=False, num_devices=1)
    build(nc, arrays)
    r = run_bass_kernel_spmd(nc, [{f"in_{k}": v for k, v in arrays.items()}], core_ids=[0])
    return r.results[0]["out_0"].reshape(1, T, D)
```

```python
from contextlib import ExitStack

import concourse.bass as bass
from concourse import mybir

F32 = mybir.dt.float32
F32R = mybir.dt.float32r
I32 = mybir.dt.int32
ALU = mybir.AluOpType
ACT = mybir.ActivationFunctionType
AX_X = mybir.AxisListType.X

P = 128
D = 1024
T = 256
DEPTH = 2
KD = D // P
TT = T // P
SSM_W = 512
KS = SSM_W // P
GROUP_W = 16
STATE_TILES = 16
HALF = 128
TABLE_DVE = 8
PAD = 16
HEADS = 4
D_FF = 2816
FF_CHUNKS = [512] * 5 + [256]
EXPERTS = 8
D_FE = 3584
FE_CHUNKS = D_FE // 512
OVER_MAX = 3
ALPHA = (2 * DEPTH) ** 0.25
LN_EPS = 1e-5

RAW = 7
SPLIT = 4
LEAD = SPLIT - 1
UNIT = 1024
MAGIC = 12582912.0
TABLE_STEPS = [1, 2, 4, 8, 16, 32, 64]


def plan():
    units, gemms, uses = [], {}, [0, 0]

    def pair_only(name):
        gemms[name] = {"first": len(units), "end": len(units)}
        take_pair(gemms[name])

    def take_pair(g):
        g["pair"] = (uses[0] + uses[1]) % 2
        g["use"] = uses[g["pair"]]
        uses[g["pair"]] += 1

    def gemm(name, weight, stack, row0, rows, col0, cols, paired=True):
        per = UNIT // cols * P
        g = {"first": len(units), "cols": cols, "k": UNIT // cols}
        for r in range(row0, row0 + rows, per):
            units.append((weight, stack, r, UNIT // cols, col0, cols))
        g["end"] = len(units)
        if paired:
            take_pair(g)
        gemms[name] = g

    def halves(stage, layer, weight, rows, which=(0, 1)):
        for c in which:
            gemm((stage, layer, c), weight, layer, 0, rows, 512 * c, 512)

    for l in range(DEPTH):
        for c in range(6):
            gemm(("in", l, c), "w_in", l, 0, D, 512 * c, 512)
        if l == 0:
            halves("v", l, "xa_wv", D, (0,))
        pair_only(("pool_mix", l))
        halves("v", l, "xa_wv", D, (1,))
        if l == 0:
            halves("k", l, "xa_wk", D, (0,))
        halves("pool_up", l, "w_pool_up", SSM_W, (0,))
        if l == 0:
            halves("pool_up", l, "w_pool_up", SSM_W, (1,))
        gemm(("glu", l, 0), "ssm_w_glu", l, 0, SSM_W, 0, 512)
        if l:
            halves("pool_up", l, "w_pool_up", SSM_W, (1,))
        halves("ssm_up", l, "w_ssm_up", SSM_W)
        halves("out", l, "w_out", D)
        halves("k", l, "xa_wk", D, (1,))
        halves("q", l, "xa_wq", D)
        first = len(units)
        for h in range(HEADS):
            for c in range(2):
                units.append(("xa_wo", l, D // HEADS * h, 2, 512 * c, 512))
        for c in range(2):
            gemms[("o", l, c)] = {"first": first, "end": len(units) - 1 + c}
            take_pair(gemms[("o", l, c)])
        if l == 0:
            halves("v", 1, "xa_wv", D, (0,))
            for c, cols in enumerate(FF_CHUNKS):
                gemm(("ffn1", c), "ffn_w1", 0, 0, D, 512 * c, cols)
                gemm(("ffn3", c), "ffn_w3", 0, 0, D, 512 * c, cols)
                if c:
                    for h in range(2):
                        gemm(("ffn2", c - 1, h), "ffn_w2", 0, 512 * (c - 1), 512, 512 * h, 512, False)
            c = len(FF_CHUNKS) - 1
            for h in range(2):
                gemm(("ffn2", c, h), "ffn_w2", 0, 512 * c, FF_CHUNKS[c], 512 * h, 512, False)
            halves("k", 1, "xa_wk", D, (0,))
    return units, gemms


def plan_job():
    stages = [("w1", 0), ("w3", 0)]
    for c in range(1, FE_CHUNKS):
        stages += [("w1", c), ("w3", c), ("w2", c - 1)]
    return stages + [("w2", FE_CHUNKS - 1)]


def job_units(stages):
    units = []
    for kind, c in stages:
        if kind == "w2":
            units += [("moe_w2", 512 * c + 256 * k, 512 * h) for h in range(2) for k in range(2)]
        else:
            units += [("moe_" + kind, 256 * k, 512 * c) for k in range(4)]
    return units


def plan_rounds():
    rounds = [("out", 0, ("w1", 0), 4), ("out", 1, ("w3", 0), 4)]
    extra = {1: [("out", 2), ("out", 3)], 2: [("gates", 0), ("in", 0)], 3: [("in", 1)], 4: [("in", 2)], 5: [("in", 3)]}
    for c in range(1, FE_CHUNKS):
        rounds.append(("turn", c - 1, ("w1", c), 4))
        places = [("w3", c), ("w2", c - 1)] if c < 3 else [("w2", c - 1)]
        rounds += [(kind, i, place, 4) for (kind, i), place in zip(extra.get(c, []), places)]
    rounds.append(("turn", FE_CHUNKS - 1, ("w2", FE_CHUNKS - 2), 2))
    return rounds


class Order:

    def __init__(self, engine, sem):
        self.engine, self.sem, self.n, self.turns = engine, sem, 0, 0

    def add(self, instruction):
        instruction.then_inc(self.sem, 1)
        self.n += 1

    def settle(self):
        self.engine.wait_ge(self.sem, self.n + self.turns)

    def link(self, instruction):
        self.add(instruction)
        self.settle()


def build_trunk(nc, a, out):
    units, gemms = plan()
    stages = plan_job()
    moe_units = job_units(stages)
    N0 = len(units)
    NJ = len(moe_units)
    assert NJ % RAW == 0 and NJ % SPLIT == 0
    stage_at = {s: 4 * i for i, s in enumerate(stages)}
    rounds = plan_rounds()
    NR = len(rounds)
    FIRST = 4
    assert NR % 2 == 0
    round_of = {(kind, i): r for r, (kind, i, _, _) in enumerate(rounds)}
    rounds_at = {}
    for r, (_, _, stage, n) in enumerate(rounds):
        rounds_at.setdefault(stage_at[stage] + n, []).append(r)

    ctx = ExitStack()
    with ctx:
        def sb(name, shape, dt=F32, stack=ctx):
            return stack.enter_context(nc.sbuf_tensor(name, shape, dt))

        def sem(name):
            return ctx.enter_context(nc.semaphore(name))

        raw = sb("raw", [P, RAW, UNIT])
        w_hi = sb("w_hi", [P, SPLIT, UNIT], F32R)
        w_lo = sb("w_lo", [P, SPLIT, UNIT], F32R)
        x_tok = sb("x_tok", [P, TT, D])
        xs = sb("xs", [P, 16, T], F32R)
        v_sb = sb("v_sb", [P, 2, D])
        k_sb = sb("k_sb", [P, KD, T])
        ln_gb = sb("ln_gb", [P, 2, D])
        ident = sb("ident", [P, P])
        iota8 = sb("iota8", [P, 8])
        tiny = sb("tiny", [P, 64])
        small = sb("small", [P, 3, DEPTH, KS])
        pool_w = sb("pool_w", [P, KS, P])
        inv_count = sb("inv_count", [P, KS, PAD])
        router = sb("router", [P, KD * EXPERTS])
        router_s = sb("router_s", [P, 2, KD * EXPERTS], F32R)
        sp_in = sb("sp_in", [P, 3, 2 * STATE_TILES])
        sp = sb("sp", [P, 14, 2 * STATE_TILES])
        turn = sb("turn", [P, 2, STATE_TILES])
        turn_t = sb("turn_t", [P, 3, STATE_TILES])
        carry = sb("carry", [P, 4, 4])

        mixer = ExitStack()
        ms = sb("ms", [P, 16, T], F32R, mixer)
        table = sb("table", [P, 2, STATE_TILES, HALF], F32, mixer)
        prod = sb("prod", [P, 2048], F32, mixer)
        u_sb = sb("u_sb", [P, KS, T], F32, mixer)
        u_pool = sb("u_pool", [P, KS, PAD + T], F32, mixer)
        rot = sb("rot", [P, 2 * T], F32, mixer)
        h_first = sb("h_first", [P, 2 * T], F32, mixer)
        sum_second = sb("sum_second", [P, PAD + T], F32, mixer)
        b_t = sb("b_t", [P, 2, KS, P], F32, mixer)
        c_t = sb("c_t", [P, 2, STATE_TILES * 32], F32, mixer)
        first = ExitStack()
        wave = sb("wave", [P, 4096], F32, first)
        first.close()
        second = ExitStack()
        mx = sb("mx", [P, 16, T], F32R, second)
        second.close()
        skip = ExitStack()
        sb("wave_place", [P, 4096], F32, skip)
        g1 = ExitStack()
        gates = sb("gates", [P, 16, T], F32, g1)
        g1.close()
        g2 = ExitStack()
        hs = sb("hs", [P, 2, 2, 4, T], F32R, g2)
        g2.close()
        skip.close()
        mixer.close()
        moe = ExitStack()
        acc = sb("acc", [P, TT, D], F32, moe)
        xts = sb("xts", [P, 2, TT, D], F32R, moe)
        sel = sb("sel", [P, TT, P], F32R, moe)
        gsel = sb("gsel", [P, TT, P], F32, moe)
        gsel2 = sb("gsel2", [P, TT, P], F32, moe)
        gsel_t = sb("gsel_t", [P, TT, P], F32, moe)
        xe = sb("xe", [P, 2, 2, KD, P], F32R, moe)
        he = sb("he", [P, 2, 512], F32, moe)
        het = sb("het", [P, 2, 2, 4, P], F32R, moe)
        y_sb = sb("y_sb", [P, D], F32, moe)
        tri = sb("tri", [P, P], F32, moe)
        ones = sb("ones", [P, P], F32, moe)
        iota = sb("iota", [P, P], F32, moe)
        rt = sb("rt", [P, 12, TT, EXPERTS], F32, moe)
        rs = sb("rs", [P, 12, TT], F32, moe)
        dest = sb("dest", [P, 2, TT], F32, moe)
        gate_w = sb("gate_w", [P, 2, TT], F32, moe)
        ovf = sb("ovf", [P, 9, EXPERTS], F32, moe)
        jobs_f = sb("jobs_f", [P, 16], F32, moe)
        jobs = sb("jobs", [P, 16], I32, moe)
        moe.close()

        ps = ctx.enter_context(nc.psum_tensor("ps", [P, 8, 512], F32))

        raw_landed = [sem(f"raw_landed{i}") for i in range(RAW)]
        hi_ready, lo_ready, unit_used = sem("hi_ready"), sem("lo_ready"), sem("unit_used")
        pair_free = [sem("pair_free0"), sem("pair_free1")]
        x_in, mem_in, par_in = [sem("x_in0"), sem("x_in1")], sem("mem_in"), sem("par_in")
        small_in, bc_in = sem("small_in"), [sem("bc_in0"), sem("bc_in1")]
        xtok_in, poolw_in, ln_in, moe_in = sem("xtok_in"), [sem("poolw_in0"), sem("poolw_in1")], sem("ln_in"), sem("moe_in")
        xs_hi, xs_ready = sem("xs_hi"), sem("xs_ready")
        ms_hi, ms_ready = sem("ms_hi"), sem("ms_ready")
        dve_order, dve_tail, pool_order = sem("dve_order"), sem("dve_tail"), sem("pool_order")
        bb_ready, bt_done, bt_ready = sem("bb_ready"), sem("bt_done"), sem("bt_ready")
        table_ready, table0_ready = sem("table_ready"), sem("table0_ready")
        y_copied, y_turned = sem("y_copied"), sem("y_turned")
        spun, half_gate, warmed = sem("spun"), sem("half_gate"), sem("warmed")
        prep_ready = sem("prep_ready")
        bu_done, rotated, z_ready = sem("bu_done"), sem("rotated"), sem("z_ready")
        prod_ready, h_ready, y_used = sem("prod_ready"), sem("h_ready"), sem("y_used")
        y_linear, y_gelu, ys_hi, ys_ready = sem("y_linear"), sem("y_gelu"), sem("ys_hi"), sem("ys_ready")
        pooled, pool_mixed, pool_scaled = sem("pooled"), sem("pool_mixed"), sem("pool_scaled")
        pad_ready = sem("pad_ready")
        mx_ready = sem("mx_ready")
        ln_var, ln_rstd, ln_shift, ln_norm = sem("ln_var"), sem("ln_rstd"), sem("ln_shift"), sem("ln_norm")
        ln_done, xt_done, xt_hi, xt_ready = sem("ln_done"), sem("xt_done"), sem("xt_hi"), sem("xt_ready")
        score_done, score_max, prob_exp, prob_ready = sem("score_done"), sem("score_max"), sem("prob_exp"), sem("prob_ready")
        pt_done, pt_ready, pv_done, at_hi, at_ready = sem("pt_done"), sem("pt_ready"), sem("pv_done"), sem("at_hi"), sem("at_ready")
        silu_ready, hs_ready = sem("silu_ready"), sem("hs_ready")
        router_hi, router_ready, logits_done = sem("router_hi"), sem("router_ready"), sem("logits_done")
        scored, scored_out = sem("scored"), sem("scored_out")
        expo_in, expo_done, picked, ranked, routed = sem("expo_in"), sem("expo_done"), sem("picked"), sem("ranked"), sem("routed")
        ones_ready = sem("ones_ready")
        xts_hi, xts_ready, c_ready = sem("xts_hi"), sem("xts_ready"), sem("c_ready")
        sel_ready, gsel_ready = sem("sel_ready"), sem("gsel_ready")
        misc_filled, misc_free = sem("misc_filled"), [sem("misc_free0"), sem("misc_free1")]
        het_hi = sem("het_hi")
        w1_free, w3_free, y_ready = sem("w1_free"), sem("w3_free"), sem("y_ready")
        out_ready, out_landed = sem("out_ready"), sem("out_landed")

        block = ctx.enter_context(nc.Block())

        def evacuated(engine, name):
            g = gemms[name]
            engine.wait_ge(pair_free[g["pair"]], g["use"] + 1)

        def gemm_ended(engine, name):
            engine.wait_ge(unit_used, gemms[name]["end"])

        def pair_of(name):
            return ps[:, 2 * gemms[name]["pair"]:2 * gemms[name]["pair"] + 2, :]

        def blocks(ap):
            return ap.rearrange("p b (h t) -> p (b h) t", t=T)

        def freed(instruction, name):
            instruction.then_inc(pair_free[gemms[name]["pair"]], 1)

        def view(buffer, slot, n, cols):
            return buffer[:, n % slot, :].rearrange("p (k c) -> p k c", c=cols)

        def hi_blocks(t, i, n):
            return t[:, i:i + n, :]

        logits_t = he[0:EXPERTS, 0, 0:T]
        spare = ln_gb[:, :, :].rearrange("p a d -> p (a d)")
        rots = [rot[:, :], spare[:, 0:512]]
        y_tok = spare[:, 512:1024].rearrange("p (t c) -> p t c", t=TT)
        h_buf = [x.rearrange("p (r t) -> p r t", r=2) for x in (h_first[:, :], spare[:, 1024:1536])]
        sums = [spare[:, 1536:1536 + PAD + T], sum_second[:, :]]
        wave_v = wave[:, :].rearrange("p (b j r t) -> p b j r t", b=2, j=4, r=2)
        prod_v = prod[:, :].rearrange("p (b q r t) -> p b q r t", b=2, q=2, r=2)
        y_v = u_pool[:, :, PAD:PAD + T]
        sil_v = wave[:, 0:2048].rearrange("p (b f t) -> p b f t", b=2, f=4)
        q_v = gates[:, 0:8, :]
        probs = gates[:, 8:12, :].rearrange("p (b q) t -> p b q t", b=2)
        probs_t = gates[:, 12:16, :].rearrange("p (b m) t -> p b m t", b=2)
        b_in = k_sb[:, 0:4, :].rearrange("p (r a) t -> p r (a t)", r=2)
        bb = prod[:, 0:1024].rearrange("p (r n) -> p r n", r=2)
        SSM_SLOTS = STATE_TILES + 8
        Y_LAG = 8
        H_LAG = 6
        WINDOWS_AT = 1

        def ssm_units(l):
            return gemms[("in", l, 4)]["first"] if l == 0 else gemms[("in", l, 2)]["first"] - 2

        def discretise(engine, order, l, done, between=None):
            def wide(i):
                return sp[:, i, STATE_TILES * l:STATE_TILES * (l + 1)].unsqueeze(2).broadcast_to([P, STATE_TILES, 32])
            def per_tile(ap):
                return ap.rearrange("p (j c) -> p j c", c=32)
            b_re, b_im = per_tile(b_in[:, 0, :]), per_tile(b_in[:, 1, :])
            t1, t2 = per_tile(prod[:, 1024:1536]), per_tile(prod[:, 1536:2048])
            for k, (x, y, op) in enumerate(((b_re, b_im, ALU.subtract), (b_im, b_re, ALU.add))):
                order.add(engine.tensor_tensor(t1, x, wide(6), ALU.mult))
                order.link(engine.tensor_tensor(t2, y, wide(7), ALU.mult))
                last = engine.tensor_tensor(per_tile(bb[:, k, :]), t1, t2, op)
                if k == 0:
                    order.link(last)
                    if between:
                        between()
            last.then_inc(done, 1)

        def phase_table(engine, order, l, j0, j1, scratch, done, between):
            nj = j1 - j0
            js = slice(STATE_TILES * l + j0, STATE_TILES * l + j1)
            tt = engine.tensor_tensor
            cos, sin = table[:, 0, j0:j1], table[:, 1, j0:j1]
            pc_, ps_ = turn[:, 0, j0:j1], turn[:, 1, j0:j1]
            sq = [turn_t[:, i, j0:j1] for i in range(3)]
            order.add(engine.memset(cos[:, :, 0:1], 1.0))
            order.add(engine.memset(sin[:, :, 0:1], 0.0))
            order.add(engine.tensor_copy(pc_, sp[:, 4, js]))
            order.link(engine.tensor_copy(ps_, sp[:, 5, js]))
            for m in TABLE_STEPS:
                wc, ws = [x.unsqueeze(2).broadcast_to([P, nj, m]) for x in (pc_, ps_)]
                t1, t2, t3, t4 = [x[:, 0:nj * m].rearrange("p (j t) -> p j t", t=m) for x in scratch]
                c, s = cos[:, :, 0:m], sin[:, :, 0:m]
                order.add(tt(t1, c, wc, ALU.mult))
                order.add(tt(t2, s, ws, ALU.mult))
                order.add(tt(t3, s, wc, ALU.mult))
                order.add(tt(t4, c, ws, ALU.mult))
                order.add(tt(sq[0], pc_, pc_, ALU.mult))
                order.add(tt(sq[1], ps_, ps_, ALU.mult))
                order.link(tt(sq[2], pc_, ps_, ALU.mult))
                order.add(tt(cos[:, :, m:2 * m], t1, t2, ALU.subtract))
                order.add(tt(sin[:, :, m:2 * m], t3, t4, ALU.add))
                order.link(tt(pc_, sq[0], sq[1], ALU.subtract))
                last = tt(ps_, sq[2], sq[2], ALU.add)
                if m < TABLE_STEPS[-1]:
                    order.link(last)
                between(m)
            last.then_inc(done, 1)

        def window_means(engine, order, l, g):
            order.add(engine.memset(sums[0][:, 0:PAD], 0.0))
            order.link(engine.memset(sums[1][:, 0:PAD], 0.0))
            s = u_pool[:, g, :]
            for level in range(g + 1):
                d = sums[level % 2]
                order.link(engine.tensor_tensor(d[:, PAD:], s[:, PAD:], s[:, PAD - 2 ** level:PAD + T - 2 ** level], ALU.add))
                s = d
            u = u_pool[:, g, :]
            order.link(engine.tensor_tensor(s[:, PAD:2 * PAD], s[:, PAD:2 * PAD], inv_count[:, g, :], ALU.mult))
            order.link(engine.tensor_tensor(s[:, 2 * PAD:], s[:, 2 * PAD:], inv_count[:, g, PAD - 1:PAD].broadcast_to([P, T - PAD]), ALU.mult))
            engine.tensor_tensor(u[:, PAD:], s[:, PAD:], u[:, PAD:], ALU.subtract).then_inc(pooled, 1)
            engine.wait_ge(pooled, KS * l + g + 1)

        @block.sync
        def _(sp_):
            def load_x(h):
                sp_.dma_start(wave[:, 1024 * h:1024 * h + 1024].rearrange("p (k t) -> p k t", t=T),
                              a["x_t"][:, 4 * h:4 * h + 4, :]).then_inc(x_in[h], 16)

            load_x(0)
            for n, (name, stack, r0, k, c0, cols) in enumerate(units):
                if n >= RAW:
                    sp_.wait_ge(lo_ready, n - RAW + 1)
                src = a[name][stack, r0:r0 + k * P, c0:c0 + cols].rearrange("(k p) c -> p k c", p=P)
                sp_.dma_start(view(raw, RAW, n, cols), src).then_inc(raw_landed[n % RAW], 16)
                if n == 0:
                    load_x(1)

            def load(i, expert, shift):
                name, r0, c0 = moe_units[i % NJ]
                n = N0 + i
                sp_.wait_ge(lo_ready, n - RAW + 1 + shift)
                rows = a[name].shape[1]
                src = a[name].rearrange("e r c -> (e r) c")[bass.ds(expert * rows + r0, 2 * P), c0:c0 + 512]
                src = src.rearrange("(k p) c -> p k c", p=P)
                sp_.dma_start(view(raw, RAW, n, 512), src).then_inc(raw_landed[n % RAW], 16)

            for i in range(LEAD):
                load(i, 0, 0)

            def job(j, expert, following):
                for i in range(LEAD, NJ):
                    load(i, expert, NJ * j)
                nxt = following()
                for i in range(NJ, NJ + LEAD):
                    load(i, nxt, NJ * j)

            with sp_.Fori(0, EXPERTS - 1) as j:
                job(j, j, lambda: j + 1)
            sp_.wait_ge(routed, 1)
            over = sp_.value_load(jobs[0:1, 0:1], min_val=0, max_val=OVER_MAX)
            job(EXPERTS - 1, EXPERTS - 1,
                lambda: sp_.value_load(jobs[0:1, 1:2], min_val=0, max_val=EXPERTS - 1))
            for o in range(OVER_MAX):
                with sp_.If(over > o):
                    expert = sp_.value_load(jobs[0:1, 1 + o:2 + o], min_val=0, max_val=EXPERTS - 1)
                    job(EXPERTS + o, expert,
                        lambda: sp_.value_load(jobs[0:1, 2 + o:3 + o], min_val=0, max_val=EXPERTS - 1))
                sp_.nop()
            for t in range(TT):
                sp_.wait_ge(out_ready, t + 1)
                sp_.dma_start(out[t * P:(t + 1) * P, :], acc[:, t, :]).then_inc(out_landed, 16)
            sp_.wait_ge(out_landed, 16 * TT)

        @block.scalar
        def _(act):
            split = [0]

            def split_hi(n):
                act.wait_ge(raw_landed[n % RAW], 16 * (n // RAW + 1))
                if n >= SPLIT:
                    act.wait_ge(unit_used, n - SPLIT + 1)
                nc.scalar.activation(w_hi[:, n % SPLIT, :], raw[:, n % RAW, :], ACT.Copy).then_inc(hi_ready, 1)

            def splits_to(n):
                while split[0] < min(n + LEAD, N0 + LEAD):
                    split_hi(split[0])
                    split[0] += 1

            for h in range(2):
                act.wait_ge(x_in[h], 16)
                nc.scalar.activation(xs[:, 4 * h:4 * h + 4, :], wave[:, 1024 * h:1024 * h + 1024].rearrange("p (k t) -> p k t", t=T),
                                     ACT.Copy).then_inc(xs_hi, 1)
                splits_to(1 - LEAD + h)
            splits_to(1)
            act.dma_start(wave[:, 2048:4096].rearrange("p (k t) -> p k t", t=T), a["mem_t"]).then_inc(mem_in, 16)
            act.dma_start(x_tok[:, :, :], a["x"].rearrange("(t p) d -> p t d", p=P)).then_inc(xtok_in, 16)
            splits_to(3)

            def warm(function):
                nc.scalar.activation(tiny[:, 61:62], ident[:, 0:1], function).then_inc(warmed, 1)

            def epilogue(name, fn):
                splits_to(gemms[name]["end"])
                gemm_ended(act, name)
                freed(fn(pair_of(name)), name)

            def values(l, c):
                epilogue(("v", l, c), lambda p: nc.scalar.activation(v_sb[:, :, 512 * c:512 * c + 512], p, ACT.Copy))

            def keys(l, c):
                epilogue(("k", l, c), lambda p: nc.scalar.activation(k_sb[:, 4 * c:4 * c + 4, :], blocks(p), ACT.Copy))

            def hi_of_x(i, tiles=range(TT)):
                for t in tiles:
                    act.wait_ge(xt_done, TT * i + t + 1)
                    src = ps[:, 4 + 2 * t:6 + 2 * t, :].rearrange("p b (k t) -> p (b k) t", t=P)
                    nc.scalar.activation(xs[:, 0:8, t * P:(t + 1) * P], src, ACT.Copy).then_inc(xt_hi, 1)

            def normalise(i, tensor):
                for t in range(TT):
                    act.wait_ge(ln_shift, TT * i + t + 1)
                    nc.scalar.activation(tensor[:, t, :], tensor[:, t, :], ACT.Identity,
                                         scale=tiny[:, 4 * t + 2:4 * t + 3], bias=tiny[:, 4 * t + 3:4 * t + 4]
                                         ).then_inc(ln_norm, 1)

            for l in range(DEPTH):
                base = ssm_units(l)

                def copy_y(h):
                    splits_to(base + STATE_TILES // 2 * (h + 1) + Y_LAG)
                    act.wait_ge(y_used, STATE_TILES * l + STATE_TILES // 2 * (h + 1))
                    if h or l:
                        act.wait_ge(y_turned, 2 * l + h)
                    nc.scalar.activation(y_tok, ps[:, 6 + h, :].rearrange("p (t c) -> p t c", t=TT), ACT.Copy).then_inc(y_copied, 1)

                epilogue(("in", l, 0), lambda p: nc.scalar.activation(u_sb[:, :, :], blocks(p), ACT.Copy))

                def copy_b():
                    act.wait_ge(bt_done, l + 1)
                    nc.scalar.activation(b_t[:, :, :, :], ps[:, 4:6, :].rearrange("p r (j s) -> p r j s", s=P),
                                         ACT.Copy).then_inc(bt_ready, 1)

                if l:
                    copy_b()
                if l == 0:
                    act.wait_ge(pad_ready, 1)
                epilogue(("in", l, 1), lambda p: nc.scalar.activation(u_pool[:, :, PAD:PAD + T], blocks(p), ACT.Copy))
                if l == 0:
                    act.wait_ge(mem_in, 16)
                    nc.scalar.activation(ms[:, 0:8, :], wave[:, 2048:4096].rearrange("p (k t) -> p k t", t=T),
                                         ACT.Copy).then_inc(ms_hi, 1)
                    act.wait_ge(small_in, 80)
                    nc.scalar.activation(router_s[:, 0, :], router[:, :], ACT.Copy).then_inc(router_hi, 1)
                for c in range(2, 6):
                    epilogue(("in", l, c), lambda p, c=c: nc.scalar.activation(
                        gates[:, 4 * (c - 2):4 * (c - 2) + 4, :], blocks(p), ACT.Sigmoid))
                    if l == 0 and c == 3:
                        copy_b()
                    if l == 1 and c == 5:
                        copy_y(0)
                if l == 0:
                    act.wait_ge(table_ready, 1)
                    values(0, 0)
                act.wait_ge(pool_mixed, l + 1)
                gemm_ended(act, ("in", l, 5))
                for g in range(KS):
                    last = nc.scalar.activation(xs[:, 8 + g, :], blocks(pair_of(("pool_mix", l)))[:, g, :],
                                                ACT.Copy, scale=small[:, 2, l, g:g + 1])
                    if g % 2:
                        last.then_inc(pool_scaled, 1)
                values(l, 1)
                if l == 0:
                    copy_y(0)
                    keys(0, 0)
                warm(ACT.Gelu_apprx_tanh)

                def gelu_y(h):
                    act.wait_ge(y_linear, 2 * l + h + 1)
                    nc.scalar.activation(y_v[:, 2 * h:2 * h + 2, :], y_v[:, 2 * h:2 * h + 2, :], ACT.Gelu_apprx_tanh).then_inc(y_gelu, 1)
                    act.wait_ge(y_gelu, 2 * l + h + 1)
                    nc.scalar.activation(xs[:, 2 * h:2 * h + 2, :], y_v[:, 2 * h:2 * h + 2, :], ACT.Copy).then_inc(ys_hi, 1)

                splits_to(base + SSM_SLOTS - 3)
                gelu_y(0)
                copy_y(1)
                gelu_y(1)
                warm(ACT.Sigmoid)
                splits_to(gemms[("glu", l, 0)]["end"])
                gemm_ended(act, ("glu", l, 0))
                for f in range(KS):
                    last = nc.scalar.activation(u_sb[:, f, :], blocks(pair_of(("glu", l, 0)))[:, f, :], ACT.Sigmoid,
                                                bias=small[:, 1, l, f:f + 1])
                    if f == 1:
                        last.then_inc(half_gate, 1)
                freed(last, ("glu", l, 0))
                splits_to(gemms[("out", l, 1)]["end"])
                normalise(3 * l, x_tok)
                splits_to(gemms[("k", l, 1)]["end"] - 1)
                hi_of_x(3 * l, (0,))
                keys(l, 1)
                hi_of_x(3 * l, (1,))
                for c in range(2):
                    epilogue(("q", l, c), lambda p, c=c: nc.scalar.activation(
                        q_v[:, 4 * c:4 * c + 4, :], blocks(p), ACT.Copy, scale=1.0 / 16.0))
                def exponent(h):
                    act.wait_ge(score_max, HEADS * l + h + 1)
                    for t in range(TT):
                        last = nc.scalar.activation(probs[:, h % 2, t, :], ps[:, 4 + h % 2, T * t:T * t + T], ACT.Exp,
                                                    bias=tiny[:, 16 + 4 * (h % 2) + t:17 + 4 * (h % 2) + t],
                                                    accum_out=tiny[:, 24 + 4 * (h % 2) + t:25 + 4 * (h % 2) + t])
                    last.then_inc(prob_exp, 1)

                warm(ACT.Exp)
                exponent(0)
                exponent(1)
                for h in range(HEADS):
                    n = HEADS * l + h
                    act.wait_ge(pt_done, n + 1)
                    nc.scalar.activation(probs_t[:, h % 2, :, :], ps[:, 6, :].rearrange("p (m t) -> p m t", t=T),
                                         ACT.Copy).then_inc(pt_ready, 1)
                    act.wait_ge(pv_done, n + 1)
                    nc.scalar.activation(xs[:, 2 * h:2 * h + 2, :], ps[:, 7, :].rearrange("p (b t) -> p b t", t=T),
                                         ACT.Copy).then_inc(at_hi, 1)
                    if h + 2 < HEADS:
                        exponent(h + 2)
                    splits_to(gemms[("o", l, 0)]["first"] + 2 * h + 1)
                splits_to(gemms[("o", l, 1)]["end"])
                normalise(3 * l + 1, x_tok)
                if l == 0:
                    splits_to(gemms[("v", 1, 0)]["end"] - 1)
                hi_of_x(3 * l + 1, (0,))
                if l == 0:
                    values(1, 0)
                hi_of_x(3 * l + 1, (1,))
                if l == 0:
                    for c, cols in enumerate(FF_CHUNKS):
                        name, f = ("ffn1", c), cols // P
                        splits_to(gemms[name]["end"])
                        gemm_ended(act, name)
                        if c >= 2:
                            act.wait_ge(hs_ready, c - 1)
                        freed(nc.scalar.activation(sil_v[:, c % 2, 0:f, :], blocks(pair_of(name))[:, 0:f, :], ACT.Silu), name)
                    splits_to(gemms[("ffn2", len(FF_CHUNKS) - 1, 1)]["end"])
                    normalise(2, x_tok)
                    splits_to(gemms[("k", 1, 0)]["end"] - 1)
                    hi_of_x(2, (0,))
                    act.wait_ge(bb_ready, 2)
                    keys(1, 0)
                    hi_of_x(2, (1,))

            act.wait_ge(ln_done, 2 * 5)
            nc.scalar.activation(xts[:, 0, :, :], x_tok[:, :, :], ACT.Copy).then_inc(xts_hi, 1)
            nc.scalar.activation(acc[:, :, :], x_tok[:, :, :], ACT.Copy, scale=ALPHA).then_inc(w1_free, 1)
            act.wait_ge(scored, 1)
            nc.scalar.activation(logits_t, ps[0:EXPERTS, 4, 0:T], ACT.Copy).then_inc(scored_out, 1)
            warm(ACT.Exp)
            act.wait_ge(expo_in, 1)
            nc.scalar.activation(rs[:, 3, :], rs[:, 2, :], ACT.Exp).then_inc(expo_done, 1)

            def tokens_out(i, r, buffer, turn_):
                act.wait_ge(misc_filled, r + 1 + turn_)
                nc.scalar.activation(xe[:, buffer, i // 2, 4 * (i % 2):4 * (i % 2) + 4, :],
                                     ps[:, 6 + r % 2, :].rearrange("p (k s) -> p k s", s=P),
                                     ACT.Copy).then_inc(misc_free[r % 2], 1)

            for i in range(4):
                tokens_out(i, i, 0, 0)

            def job(j, h):
                filled = NR * j + (NR * h + FIRST)

                def through(n0, n1):
                    for i in range(n0 + LEAD, n1 + LEAD):
                        m = N0 + i
                        act.wait_ge(raw_landed[m % RAW], NJ // RAW * 16 * j + (16 * (m // RAW + 1) + NJ // RAW * 16 * h))
                        act.wait_ge(unit_used, NJ * j + (m - SPLIT + 1 + NJ * h))
                        nc.scalar.activation(w_hi[:, m % SPLIT, :], raw[:, m % RAW, :], ACT.Copy).then_inc(hi_ready, 1)

                for i, (kind, c) in enumerate(stages):
                    for n in range(4 * i, 4 * i + 4):
                        through(n, n + 1)
                        if kind == "w1" and n == 4 * i + 3:
                            act.wait_ge(unit_used, NJ * j + (N0 + n + 1 + NJ * h))
                            nc.scalar.activation(he[:, c % 2, :], ps[:, 2 * (c % 2), :], ACT.Silu).then_inc(w1_free, 1)
                        for r in rounds_at.get(n + 1, ()):
                            what, q = rounds[r][:2]
                            bank = ps[:, 6 + r % 2, :]
                            if what == "turn":
                                act.wait_ge(misc_filled, filled + (r + 1))
                                nc.scalar.activation(het[:, q % 2, 0, :, :], bank.rearrange("p (k s) -> p k s", s=P),
                                                     ACT.Copy).then_inc(het_hi, 1)
                            elif what == "gates":
                                act.wait_ge(misc_filled, filled + (r + 1))
                                nc.scalar.activation(gsel_t[:, :, :], bank[:, 0:TT * P].rearrange("p (t s) -> p t s", s=P),
                                                     ACT.Copy).then_inc(misc_free[r % 2], 1)
                            elif what == "in":
                                tokens_out(q, r, 1 - h, filled)
                act.wait_ge(unit_used, NJ * j + (N0 + NJ + NJ * h))
                nc.scalar.activation(y_sb[:, :], ps[:, 4:6, :].rearrange("p b c -> p (b c)"), ACT.Copy).then_inc(y_ready, 1)

            with act.Fori(0, EXPERTS, 2) as j:
                job(j, 0)
                job(j, 1)
            over = act.value_load(jobs[0:1, 0:1], min_val=0, max_val=OVER_MAX)
            for o in range(OVER_MAX):
                with act.If(over > o):
                    job(EXPERTS + o - o % 2, o % 2)
                act.nop()
            normalise(5, acc)

        @block.vector
        def _(dve):
            order = Order(dve, dve_order)
            add, settle = order.add, order.settle
            split = [0]
            tt = nc.vector.tensor_tensor
            ts = nc.vector.tensor_scalar
            stt = nc.vector.scalar_tensor_tensor

            def split_lo(n, shift):
                dve.wait_ge(hi_ready, n + 1 + shift)
                tt(w_lo[:, n % SPLIT, :], raw[:, n % RAW, :], w_hi[:, n % SPLIT, :].bitcast(F32),
                   ALU.subtract).then_inc(lo_ready, 1)

            def splits_to(n):
                while split[0] < min(n + LEAD, N0 + LEAD):
                    split_lo(split[0], 0)
                    split[0] += 1

            def hi_lo(hi, lo, src, last_sem):
                link(nc.vector.tensor_copy(hi, src))
                tt(lo, src, hi.bitcast(F32), ALU.subtract).then_inc(last_sem, 1)

            def lo_of_input(src, dst, h, hi_sem, h_sem, done):
                dve.wait_ge(hi_sem, h_sem)
                tt(dst[:, 8 + h[0]:8 + h[1], :], src.rearrange("p (k t) -> p k t", t=T), dst[:, h[0]:h[1], :].bitcast(F32),
                   ALU.subtract).then_inc(done, 1)

            lo_of_input(wave[:, 0:1024], xs, (0, 4), xs_hi, 1, xs_ready)
            early = {8: lambda: lo_of_input(wave[:, 1024:2048], xs, (4, 8), xs_hi, 2, xs_ready)}
            for n, at in enumerate((2, 10, 16, 22, 29, 36, 43, 50, 57, 64, 71, 78)):
                early[at] = lambda n=n: splits_to(n + 1 - LEAD)
            steps = [0]

            def link(instruction):
                order.link(instruction)
                steps[0] += 1
                if steps[0] in early:
                    early.pop(steps[0])()


            (DT, RE, TH, MAG, COS, SIN, FRE, FIM, A, B, C, E, F, G) = [sp[:, i, :] for i in range(14)]
            are, aim, ldt = sp_in[:, 0, :], sp_in[:, 1, :], sp_in[:, 2, :]
            n1, n2 = F.bitcast(I32), G.bitcast(I32)
            dve.wait_ge(par_in, 16)

            def exp_exact(dst, x):
                link(ts(A, x, -170.0, 100.0, ALU.max, ALU.min))
                link(ts(B, A, 1.4426950408889634, MAGIC, ALU.mult, ALU.add))
                link(ts(B, B, MAGIC, None, ALU.subtract))
                link(stt(C, B, -0.693359375, A, ALU.mult, ALU.add))
                link(stt(C, B, 2.12194440e-4, C, ALU.mult, ALU.add))
                link(ts(E, C, 1.9875691500e-4, None, ALU.mult))
                for k in (1.3981999507e-3, 8.3334519073e-3, 4.1665795894e-2, 1.6666665459e-1, 5.0000001201e-1, 1.0):
                    link(stt(E, E, k, C, ALU.add, ALU.mult))
                link(ts(E, E, 1.0, None, ALU.add))
                link(ts(A, B, 0.5, MAGIC, ALU.mult, ALU.add))
                link(ts(A, A, MAGIC, None, ALU.subtract))
                link(tt(B, B, A, ALU.subtract))
                link(ts(n1, A, 127.0, 8388608.0, ALU.add, ALU.mult))
                link(ts(n2, B, 127.0, 8388608.0, ALU.add, ALU.mult))
                link(tt(E, E, F, ALU.mult))
                link(tt(dst, E, G, ALU.mult))

            exp_exact(DT, ldt)
            link(tt(RE, are, DT, ALU.mult))
            exp_exact(MAG, RE)
            link(tt(TH, aim, DT, ALU.mult))
            link(ts(A, TH, 0.15915494309189535, MAGIC, ALU.mult, ALU.add))
            link(ts(A, A, MAGIC, None, ALU.subtract))
            link(stt(TH, A, -6.28125, TH, ALU.mult, ALU.add))
            link(stt(TH, A, -1.9350051879882812e-3, TH, ALU.mult, ALU.add))
            link(stt(TH, A, -3.0199159819591886e-7, TH, ALU.mult, ALU.add))
            link(ts(A, TH, 0.25, None, ALU.mult))
            link(tt(B, A, A, ALU.mult))
            link(ts(C, B, -1.9515295891e-4, 8.3321608736e-3, ALU.mult, ALU.add))
            link(tt(C, C, B, ALU.mult))
            link(stt(C, C, -1.6666654611e-1, B, ALU.add, ALU.mult))
            link(stt(SIN, C, 1.0, A, ALU.add, ALU.mult))
            link(ts(C, B, 2.443315711809948e-5, -1.388731625493765e-3, ALU.mult, ALU.add))
            link(tt(C, C, B, ALU.mult))
            link(stt(C, C, 4.166664568298827e-2, B, ALU.add, ALU.mult))
            link(stt(C, C, -0.5, B, ALU.add, ALU.mult))
            link(ts(COS, C, 1.0, None, ALU.add))
            for _ in range(2):
                link(tt(A, SIN, SIN, ALU.mult))
                link(stt(SIN, SIN, 2.0, COS, ALU.mult, ALU.mult))
                link(ts(COS, A, -2.0, 1.0, ALU.mult, ALU.add))
            link(tt(A, MAG, COS, ALU.mult))
            link(tt(B, MAG, SIN, ALU.mult))
            link(ts(A, A, 1.0, None, ALU.subtract))
            link(tt(C, are, are, ALU.mult))
            link(tt(E, aim, aim, ALU.mult))
            link(tt(C, C, E, ALU.add))
            link(nc.vector.reciprocal(C, C))
            link(tt(E, A, are, ALU.mult))
            link(tt(F, B, aim, ALU.mult))
            link(tt(E, E, F, ALU.add))
            link(tt(FRE, E, C, ALU.mult))
            link(tt(E, B, are, ALU.mult))
            link(tt(F, A, aim, ALU.mult))
            link(tt(E, E, F, ALU.subtract))
            tt(FIM, E, C, ALU.mult).then_inc(prep_ready, 1)
            dve.wait_ge(prep_ready, 1)
            assert not early, steps
            splits_to(10)
            dve.wait_ge(bc_in[0], 48)
            discretise(nc.vector, order, 0, bb_ready, lambda: splits_to(11))
            splits_to(12)
            dve.wait_ge(small_in, 80)
            after = {1: 12, 2: 13, 4: 13, 8: 14, 16: 14, 32: 15, 64: 16}
            phase_table(nc.vector, order, 0, 0, TABLE_DVE, [wave[:, 512 * i:512 * i + 512] for i in range(4)], table0_ready,
                        lambda m: splits_to(after[m]))

            def rotate(l, j):
                n = STATE_TILES * l + j
                q, b = j // 4, (j // 4) % 2
                dve.wait_ge(bu_done, n + 1)
                if q >= 2 and j % 4 == 0:
                    dve.wait_ge(prod_ready, STATE_TILES * l + 4 * (q - 1))
                elif l and j % 4 == 0:
                    dve.wait_ge(prod_ready, STATE_TILES * l)
                if n >= 2:
                    dve.wait_ge(spun, n - 1)
                w = wave_v[:, b, j % 4]
                bu = ps[:, 4 + n % 2, :]
                cos = table[:, 0, j:j + 1, :].broadcast_to([P, 4, HALF])
                sin = table[:, 1, j:j + 1, :].broadcast_to([P, 2, HALF])
                add(tt(w.rearrange("p r (s t) -> p (r s) t", t=HALF), bu.rearrange("p (s t) -> p s t", t=HALF), cos, ALU.mult))
                r2 = rots[n % 2].rearrange("p (r s t) -> p r s t", r=2, t=HALF)
                add(tt(r2[:, 0], bu[:, T:2 * T].rearrange("p (s t) -> p s t", t=HALF), sin, ALU.mult))
                tt(r2[:, 1], bu[:, 0:T].rearrange("p (s t) -> p s t", t=HALF), sin, ALU.mult).then_inc(rotated, 1)

            def scan(l, q, half):
                w = wave_v[:, q % 2]
                dve.wait_ge(spun, STATE_TILES * l + 4 * q + 4)
                for j in range(4):
                    mag = MAG[:, STATE_TILES * l + 4 * q + j:STATE_TILES * l + 4 * q + j + 1].broadcast_to([P, HALF])
                    for r in range(2):
                        z = w[:, j, r, HALF * half:HALF * half + HALF]
                        init = carry[:, 2 + r, j:j + 1] if half else 0.0
                        last = nc.vector.tensor_tensor_scan(z, mag, z, init, ALU.mult, ALU.add)
                        if half and (j, r) == (3, 1):
                            last.then_inc(z_ready, 1)
                        else:
                            add(last)
                if not half:
                    settle()
                    zr, zi = w[:, :, 0, HALF - 1:HALF].rearrange("p j t -> p (j t)"), w[:, :, 1, HALF - 1:HALF].rearrange("p j t -> p (j t)")
                    c, s = turn[:, 0, 4 * q:4 * q + 4], turn[:, 1, 4 * q:4 * q + 4]
                    add(tt(carry[:, 0, :], zr, c, ALU.mult))
                    add(tt(carry[:, 1, :], zi, s, ALU.mult))
                    link(tt(carry[:, 3, :], zr, s, ALU.mult))
                    link(tt(carry[:, 2, :], carry[:, 0, :], carry[:, 1, :], ALU.subtract))
                    link(tt(carry[:, 0, :], zi, c, ALU.mult))
                    link(tt(carry[:, 3, :], carry[:, 3, :], carry[:, 0, :], ALU.add))

            def layer_norm(i, sources, tensor, released=None, scaled=True):
                def shift(t):
                    dve.wait_ge(ln_rstd, TT * i + t + 1)
                    stt(tiny[:, 4 * t + 3:4 * t + 4], tiny[:, 4 * t:4 * t + 1], -1.0, tiny[:, 4 * t + 2:4 * t + 3],
                        ALU.mult, ALU.mult).then_inc(ln_shift, 1)

                st = tiny[:, 32:56].rearrange("p (t h s) -> p t h s", t=TT, h=2)
                if not scaled:
                    for t in range(TT):
                        released(t)
                        if t:
                            shift(t - 1)
                        for half in range(2):
                            add(nc.vector.bn_stats(st[:, t, half, :], tensor[:, t, 512 * half:512 * half + 512]))
                        settle()
                        link(nc.vector.bn_aggr(tiny[:, 4 * t:4 * t + 2], st[:, t, :, :].rearrange("p h s -> p (h s)")))
                        ts(tiny[:, 8 + t:9 + t], tiny[:, 4 * t + 1:4 * t + 2], LN_EPS, None, ALU.add).then_inc(ln_var, 1)
                for half in range(2) if scaled else ():
                    wait, bank, release = sources[half]
                    wait()
                    for t in range(TT):
                        xt = tensor[:, t, 512 * half:512 * half + 512]
                        last = stt(xt, xt, ALPHA, bank(t), ALU.mult, ALU.add)
                        if t == TT - 1:
                            release(last)
                        else:
                            link(last)
                    for t in range(TT):
                        if t == TT - 1:
                            settle()
                            released[half]()
                        add(nc.vector.bn_stats(st[:, t, half, :], tensor[:, t, 512 * half:512 * half + 512]))
                        if half:
                            settle()
                            link(nc.vector.bn_aggr(tiny[:, 4 * t:4 * t + 2], st[:, t, :, :].rearrange("p h s -> p (h s)")))
                            ts(tiny[:, 8 + t:9 + t], tiny[:, 4 * t + 1:4 * t + 2], LN_EPS, None, ALU.add).then_inc(ln_var, 1)
                for t in range(TT) if scaled else (TT - 1,):
                    shift(t)

                def rest(t):
                    dve.wait_ge(ln_norm, TT * i + t + 1)
                    if t == 0:
                        dve.wait_ge(ln_in, 32 * (i + 1))
                    link(tt(tensor[:, t, :], tensor[:, t, :], ln_gb[:, 0, :], ALU.mult))
                    tt(tensor[:, t, :], tensor[:, t, :], ln_gb[:, 1, :], ALU.add).then_inc(ln_done if i < 5 else out_ready, 1)
                return rest

            def rest_and_filler(i, rest, filler):
                first_, end = gemms[filler]["first"], gemms[filler]["end"]
                rest(0)
                splits_to(first_ + 1)
                rest(1)
                lo_of_x(i, (0,))
                splits_to(end - 2)
                lo_of_x(i, (1,))
                splits_to(end)

            def paired_source(name, half_tokens):
                g = gemms[name]
                return (lambda: (splits_to(g["end"]), gemm_ended(dve, name)), lambda t: ps[:, 2 * g["pair"] + t, :], lambda ins: freed(ins, name))

            def lo_of_x(i, tiles=range(TT)):
                for t in tiles:
                    dve.wait_ge(xt_hi, TT * i + t + 1)
                    src = ps[:, 4 + 2 * t:6 + 2 * t, :].rearrange("p b (k t) -> p (b k) t", t=P)
                    tt(xs[:, 8:16, t * P:(t + 1) * P], src, xs[:, 0:8, t * P:(t + 1) * P].bitcast(F32),
                       ALU.subtract).then_inc(xt_ready, 1)

            for l in range(DEPTH):
                base = ssm_units(l)
                splits_to(base)
                if l == 0:
                    dve.wait_ge(table0_ready, 1)
                else:
                    dve.wait_ge(table_ready, 2)
                dve.wait_ge(bc_in[l], 48)
                ts(c_t[:, 1, :], c_t[:, 1, :], -1.0, None, ALU.mult).then_inc(c_ready, 1)

                def linear(h):
                    dve.wait_ge(y_turned, 2 * l + h + 1)
                    if h == 0:
                        evacuated(dve, ("in", l, 0))
                    for f in (2 * h, 2 * h + 1):
                        last = stt(y_v[:, f, :], u_sb[:, f, :], small[:, 0, l, f:f + 1], ps[:, 6 + h, T * (f % 2):T * (f % 2) + T],
                                   ALU.mult, ALU.add)
                        if f % 2 == 0:
                            add(last)
                    last.then_inc(y_linear, 1)

                def combine(j):
                    n = STATE_TILES * l + j
                    p = prod_v[:, j % 2]
                    dve.wait_ge(prod_ready, n + 1)
                    if n >= 2:
                        dve.wait_ge(y_used, n - 1)
                    add(tt(h_buf[j % 2][:, 0, :], p[:, 0, 0, :], p[:, 1, 1, :], ALU.subtract))
                    tt(h_buf[j % 2][:, 1, :], p[:, 0, 1, :], p[:, 1, 0, :], ALU.add).then_inc(h_ready, 1)

                def lo_of_y(h):
                    dve.wait_ge(ys_hi, 2 * l + h + 1)
                    tt(xs[:, 4 + 2 * h:6 + 2 * h, :], y_v[:, 2 * h:2 * h + 2, :], xs[:, 2 * h:2 * h + 2, :].bitcast(F32),
                       ALU.subtract).then_inc(ys_ready, 1)

                def gate_pool(c):
                    name = ("pool_up", l, c)
                    splits_to(gemms[name]["end"])
                    gemm_ended(dve, name)
                    g = gates[:, 8 + 4 * c:12 + 4 * c, :]
                    freed(tt(g, blocks(pair_of(name)), g, ALU.mult), name)

                def pooling_lo():
                    for g in range(KS):
                        if g % 2 == 0:
                            dve.wait_ge(pool_scaled, 2 * l + g // 2 + 1)
                        last = stt(xs[:, 12 + g, :], blocks(pair_of(("pool_mix", l)))[:, g, :], small[:, 2, l, g:g + 1],
                                   xs[:, 8 + g, :].bitcast(F32), ALU.mult, ALU.subtract)
                        if g < KS - 1:
                            add(last)
                    freed(last, ("pool_mix", l))

                mixed = gemms[("pool_mix", l)]["first"] - base - 1
                for i in range(STATE_TILES):
                    splits_to(base + 1 + i)
                    if l == 0 and i == TABLE_DVE:
                        dve.wait_ge(table_ready, 1)
                    if i % 4 < 2 and i >= 4:
                        scan(l, i // 4 - 1, i % 4)
                    rotate(l, i)
                    if i >= H_LAG:
                        combine(i - H_LAG)
                    if i == mixed:
                        pooling_lo()
                for i in range(STATE_TILES, SSM_SLOTS):
                    splits_to(base + 1 + i)
                    if i < STATE_TILES + 2:
                        scan(l, STATE_TILES // 4 - 1, i % 4)
                    if i < STATE_TILES + H_LAG:
                        combine(i - H_LAG)
                    if i == mixed:
                        pooling_lo()
                    if l == 0 and i == SSM_SLOTS - 2:
                        gate_pool(0)
                    if i == SSM_SLOTS - 4:
                        linear(0)
                    if i == SSM_SLOTS - 3:
                        lo_of_y(0)
                linear(1)
                lo_of_y(1)

                gate_pool(1 if l == 0 else 0)
                splits_to(gemms[("glu", l, 0)]["end"])
                for h in range(2):
                    if h == 0:
                        dve.wait_ge(half_gate, l + 1)
                    else:
                        evacuated(dve, ("glu", l, 0))
                    hf = slice(2 * h, 2 * h + 2)
                    link(tt(y_v[:, hf, :], y_v[:, hf, :], u_sb[:, hf, :], ALU.mult))
                    hi_lo(xs[:, hf, :], xs[:, 4 + 2 * h:6 + 2 * h, :], y_v[:, hf, :], ys_ready)
                if l:
                    gate_pool(1)
                for c in range(2):
                    name = ("ssm_up", l, c)
                    splits_to(gemms[name]["end"])
                    gemm_ended(dve, name)
                    g = gates[:, 4 * c:4 * c + 4, :]
                    freed(tt(g, blocks(pair_of(name)), g, ALU.mult), name)
                    evacuated(dve, name)
                    evacuated(dve, ("pool_up", l, c))
                    link(tt(g, g, gates[:, 8 + 4 * c:12 + 4 * c, :], ALU.add))
                    hi_lo(mx[:, 4 * c:4 * c + 4, :], mx[:, 8 + 4 * c:12 + 4 * c, :], g, mx_ready)
                if l == 0:
                    dve.wait_ge(xtok_in, 16)
                rest = layer_norm(3 * l, [paired_source(("out", l, c), c) for c in range(2)], x_tok,
                                  [lambda c=c: evacuated(dve, ("out", l, c)) for c in range(2)])
                rest_and_filler(3 * l, rest, ("k", l, 1))
                splits_to(gemms[("q", l, 1)]["end"])
                def maximum(h):
                    n, o = HEADS * l + h, 4 * (h % 2)
                    dve.wait_ge(score_done, n + 1)
                    link(nc.vector.tensor_reduce(tiny[:, 56:58], ps[:, 4 + h % 2, :].rearrange("p (t m) -> p t m", t=TT), AX_X, ALU.max))
                    ts(tiny[:, 16 + o:18 + o], tiny[:, 56:58], -1.0, None, ALU.mult).then_inc(score_max, 1)
                    dve.wait_ge(score_max, n + 1)

                def divide(h):
                    n, o = HEADS * l + h, 4 * (h % 2)
                    dve.wait_ge(prob_exp, n + 1)
                    link(nc.vector.reciprocal(tiny[:, 58:60], tiny[:, 24 + o:26 + o]))
                    for t in range(TT):
                        last = ts(probs[:, h % 2, t, :], probs[:, h % 2, t, :], tiny[:, 58 + t:59 + t], None, ALU.mult)
                        if t < TT - 1:
                            add(last)
                    last.then_inc(prob_ready, 1)
                    dve.wait_ge(prob_ready, n + 1)

                maximum(0)
                divide(0)
                maximum(1)
                for h in range(HEADS):
                    if h + 1 < HEADS:
                        divide(h + 1)
                    dve.wait_ge(at_hi, HEADS * l + h + 1)
                    tt(xs[:, 8 + 2 * h:10 + 2 * h, :], ps[:, 7, :].rearrange("p (b t) -> p b t", t=T),
                       xs[:, 2 * h:2 * h + 2, :].bitcast(F32), ALU.subtract).then_inc(at_ready, 1)
                    if h + 2 < HEADS:
                        maximum(h + 2)
                    splits_to(gemms[("o", l, 0)]["first"] + 2 * h + 1)
                rest = layer_norm(3 * l + 1, [paired_source(("o", l, c), c) for c in range(2)], x_tok,
                                  [lambda c=c: evacuated(dve, ("o", l, c)) for c in range(2)])
                if l == 0:
                    rest_and_filler(1, rest, ("v", 1, 0))
                else:
                    rest(0)
                    rest(1)
                    lo_of_x(4)
                if l == 0:
                    for c, cols in enumerate(FF_CHUNKS):
                        name, f = ("ffn3", c), cols // P
                        splits_to(gemms[name]["end"])
                        gemm_ended(dve, name)
                        evacuated(dve, ("ffn1", c))
                        if c >= 2:
                            gemm_ended(dve, ("ffn2", c - 2, 1))
                        h_ = sil_v[:, c % 2, 0:f, :]
                        freed(tt(h_, blocks(pair_of(name))[:, 0:f, :], h_, ALU.mult), name)
                        evacuated(dve, name)
                        hi_lo(hs[:, c % 2, 0, 0:f, :], hs[:, c % 2, 1, 0:f, :], h_, hs_ready)
                    last = ("ffn2", len(FF_CHUNKS) - 1, 1)
                    rest = layer_norm(2, [(lambda h=h: (splits_to(gemms[last]["end"] - 1 + h), gemm_ended(dve, ("ffn2", len(FF_CHUNKS) - 1, h))),
                                           lambda t, h=h: ps[:, 4 + 2 * t + h, :], add) for h in range(2)], x_tok, [lambda: None] * 2)
                    rest_and_filler(2, rest, ("k", 1, 0))

            lg, eq, oh1, oh2, lg2, both, rank, dexp, hi_r, tmp = [rt[:, i] for i in range(10)]
            m1, m2, diff, ex, idx, i1, i2 = [rs[:, i] for i in range(7)]

            def per_token(x):
                return x.unsqueeze(2).broadcast_to([P, TT, EXPERTS])

            def per_expert(x):
                return x.unsqueeze(1).broadcast_to([P, TT, EXPERTS])

            dve.wait_ge(ln_done, 2 * 5)
            dve.wait_ge(xts_hi, 1)
            tt(xts[:, 1, :, :], x_tok[:, :, :], xts[:, 0, :, :].bitcast(F32), ALU.subtract).then_inc(xts_ready, 1)
            nc.vector.memset(gsel_t[:, :, :], 0.0).then_inc(w3_free, 1)
            nc.vector.memset(y_sb[:, :], 0.0).then_inc(y_ready, 1)
            cnt, over_, incl, pos, base_o, sel_o, one8, base_c, low = [ovf[:, i, :] for i in range(9)]
            add(nc.vector.memset(one8, 1.0))
            add(ts(low, iota8[:, :], -8.0, None, ALU.add))
            add(ts(base_c, iota8[:, :], -128.0, 128.0 * (EXPERTS - 1), ALU.mult, ALU.add))
            dve.wait_ge(logits_done, 1)
            link(nc.vector.tensor_copy(lg, ps[:, 5, 0:TT * EXPERTS].rearrange("p (t e) -> p t e", t=TT)))

            def best(scores, m, i_, oh):
                link(nc.vector.tensor_reduce(m, scores, AX_X, ALU.max))
                link(tt(eq, scores, per_token(m), ALU.is_equal))
                link(tt(eq, eq, per_expert(low), ALU.mult))
                link(nc.vector.tensor_reduce(i_, eq, AX_X, ALU.min))
                link(tt(oh, per_expert(low), per_token(i_), ALU.is_equal))

            best(lg, m1, i1, oh1)
            link(stt(lg2, oh1, -1e30, lg, ALU.mult, ALU.add))
            best(lg2, m2, i2, oh2)
            tt(both, oh1, oh2, ALU.add).then_inc(picked, 1)
            tt(diff, m2, m1, ALU.subtract).then_inc(expo_in, 1)
            dve.wait_ge(ranked, 1)
            rank_ps = ps[:, 6, 0:TT * EXPERTS].rearrange("p (t e) -> p t e", t=TT)
            add(ts(over_, ps[:, 6, TT * EXPERTS:(TT + 1) * EXPERTS], 128.0, None, ALU.is_gt))
            add(stt(dexp, per_expert(iota8[:, :]), 128.0, rank_ps, ALU.mult, ALU.add))
            link(ts(hi_r, rank_ps, 128.0, None, ALU.is_ge))
            link(nc.vector.tensor_tensor_scan(incl, one8, over_, 0.0, ALU.mult, ALU.add))
            link(tt(pos, incl, over_, ALU.subtract))
            link(stt(base_o, pos, 128.0, base_c, ALU.mult, ALU.add))
            link(tt(hi_r, hi_r, per_expert(base_o), ALU.mult))
            link(tt(dexp, dexp, hi_r, ALU.add))
            add(tt(tmp, oh1, dexp, ALU.mult))
            link(tt(eq, oh2, dexp, ALU.mult))
            add(nc.vector.tensor_reduce(dest[:, 0, :], tmp, AX_X, ALU.add))
            link(nc.vector.tensor_reduce(dest[:, 1, :], eq, AX_X, ALU.add))
            dve.wait_ge(moe_in, 32)

            def select(t):
                link(ts(gsel2[:, t, :], iota[:, :], dest[:, 0, t:t + 1], None, ALU.is_equal))
                stt(sel[:, t, :], iota[:, :], dest[:, 1, t:t + 1], gsel2[:, t, :], ALU.is_equal, ALU.add).then_inc(sel_ready, 1)

            def select_gated(t):
                add(ts(gsel[:, t, :], iota[:, :], dest[:, 0, t:t + 1], gate_w[:, 0, t:t + 1], ALU.is_equal, ALU.mult))
                link(ts(gsel2[:, t, :], iota[:, :], dest[:, 1, t:t + 1], gate_w[:, 1, t:t + 1], ALU.is_equal, ALU.mult))
                tt(gsel[:, t, :], gsel[:, t, :], gsel2[:, t, :], ALU.add).then_inc(gsel_ready, 1)

            for t in range(TT):
                select(t)
            link(nc.vector.memset(jobs_f[:, :], 0.0))
            link(nc.vector.tensor_copy(jobs_f[:, 0:1], incl[:, EXPERTS - 1:EXPERTS]))
            for o in range(OVER_MAX):
                link(stt(sel_o, pos, float(o), over_, ALU.is_equal, ALU.mult))
                link(tt(sel_o, sel_o, iota8[:, :], ALU.mult))
                link(nc.vector.tensor_reduce(jobs_f[:, 1 + o:2 + o], sel_o, AX_X, ALU.add))
            nc.vector.tensor_copy(jobs[:, :], jobs_f[:, :]).then_inc(routed, 1)
            dve.wait_ge(expo_done, 1)
            link(ts(idx, ex, 1.0, None, ALU.add))
            link(nc.vector.reciprocal(gate_w[:, 0, :], idx))
            link(tt(gate_w[:, 1, :], ex, gate_w[:, 0, :], ALU.mult))

            def add_out(q, r, turn_):
                dve.wait_ge(misc_filled, FIRST + r + 1 + turn_)
                piece = acc[:, q // 2, 512 * (q % 2):512 * (q % 2) + 512]
                tt(piece, ps[:, 6 + r % 2, :], piece, ALU.add).then_inc(misc_free[r % 2], 1)

            def job(j, steps):
                order.turns = steps * j

                for i, (kind, c) in enumerate(stages):
                    for n in range(4 * i, 4 * i + 4):
                        split_lo(N0 + n + LEAD, NJ * j)
                        if kind == "w3" and n == 4 * i + 3:
                            dve.wait_ge(unit_used, N0 + n + 1 + NJ * j)
                            dve.wait_ge(w1_free, 2 + c + FE_CHUNKS * j)
                            tt(he[:, c % 2, :], ps[:, 2 * (c % 2) + 1, :], he[:, c % 2, :], ALU.mult).then_inc(w3_free, 1)
                        for r in rounds_at.get(n + 1, ()):
                            what, q = rounds[r][:2]
                            if what == "out":
                                add_out(q, r, NR * j)
                            elif what == "turn":
                                dve.wait_ge(het_hi, q + 1 + FE_CHUNKS * j)
                                tt(het[:, q % 2, 1, :, :], ps[:, 6 + r % 2, :].rearrange("p (k s) -> p k s", s=P),
                                   het[:, q % 2, 0, :, :].bitcast(F32), ALU.subtract).then_inc(misc_free[r % 2], 1)
                        if kind == "w1" and c in (1, 2) and n == 4 * i + 1:
                            if c == 1:
                                dve.wait_ge(misc_filled, FIRST + NR * j)
                                dve.wait_ge(sel_ready, TT + TT * j)
                            select_gated(c - 1)
                        if (kind, c) in (("w3", 2), ("w2", 1)) and n == 4 * i + 1:
                            if kind == "w3":
                                dve.wait_ge(gsel_ready, TT + TT * j)
                                link(ts(dest[:, :, :], dest[:, :, :], -128.0, None, ALU.add))
                            select(0 if kind == "w3" else 1)
            JOB_STEPS = 7
            with dve.Fori(0, EXPERTS) as j:
                before = order.n
                job(j, JOB_STEPS)
                assert order.n - before == JOB_STEPS, order.n - before
            order.n = before
            over = dve.value_load(jobs[0:1, 0:1], min_val=0, max_val=OVER_MAX)
            for o in range(OVER_MAX):
                with dve.If(over > o):
                    order.n = before
                    job(EXPERTS + o, JOB_STEPS)
                dve.nop()
            order.sem, order.n, order.turns = dve_tail, 0, 0
            def arrived(t):
                for r in (2 * t, 2 * t + 1):
                    add_out(r, r, over * NR + EXPERTS * NR)
                for b in range(2):
                    dve.wait_ge(misc_free[b], over * (NR // 2) + (FIRST // 2 + NR // 2 * EXPERTS + t + 1))

            rest = layer_norm(5, None, acc, arrived, scaled=False)
            rest(0)
            rest(1)

        @block.gpsimd
        def _(pool):
            order = Order(pool, pool_order)

            def load_ln(i):
                l, which = divmod(i, 3)
                g, b = (("ln_mix_g", "ln_mix_b"), ("ln_xa_g", "ln_xa_b"), ("ln_ffn_g", "ln_ffn_b"))[which]
                if i:
                    pool.wait_ge(ln_done, TT * i)
                pool.dma_start(ln_gb[:, 0, :], a[g][l:l + 1, :].broadcast_to([P, D])).then_inc(ln_in, 16)
                pool.dma_start(ln_gb[:, 1, :], a[b][l:l + 1, :].broadcast_to([P, D])).then_inc(ln_in, 16)

            def deviation(i):
                for t in range(TT):
                    pool.wait_ge(ln_var, TT * i + t + 1)
                    nc.gpsimd.tensor_tensor(tiny[:, 4 * t + 2:4 * t + 3], tiny[:, 8 + t:9 + t], tiny[:, 60:61],
                                            ALU.pow).then_inc(ln_rstd, 1)

            pool.dma_start(sp_in[:, :, :], a["ssm_par"]).then_inc(par_in, 16)
            pool.dma_start(b_in, a["ssm_b"][0]).then_inc(bc_in[0], 16)
            pool.dma_start(c_t[:, 0, :], a["ssm_c"][0, 0]).then_inc(bc_in[0], 16)
            pool.dma_start(c_t[:, 1, :], a["ssm_c"][0, 1]).then_inc(bc_in[0], 16)
            pool.dma_start(small[:, :, :, :], a["chan_par"]).then_inc(small_in, 16)
            pool.dma_start(ident[:, :], a["c_ident"]).then_inc(small_in, 16)
            pool.dma_start(iota8[:, :], a["c_iota8"]).then_inc(small_in, 16)
            pool.dma_start(inv_count[:, :, :], a["c_inv"]).then_inc(small_in, 16)
            pool.dma_start(router[:, :], a["router"]).then_inc(small_in, 16)
            pool.dma_start(pool_w[:, :, :], a["pool_wt"][0]).then_inc(poolw_in[0], 16)
            nc.gpsimd.memset(u_pool[:, :, 0:PAD], 0.0).then_inc(pad_ready, 1)
            order.link(nc.gpsimd.memset(tiny[:, 60:61], -0.5))
            pool.wait_ge(ms_hi, 1)
            nc.gpsimd.tensor_tensor(ms[:, 8:16, :], wave[:, 2048:4096].rearrange("p (k t) -> p k t", t=T), ms[:, 0:8, :].bitcast(F32),
                                    ALU.subtract).then_inc(ms_ready, 1)
            pool.wait_ge(small_in, 80)
            pool.wait_ge(router_hi, 1)
            nc.gpsimd.tensor_tensor(router_s[:, 1, :], router[:, :], router_s[:, 0, :].bitcast(F32), ALU.subtract).then_inc(router_ready, 1)
            pool.wait_ge(prep_ready, 1)
            phase_table(nc.gpsimd, order, 0, TABLE_DVE, STATE_TILES, [v_sb[:, i // 2, 512 * (i % 2):512 * (i % 2) + 512] for i in range(4)], table_ready,
                        lambda m: None)
            for l in range(DEPTH):
                pool.wait_ge(small_in, 80)
                if l:
                    pool.wait_ge(ln_done, TT * 3)
                pool.wait_ge(pad_ready, 1)
                for i in range(STATE_TILES + 5):
                    if i >= 5:
                        j = i - 5
                        n = STATE_TILES * l + j
                        if j % 4 == 0:
                            pool.wait_ge(z_ready, 4 * l + j // 4 + 1)
                        if n >= 2:
                            pool.wait_ge(h_ready, n - 1)
                        z = wave_v[:, (j // 4) % 2, j % 4].rearrange("p r (s t) -> p (r s) t", t=HALF)
                        for k in range(2):
                            tab = table[:, k, j:j + 1, :].broadcast_to([P, 4, HALF])
                            dst = prod_v[:, j % 2, k].rearrange("p r (s t) -> p (r s) t", t=HALF)
                            last = nc.gpsimd.tensor_tensor(dst, z, tab, ALU.mult)
                            if k == 0:
                                order.add(last)
                        last.then_inc(prod_ready, 1)
                    if i < STATE_TILES:
                        n = STATE_TILES * l + i
                        pool.wait_ge(rotated, n + 1)
                        w, r2 = wave_v[:, (i // 4) % 2, i % 4], rots[n % 2]
                        order.add(nc.gpsimd.tensor_tensor(w[:, 0, :], w[:, 0, :], r2[:, 0:T], ALU.add))
                        nc.gpsimd.tensor_tensor(w[:, 1, :], w[:, 1, :], r2[:, T:2 * T], ALU.subtract).then_inc(spun, 1)
                    if WINDOWS_AT <= i < WINDOWS_AT + KS:
                        if i == WINDOWS_AT:
                            evacuated(pool, ("in", l, 1))
                        window_means(nc.gpsimd, order, l, i - WINDOWS_AT)
                pool.wait_ge(y_turned, 2 * (l + 1))
                pool.wait_ge(pooled, KS * (l + 1))
                load_ln(3 * l)
                deviation(3 * l)
                load_ln(3 * l + 1)
                deviation(3 * l + 1)
                load_ln(3 * l + 2)
                if l == 0:
                    pool.wait_ge(y_used, STATE_TILES)
                    pool.dma_start(c_t[:, 0, :], a["ssm_c"][1, 0]).then_inc(bc_in[1], 16)
                    pool.dma_start(c_t[:, 1, :], a["ssm_c"][1, 1]).then_inc(bc_in[1], 16)
                    pool.dma_start(b_in, a["ssm_b"][1]).then_inc(bc_in[1], 16)
                    pool.dma_start(pool_w[:, :, :], a["pool_wt"][1]).then_inc(poolw_in[1], 16)
                    pool.wait_ge(bc_in[1], 48)
                    pool.wait_ge(prep_ready, 1)
                    phase_table(nc.gpsimd, order, 1, 0, STATE_TILES, [x[:, 1024 * i:1024 * i + 1024] for x, i in ((prod, 0), (prod, 1), (wave, 2), (wave, 3))], table_ready,
                                lambda m: None)
                    discretise(nc.gpsimd, order, 1, bb_ready)
                    deviation(2)
            pool.wait_ge(ln_done, 2 * 5)
            pool.dma_start(tri[:, :], a["c_tri"]).then_inc(moe_in, 16)
            pool.dma_start(iota[:, :], a["c_iota"]).then_inc(moe_in, 16)
            nc.gpsimd.memset(ones[:, :], 1.0).then_inc(ones_ready, 1)
            deviation(5)

        @block.tensor
        def _(pe):
            mm = nc.tensor.matmul

            def take(n, cols, shift=0):
                pe.wait_ge(hi_ready, n + 1 + shift)
                return view(w_hi, SPLIT, n, cols), view(w_lo, SPLIT, n, cols)

            def claim(name):
                g = gemms[name]
                if g["use"]:
                    pe.wait_ge(pair_free[g["pair"]], g["use"])

            def by_feature(name, hi, lo, hook=None):
                g = gemms[name]
                claim(name)
                out_ = blocks(pair_of(name))
                fs, k = g["cols"] // P, 0
                for n in range(g["first"], g["end"]):
                    wh, wl = take(n, g["cols"])
                    for i in range(g["k"]):
                        for f in range(fs):
                            w = wh[:, i, f * P:(f + 1) * P]
                            mm(out_[:, f, :], w, hi(k + i), start=(k + i == 0 and f % 2 == 0), stop=False, skip_group_check=True)
                            mm(out_[:, f, :], w, lo(k + i), start=False, stop=False, skip_group_check=True)
                    pe.wait_ge(lo_ready, n + 1)
                    for i in range(g["k"]):
                        for f in range(fs):
                            last = mm(out_[:, f, :], wl[:, i, f * P:(f + 1) * P], hi(k + i), start=False,
                                      stop=(n == g["end"] - 1 and i == g["k"] - 1), skip_group_check=True)
                    last.then_inc(unit_used, 1)
                    k += g["k"]
                    if hook:
                        hook(n)

            def token_unit(n, cols, banks, hi, lo, k0, first_, last_):
                wh, wl = take(n, cols)
                kn = UNIT // cols
                for i in range(kn):
                    for t in range(TT):
                        mm(ps[:, banks[t], :], hi(k0 + i, t), wh[:, i, :], start=(first_ and i == 0), stop=False, skip_group_check=True)
                        mm(ps[:, banks[t], :], lo(k0 + i, t), wh[:, i, :], start=False, stop=False, skip_group_check=True)
                pe.wait_ge(lo_ready, n + 1)
                for i in range(kn):
                    for t in range(TT):
                        last = mm(ps[:, banks[t], :], hi(k0 + i, t), wl[:, i, :], start=False,
                                  stop=(last_ and i == kn - 1), skip_group_check=True)
                last.then_inc(unit_used, 1)

            def by_token(name, hi, lo, banks=None, first_=True, last_=True, hook=None):
                g = gemms[name]
                if banks is None:
                    claim(name)
                    banks = [2 * g["pair"] + t for t in range(TT)]
                for n in range(g["first"], g["end"]):
                    k = (n - g["first"]) * g["k"]
                    token_unit(n, g["cols"], banks, hi, lo, k, first_ and k == 0, last_ and n == g["end"] - 1)
                    if hook:
                        hook(n)

            def pair(t, lo_at):
                return (lambda k, q=None: t[:, k, :] if q is None else t[:, k, q * P:(q + 1) * P],
                        lambda k, q=None: t[:, lo_at + k, :] if q is None else t[:, lo_at + k, q * P:(q + 1) * P])

            x_hl, mem_hl, mx_hl = pair(xs, 8), pair(ms, 8), pair(mx, 8)
            y_hl = pair(xs, 4)
            p_hl = (lambda k: xs[:, 8 + k, :], lambda k: xs[:, 12 + k, :])

            def turn_b(l):
                pe.wait_ge(bb_ready, l + 1)
                for r in range(2):
                    for q in range(KS):
                        last = nc.tensor.transpose(ps[:, 4 + r, q * P:(q + 1) * P], bb[:, r, q * P:(q + 1) * P], ident[:, :])
                last.then_inc(bt_done, 1)

            def ssm_step(l, i):
                if i == 0:
                    pe.wait_ge(bt_ready, l + 1)
                    evacuated(pe, ("in", l, 0))
                if i < STATE_TILES:
                    n, q, row = STATE_TILES * l + i, i // 4, 32 * (i % 4)
                    if i >= 2:
                        pe.wait_ge(rotated, n - 1)
                    for r in range(2):
                        last = mm(ps[:, 4 + n % 2, r * T:(r + 1) * T], b_t[row:row + 32, r, q, :], u_sb[row:row + 32, q, :],
                                  start=True, stop=True, tile_position=(row, 0))
                    last.then_inc(bu_done, 1)
                if Y_LAG <= i < STATE_TILES + Y_LAG:
                    j = i - Y_LAG
                    n, c0 = STATE_TILES * l + j, 32 * (j % 8)
                    if j == 0:
                        pe.wait_ge(c_ready, l + 1)
                    pe.wait_ge(h_ready, n + 1)
                    parts = ((0, h_buf[j % 2][:, 0, :]), (1, h_buf[j % 2][:, 1, :]))
                    for t in range(TT):
                        for s, (c, h) in enumerate(parts):
                            last = mm(ps[:, 6 + j // 8, T * t + c0:T * t + c0 + 32], h[:, t * P:(t + 1) * P], c_t[:, c, 32 * j:32 * j + 32],
                                      start=(s == 0), stop=(s == 1), skip_group_check=True)
                    last.then_inc(y_used, 1)
                if i == STATE_TILES // 2 + Y_LAG + 3:
                    turn_y(l, 0)

            def turn_first(i, filler):
                return lambda n: turn_x(i, (0,)) if n == gemms[filler]["end"] - 2 else None

            def turn_y(l, h):
                pe.wait_ge(y_copied, 2 * l + h + 1)
                for f in range(2):
                    for t in range(TT):
                        last = nc.tensor.transpose(ps[:, 6 + h, T * f + P * t:T * f + P * t + P], y_tok[:, t, f * P:(f + 1) * P], ident[:, :])
                last.then_inc(y_turned, 1)

            def turn_x(i, tiles=range(TT)):
                for t in tiles:
                    pe.wait_ge(ln_done, TT * i + t + 1)
                    for k in range(KD):
                        last = nc.tensor.transpose(ps[:, 4 + 2 * t + k // 4, P * (k % 4):P * (k % 4) + P],
                                                   x_tok[:, t, k * P:(k + 1) * P], ident[:, :])
                    last.then_inc(xt_done, 1)

            def second_half_of_x(n):
                if n == 1:
                    pe.wait_ge(xs_ready, 2)

            pe.wait_ge(xs_ready, 1)
            for l in range(DEPTH):
                if l:
                    pe.wait_ge(xt_ready, TT * 3)
                by_feature(("in", l, 0), *x_hl, hook=None if l else second_half_of_x)
                if l:
                    turn_b(l)
                base = ssm_units(l)
                step = lambda n: ssm_step(l, n - base) if n >= base else None
                for c in range(1, 6):
                    by_feature(("in", l, c), *x_hl, hook=step)
                    if l == 0 and c == 3:
                        pe.wait_ge(small_in, 80)
                        turn_b(l)
                pe.wait_ge(ms_ready, 1)
                if l == 0:
                    by_token(("v", l, 0), *mem_hl, hook=step)
                pe.wait_ge(pooled, KS * (l + 1))
                pe.wait_ge(poolw_in[l], 16)
                claim(("pool_mix", l))
                for g in range(KS):
                    last = mm(blocks(pair_of(("pool_mix", l)))[:, g, :], pool_w[:, g, :], u_pool[:, g, PAD:PAD + T],
                              start=True, stop=True)
                last.then_inc(pool_mixed, 1)
                by_token(("v", l, 1), *mem_hl, hook=step)
                if l == 0:
                    by_feature(("k", l, 0), *mem_hl, hook=step)
                evacuated(pe, ("pool_mix", l))
                by_feature(("pool_up", l, 0), *p_hl, hook=step)
                if l == 0:
                    by_feature(("pool_up", l, 1), *p_hl, hook=step)
                assert gemms[("pool_up", l, 1 if l == 0 else 0)]["end"] - base == SSM_SLOTS
                turn_y(l, 1)

                def second_half_of(name, sem_, value):
                    middle = (gemms[name]["first"] + gemms[name]["end"]) // 2 - 1
                    return lambda n: pe.wait_ge(sem_, value) if n == middle else None

                pe.wait_ge(ys_ready, 4 * l + 1)
                by_feature(("glu", l, 0), *y_hl, hook=second_half_of(("glu", l, 0), ys_ready, 4 * l + 2))
                if l:
                    by_feature(("pool_up", l, 1), *p_hl)
                pe.wait_ge(ys_ready, 4 * l + 3)
                by_feature(("ssm_up", l, 0), *y_hl, hook=second_half_of(("ssm_up", l, 0), ys_ready, 4 * l + 4))
                by_feature(("ssm_up", l, 1), *y_hl)
                pe.wait_ge(mx_ready, 2 * l + 1)
                by_token(("out", l, 0), *mx_hl, hook=second_half_of(("out", l, 0), mx_ready, 2 * l + 2))
                by_token(("out", l, 1), *mx_hl)
                by_feature(("k", l, 1), *mem_hl, hook=turn_first(3 * l, ("k", l, 1)))
                turn_x(3 * l, (1,))
                pe.wait_ge(xt_ready, TT * (3 * l + 1))
                by_feature(("q", l, 0), *x_hl)
                by_feature(("q", l, 1), *x_hl)
                def scores(h):
                    n = HEADS * l + h
                    if h % 2 == 0:
                        evacuated(pe, ("q", l, h // 2))
                        evacuated(pe, ("k", l, h // 2))
                    if h >= 2:
                        pe.wait_ge(prob_exp, n - 1)
                    for t in range(TT):
                        for e in range(2):
                            last = mm(ps[:, 4 + h % 2, T * t:T * t + T], q_v[:, 2 * h + e, t * P:(t + 1) * P],
                                      k_sb[:, 2 * h + e, :], start=(e == 0), stop=(e == 1), skip_group_check=True)
                    last.then_inc(score_done, 1)

                def turn_probs(h):
                    n = HEADS * l + h
                    pe.wait_ge(prob_ready, n + 1)
                    if h:
                        pe.wait_ge(pt_ready, n)
                    for t in range(TT):
                        for m in range(2):
                            last = nc.tensor.transpose(ps[:, 6, T * m + P * t:T * m + P * t + P],
                                                       probs[:, h % 2, t, m * P:(m + 1) * P], ident[:, :])
                    last.then_inc(pt_done, 1)

                def weighted(h):
                    n = HEADS * l + h
                    pe.wait_ge(pt_ready, n + 1)
                    if h:
                        pe.wait_ge(at_ready, n)
                    for e in range(2):
                        for m in range(2):
                            last = mm(ps[:, 7, T * e:T * e + T], v_sb[:, m, T * h + P * e:T * h + P * e + P],
                                      probs_t[:, h % 2, m, :], start=(m == 0), stop=(m == 1), skip_group_check=True)
                    last.then_inc(pv_done, 1)

                def out_of(h, c):
                    n, g = gemms[("o", l, 0)]["first"] + 2 * h + c, gemms[("o", l, c)]
                    if h == 0:
                        claim(("o", l, c))
                    pe.wait_ge(at_ready, HEADS * l + h + 1)
                    token_unit(n, 512, [2 * g["pair"] + t for t in range(TT)], *x_hl, 2 * h, h == 0, h == HEADS - 1)

                scores(0)
                scores(1)
                for h in range(HEADS):
                    turn_probs(h)
                    if h == 1:
                        out_of(h - 1, 1)
                    weighted(h)
                    if h > 1:
                        out_of(h - 1, 1)
                    if h + 2 < HEADS:
                        scores(h + 2)
                    out_of(h, 0)
                out_of(HEADS - 1, 1)
                if l == 0:
                    by_token(("v", 1, 0), *mem_hl, hook=turn_first(1, ("v", 1, 0)))
                turn_x(3 * l + 1, (1,) if l == 0 else range(TT))
                pe.wait_ge(xt_ready, TT * (3 * l + 2))
                if l == 0:
                    def down(c):
                        pe.wait_ge(hs_ready, c + 1)
                        hi = lambda k, t: hs[:, c % 2, 0, k, t * P:(t + 1) * P]
                        lo = lambda k, t: hs[:, c % 2, 1, k, t * P:(t + 1) * P]
                        for h in range(2):
                            by_token(("ffn2", c, h), hi, lo, banks=[4 + h, 6 + h], first_=(c == 0), last_=(c == len(FF_CHUNKS) - 1))

                    for c in range(len(FF_CHUNKS)):
                        by_feature(("ffn1", c), *x_hl)
                        by_feature(("ffn3", c), *x_hl)
                        if c:
                            down(c - 1)
                    down(len(FF_CHUNKS) - 1)
                    by_feature(("k", 1, 0), *mem_hl, hook=turn_first(2, ("k", 1, 0)))
                    turn_x(2, (1,))

            pe.wait_ge(router_ready, 1)
            rhs = [router_s[:, i, :].rearrange("p (k e) -> p k e", e=EXPERTS) for i in range(2)]
            for k in range(KD):
                for s, (x_part, r_part) in enumerate(((0, 0), (8, 0), (0, 1))):
                    last = mm(ps[0:EXPERTS, 4, 0:T], rhs[r_part][:, k, :], xs[:, x_part + k, :],
                              start=(k == 0 and s == 0), stop=(k == KD - 1 and s == 2), skip_group_check=True)
            last.then_inc(scored, 1)
            pe.wait_ge(scored_out, 1)
            for t in range(TT):
                last = nc.tensor.transpose(ps[:, 5, t * EXPERTS:(t + 1) * EXPERTS], logits_t[:, t * P:(t + 1) * P],
                                           ident[0:EXPERTS, 0:EXPERTS])
            last.then_inc(logits_done, 1)
            pe.wait_ge(picked, 1)
            pe.wait_ge(moe_in, 32)
            pe.wait_ge(ones_ready, 1)
            both = rt[:, 5]
            bank = ps[:, 6, :].rearrange("p (o e) -> p o e", e=EXPERTS)
            mm(bank[:, 0:2, :], tri[:, :], both, start=True, stop=False, skip_group_check=True)
            for i in range(2):
                mm(bank[:, 1 + i, :], ones[:, :], both[:, 0, :], start=False, stop=(i == 0), skip_group_check=True)
            mm(bank[:, 2, :], ones[:, :], both[:, 1, :], start=False, stop=True, skip_group_check=True).then_inc(ranked, 1)

            def gather(i, r):
                for k in range(4):
                    for t in range(TT):
                        d0 = P * (4 * (i % 2) + k)
                        last = mm(ps[:, 6 + r % 2, k * P:(k + 1) * P], xts[:, i // 2, t, d0:d0 + P], sel[:, t, :],
                                  start=(t == 0), stop=(t == TT - 1), skip_group_check=True)
                last.then_inc(misc_filled, 1)

            def scatter(r, q):
                return mm(ps[:, 6 + r % 2, :], gsel_t[:, q // 2, :], y_sb[:, 512 * (q % 2):512 * (q % 2) + 512], start=True, stop=True)

            pe.wait_ge(xts_ready, 1)
            pe.wait_ge(sel_ready, TT)
            for i in range(FIRST):
                if i >= 2:
                    pe.wait_ge(misc_free[i % 2], 1)
                gather(i, i)

            def job(j, h):
                base = NJ * j + NJ * h
                chunks = FE_CHUNKS * j + FE_CHUNKS * h

                def misc(n):
                    for r in rounds_at.get(n, ()):
                        what, q = rounds[r][:2]
                        pe.wait_ge(misc_free[r % 2], NR // 2 * j + (NR // 2 * h + FIRST // 2 + r // 2))
                        if what == "out":
                            if q == 0:
                                pe.wait_ge(y_ready, j + (1 + h))
                            scatter(r, q).then_inc(misc_filled, 1)
                        elif what == "in":
                            if q == 0:
                                pe.wait_ge(sel_ready, TT * j + (TT * h + 2 * TT))
                            gather(q, r)
                        elif what == "gates":
                            pe.wait_ge(gsel_ready, TT * j + (TT * h + TT))
                            for t in range(TT):
                                last = nc.tensor.transpose(ps[:, 6 + r % 2, t * P:(t + 1) * P], gsel[:, t, :], ident[:, :])
                            last.then_inc(misc_filled, 1)
                        else:
                            pe.wait_ge(w3_free, chunks + (1 + q + 1))
                            for k in range(4):
                                last = nc.tensor.transpose(ps[:, 6 + r % 2, k * P:(k + 1) * P], he[:, q % 2, k * P:(k + 1) * P], ident[:, :])
                            last.then_inc(misc_filled, 1)

                def products(n, bank, x_hi, x_lo, k0, first_, last_):
                    wh, wl = take(N0 + n, 512, base)
                    for i in range(2):
                        mm(ps[:, bank, :], x_hi(k0 + i), wh[:, i, :], start=(first_ and i == 0), stop=False, skip_group_check=True)
                        mm(ps[:, bank, :], x_lo(k0 + i), wh[:, i, :], start=False, stop=False, skip_group_check=True)
                    pe.wait_ge(lo_ready, base + (N0 + n + 1))
                    for i in range(2):
                        last = mm(ps[:, bank, :], x_hi(k0 + i), wl[:, i, :], start=False, stop=(last_ and i == 1), skip_group_check=True)
                    last.then_inc(unit_used, 1)
                    misc(n + 1)

                for b in range(2):
                    pe.wait_ge(misc_free[b], NR // 2 * j + (NR // 2 * h + FIRST // 2))
                for i, (kind, c) in enumerate(stages):
                    if kind == "w2":
                        r = round_of[("turn", c)]
                        pe.wait_ge(misc_free[r % 2], NR // 2 * j + (NR // 2 * h + FIRST // 2 + r // 2 + 1))
                        for n in range(4):
                            k0 = 2 * (n % 2)
                            products(4 * i + n, 4 + n // 2, lambda k: het[:, c % 2, 0, k, :], lambda k: het[:, c % 2, 1, k, :],
                                     k0, c == 0 and k0 == 0, c == FE_CHUNKS - 1 and k0 == 2)
                    else:
                        pe.wait_ge(w1_free if kind == "w1" else w3_free, chunks + (1 if c < 2 else c))
                        for n in range(4):
                            products(4 * i + n, 2 * (c % 2) + (kind == "w3"), lambda k: xe[:, h, 0, k, :], lambda k: xe[:, h, 1, k, :],
                                     2 * n, n == 0, n == 3)

            with pe.Fori(0, EXPERTS, 2) as j:
                job(j, 0)
                job(j, 1)
            over = pe.value_load(jobs[0:1, 0:1], min_val=0, max_val=OVER_MAX)
            for o in range(OVER_MAX):
                with pe.If(over > o):
                    job(EXPERTS + o - o % 2, o % 2)
                pe.nop()
            pe.wait_ge(y_ready, over + (1 + EXPERTS))
            for r in range(4):
                pe.wait_ge(misc_free[r % 2], over * (NR // 2) + (FIRST // 2 + r // 2 + NR // 2 * EXPERTS))
                scatter(r, r).then_inc(misc_filled, 1)


def build(nc, arrays):
    a = {k: nc.dram_tensor(f"in_{k}", list(v.shape), F32, kind="ExternalInput").ap() for k, v in arrays.items()}
    out = nc.dram_tensor("out_0", [T, D], F32, kind="ExternalOutput").ap()
    build_trunk(nc, a, out)


_AS_THEY_ARE = ["ln_mix_g", "ln_mix_b", "w_in", "ssm_w_glu", "w_ssm_up", "w_pool_up", "w_out", "ln_xa_g", "ln_xa_b",
                "xa_wq", "xa_wk", "xa_wv", "xa_wo", "ln_ffn_g", "ln_ffn_b", "ffn_w1", "ffn_w3", "ffn_w2"]


def lay_out(inputs):
    import numpy as np
    i = {k: np.asarray(v) for k, v in inputs.items()}
    L = DEPTH
    a = {k: i[k] for k in _AS_THEY_ARE}
    for k in ("moe_w1", "moe_w3", "moe_w2"):
        a[k] = i[k][0]
    a["x"] = i["x"][0]
    for k, n in (("x_t", "x"), ("mem_t", "mem")):
        a[k] = i[n][0].T.reshape(KD, P, T).transpose(1, 0, 2)

    def states(v):
        return v.reshape(L, STATE_TILES, P).transpose(2, 0, 1).reshape(P, L * STATE_TILES)
    log_dt = np.broadcast_to(i["ssm_log_dt"][:, :, None], i["ssm_a_re"].shape)
    a["ssm_par"] = np.stack([states(i["ssm_a_re"]), states(i["ssm_a_im"]), states(log_dt)], axis=1)

    def block_diagonal(v):
        v = v.reshape(L, STATE_TILES, 2, P // 2, GROUP_W)
        z = np.zeros((L, 2, P // 2, STATE_TILES, 2, GROUP_W), v.dtype)
        for h in range(2):
            z[:, h, :, :, h, :] = v[:, :, h].transpose(0, 2, 1, 3)
        return z.reshape(L, P, STATE_TILES * 2 * GROUP_W)
    a["ssm_b"] = np.stack([block_diagonal(i["ssm_b_re"]), block_diagonal(i["ssm_b_im"])], axis=2)
    a["ssm_c"] = np.stack([block_diagonal(i["ssm_c_re"].transpose(0, 1, 3, 2)),
                           block_diagonal(i["ssm_c_im"].transpose(0, 1, 3, 2))], axis=1)
    a["chan_par"] = np.stack([i[n].reshape(L, KS, P).transpose(2, 0, 1) for n in ("ssm_d", "ssm_b_glu", "pool_scale")], axis=1)
    a["pool_wt"] = i["pool_w"].transpose(0, 2, 1, 3)
    a["router"] = i["moe_router"][0].reshape(KD, P, EXPERTS).transpose(1, 0, 2).reshape(P, KD * EXPERTS)
    f = np.float32
    a["c_ident"] = np.eye(P, dtype=f)
    a["c_tri"] = np.triu(np.ones((P, P), f), 1)
    a["c_iota"] = np.broadcast_to(np.arange(P, dtype=f), (P, P))
    a["c_iota8"] = np.broadcast_to(np.arange(EXPERTS, dtype=f), (P, EXPERTS))
    steps = np.arange(1, PAD + 1, dtype=f)
    a["c_inv"] = np.broadcast_to(np.stack([1.0 / np.minimum(steps, f(2 ** (g + 1))) for g in range(KS)]), (P, KS, PAD))
    return {k: np.ascontiguousarray(v) for k, v in a.items()}


def kernel(**inputs):
    import concourse.bacc as bacc
    from concourse.bass_utils import run_bass_kernel_spmd

    arrays = lay_out(inputs)
    nc = bacc.Bacc("TRN2", target_bir_lowering=False, num_devices=1)
    build(nc, arrays)
    r = run_bass_kernel_spmd(nc, [{f"in_{k}": v for k, v in arrays.items()}], core_ids=[0])
    return r.results[0]["out_0"].reshape(1, T, D)
```
